# Optimizing a Trainium2 kernel written in Bass

```python
import math
import jax, jax.numpy as jnp
from jax import lax
import numpy as np

D_MODEL = 1024
BATCH = 1
SEQ = 256
DEPTH = 1

NORM_EPS = 1e-6
N_MOD = 6
MLA_HEADS = 8
MLA_Q_LORA = 768
MLA_KV_LORA = 256
MLA_NOPE = 64
MLA_ROPE = 32
MLA_QK = MLA_NOPE + MLA_ROPE
MLA_VDIM = 64
MLA_WIDTH = MLA_HEADS * MLA_VDIM
ROPE_THETA = 10000.0
ATTN_QBLOCK = 128
MOBA_HEADS = 8
MOBA_HDIM = 64
MOBA_WIDTH = MOBA_HEADS * MOBA_HDIM
MOBA_BLOCK = 256
MOBA_TOPK = 3
MOBA_QBLOCK = 32
D_MIX = MLA_WIDTH + MOBA_WIDTH
IN_WIDTHS = (MLA_Q_LORA, MLA_KV_LORA, MLA_ROPE, MOBA_WIDTH, MOBA_WIDTH, MOBA_WIDTH)
D_IN = sum(IN_WIDTHS)
REL_BUCKETS = 32
REL_MAX_DIST = 1024
PEER_NKEYS = 128
PEER_EXPERTS = PEER_NKEYS * PEER_NKEYS
PEER_HEADS = 8
PEER_TOPK = 16
PEER_DKEY = 128
PEER_HALF = PEER_DKEY // 2
PEER_TBLOCK = 128

kernel_name = "hymba_mla_moba_peer_adaln_layer"

def rmsnorm(x, g):
    xf = x.astype(jnp.float32)
    y = xf * lax.rsqrt(jnp.mean(xf * xf, axis=-1, keepdims=True) + NORM_EPS)
    return (y * g.astype(jnp.float32)).astype(x.dtype)

def rope(x, positions):
    half = x.shape[-1] // 2
    inv = ROPE_THETA ** (-jnp.arange(half, dtype=jnp.float32) / half)
    ang = positions.astype(jnp.float32)[:, :, None, None] * inv
    cos, sin = jnp.cos(ang), jnp.sin(ang)
    xf = x.astype(jnp.float32)
    x1, x2 = xf[..., :half], xf[..., half:]
    return jnp.concatenate([x1 * cos - x2 * sin, x2 * cos + x1 * sin], -1).astype(x.dtype)

def t5_bucket(dist):
    n = jnp.maximum(dist, 0)
    max_exact = REL_BUCKETS // 2
    nf = jnp.maximum(n, max_exact).astype(jnp.float32)
    large = max_exact + (jnp.log(nf / max_exact) / math.log(REL_MAX_DIST / max_exact)
                         * (REL_BUCKETS - max_exact)).astype(jnp.int32)
    large = jnp.minimum(large, REL_BUCKETS - 1)
    return jnp.where(n < max_exact, n, large)

def causal_attention(q, k, v):
    B, S, H, D = q.shape
    scale = D ** -0.5
    nq = S // ATTN_QBLOCK
    qb = q.reshape(B, nq, ATTN_QBLOCK, H, D).transpose(1, 0, 2, 3, 4)
    k_idx = jnp.arange(S)

    def one(args):
        qc, blk = args
        s = jnp.einsum('bqhd,bkhd->bhqk', qc, k).astype(jnp.float32) * scale
        q_idx = blk * ATTN_QBLOCK + jnp.arange(ATTN_QBLOCK)
        s = jnp.where(k_idx[None, :] <= q_idx[:, None], s, -jnp.inf)
        p = jax.nn.softmax(s, axis=-1).astype(v.dtype)
        return jnp.einsum('bhqk,bkhd->bqhd', p, v)

    o = lax.map(one, (qb, jnp.arange(nq)))
    return o.transpose(1, 0, 2, 3, 4).reshape(B, S, H, v.shape[-1])

def mla_group(c_q, c_kv, k_rope, positions, g_qa, w_uq, g_kva, w_ukv):
    B, S, _ = c_q.shape
    q = (rmsnorm(c_q, g_qa) @ w_uq).reshape(B, S, MLA_HEADS, MLA_QK)
    kv = (rmsnorm(c_kv, g_kva) @ w_ukv).reshape(B, S, MLA_HEADS, MLA_NOPE + MLA_VDIM)
    k_nope, v = kv[..., :MLA_NOPE], kv[..., MLA_NOPE:]
    q = jnp.concatenate([q[..., :MLA_NOPE], rope(q[..., MLA_NOPE:], positions)], -1)
    k_r = rope(k_rope[:, :, None, :], positions)
    k = jnp.concatenate([k_nope, jnp.broadcast_to(k_r, (B, S, MLA_HEADS, MLA_ROPE))], -1)
    return causal_attention(q, k, v).reshape(B, S, MLA_WIDTH)

def moba_group(q, k, v, rel_bias):
    B, S, _ = q.shape
    H, Dh, BS = MOBA_HEADS, MOBA_HDIM, MOBA_BLOCK
    q, k, v = (t.reshape(B, S, H, Dh).transpose(0, 2, 1, 3) for t in (q, k, v))
    nb = -(-S // BS)
    pad = nb * BS - S
    kb = jnp.pad(k, ((0, 0), (0, 0), (0, pad), (0, 0))).reshape(B, H, nb, BS, Dh)
    vb = jnp.pad(v, ((0, 0), (0, 0), (0, pad), (0, 0))).reshape(B, H, nb, BS, Dh)
    kmean = jnp.mean(kb, axis=3)
    n_sel = min(MOBA_TOPK, nb)
    scale = Dh ** -0.5
    bi = jnp.arange(B)[:, None, None, None]
    hi = jnp.arange(H)[None, :, None, None]
    hi5 = jnp.arange(H)[:, None, None, None]
    bias_hb = rel_bias.T.astype(jnp.float32)
    t_blk = jnp.arange(BS)
    nq = S // MOBA_QBLOCK
    qb = q.reshape(B, H, nq, MOBA_QBLOCK, Dh).transpose(2, 0, 1, 3, 4)

    def one(args):
        qc, blk = args
        q_idx = blk * MOBA_QBLOCK + jnp.arange(MOBA_QBLOCK)
        own = (blk * MOBA_QBLOCK) // BS
        gate = jnp.einsum('bhqd,bhnd->bhqn', qc, kmean).astype(jnp.float32)
        gate = jnp.where(jnp.arange(nb) < own, gate, -jnp.inf)
        _, sel = lax.top_k(gate, n_sel)
        slot_ok = jnp.arange(n_sel) < own
        k_sel = kb[bi, hi, sel]
        v_sel = vb[bi, hi, sel]
        s_sel = jnp.einsum('bhqd,bhqntd->bhqnt', qc, k_sel).astype(jnp.float32) * scale
        k_pos = sel[..., None] * BS + t_blk
        dist = q_idx[None, None, :, None, None] - k_pos
        s_sel = s_sel + bias_hb[hi5, t5_bucket(dist)]
        s_sel = jnp.where(slot_ok[:, None], s_sel, -jnp.inf)
        k_own = lax.dynamic_slice_in_dim(kb, own, 1, axis=2)[:, :, 0]
        v_own = lax.dynamic_slice_in_dim(vb, own, 1, axis=2)[:, :, 0]
        d_own = q_idx[:, None] - (own * BS + t_blk)[None, :]
        s_own = jnp.einsum('bhqd,bhtd->bhqt', qc, k_own).astype(jnp.float32) * scale
        s_own = s_own + bias_hb[:, t5_bucket(d_own)]
        s_own = jnp.where(d_own >= 0, s_own, -jnp.inf)
        s_all = jnp.concatenate([s_sel.reshape(B, H, MOBA_QBLOCK, n_sel * BS), s_own], -1)
        p = jax.nn.softmax(s_all, axis=-1).astype(v.dtype)
        p_sel = p[..., :n_sel * BS].reshape(B, H, MOBA_QBLOCK, n_sel, BS)
        p_own = p[..., n_sel * BS:]
        return (jnp.einsum('bhqnt,bhqntd->bhqd', p_sel, v_sel)
                + jnp.einsum('bhqt,bhtd->bhqd', p_own, v_own))

    o = lax.map(one, (qb, jnp.arange(nq)))
    o = o.transpose(1, 0, 3, 2, 4).reshape(B, S, H * Dh)
    return o

def peer_ffn(h, w_pq, sub_keys, u_tab, v_tab):
    B, S, D = h.shape
    K = PEER_TOPK
    q = (h @ w_pq).reshape(B, S, PEER_HEADS, 2, PEER_HALF)
    s = jnp.einsum('bshpd,hpnd->bshpn', q, sub_keys).astype(jnp.float32)
    s_top, i_top = lax.top_k(s, K)
    cand = (s_top[..., 0, :, None] + s_top[..., 1, None, :]).reshape(B, S, PEER_HEADS, K * K)
    cand_idx = (i_top[..., 0, :, None] * PEER_NKEYS + i_top[..., 1, None, :]).reshape(B, S, PEER_HEADS, K * K)
    best, pos = lax.top_k(cand, K)
    expert = jnp.take_along_axis(cand_idx, pos, axis=-1)
    gate = jax.nn.softmax(best, axis=-1).astype(h.dtype)
    nt = S // PEER_TBLOCK
    hc = h.reshape(B, nt, PEER_TBLOCK, D).transpose(1, 0, 2, 3)
    ec = expert.reshape(B, nt, PEER_TBLOCK, PEER_HEADS, K).transpose(1, 0, 2, 3, 4)
    gc = gate.reshape(B, nt, PEER_TBLOCK, PEER_HEADS, K).transpose(1, 0, 2, 3, 4)

    def one(args):
        hb, eb, gb = args
        a = jnp.einsum('btd,bthkd->bthk', hb, u_tab[eb])
        a = jax.nn.gelu(a, approximate=False) * gb
        return jnp.einsum('bthk,bthkd->btd', a, v_tab[eb])

    y = lax.map(one, (hc, ec, gc))
    return y.transpose(1, 0, 2, 3).reshape(B, S, D)

def setup_inputs(seed: int = 0) -> dict:
    key = jax.random.key(seed)
    ks = jax.random.split(key, 20)
    f32 = jnp.float32

    def nrm(k, shape, scale):
        return jax.random.normal(k, shape, f32) * scale

    def gain(k, shape):
        return 1.0 + 0.02 * jax.random.normal(k, shape, f32)

    L, D = DEPTH, D_MODEL
    offset = jax.random.randint(ks[2], (BATCH, 1), 0, 1024, dtype=jnp.int32)
    return {
        "x": nrm(ks[0], (BATCH, SEQ, D), 1.0),
        "c": nrm(ks[1], (BATCH, D), 1.0),
        "positions": (jnp.arange(SEQ, dtype=jnp.int32)[None, :] + offset).astype(jnp.int32),
        "w_ada": nrm(ks[3], (L, D, N_MOD * D), 0.5 * D ** -0.5),
        "b_ada": nrm(ks[4], (L, N_MOD * D), 0.02),
        "g_mix": gain(ks[5], (L, D)),
        "w_in": nrm(ks[6], (L, D, D_IN), D ** -0.5),
        "g_qa": gain(ks[7], (L, MLA_Q_LORA)),
        "w_uq": nrm(ks[8], (L, MLA_Q_LORA, MLA_HEADS * MLA_QK), MLA_Q_LORA ** -0.5),
        "g_kva": gain(ks[9], (L, MLA_KV_LORA)),
        "w_ukv": nrm(ks[10], (L, MLA_KV_LORA, MLA_HEADS * (MLA_NOPE + MLA_VDIM)), MLA_KV_LORA ** -0.5),
        "rel_bias": nrm(ks[11], (REL_BUCKETS, MOBA_HEADS), 0.5),
        "w_out": nrm(ks[12], (L, D_MIX, D), D_MIX ** -0.5),
        "g_ffn": gain(ks[13], (L, D)),
        "w_pq": nrm(ks[14], (L, D, PEER_HEADS * PEER_DKEY), D ** -0.5),
        "peer_keys": nrm(ks[15], (L, PEER_HEADS, 2, PEER_NKEYS, PEER_HALF), PEER_HALF ** -0.5),
        "peer_u": nrm(ks[16], (L, PEER_EXPERTS, D), D ** -0.5),
        "peer_v": nrm(ks[17], (L, PEER_EXPERTS, D), PEER_HEADS ** -0.5),
        "g_final": gain(ks[18], (D,)),
    }

def reference(x, c, positions, w_ada, b_ada, g_mix, w_in, g_qa, w_uq, g_kva, w_ukv,
              rel_bias, w_out, g_ffn, w_pq, peer_keys, peer_u, peer_v, g_final):
    split_at = [int(s) for s in np.cumsum(IN_WIDTHS)[:-1]]
    for l in range(DEPTH):
        mod = (jax.nn.silu(c) @ w_ada[l] + b_ada[l])[:, None, :]
        sh_a, sc_a, gt_a, sh_f, sc_f, gt_f = jnp.split(mod, N_MOD, axis=-1)
        h = rmsnorm(x, g_mix[l]) * (1.0 + sc_a) + sh_a
        z = h @ w_in[l]
        c_q, c_kv, k_rope, mq, mk, mv = jnp.split(z, split_at, axis=-1)
        o_mla = mla_group(c_q, c_kv, k_rope, positions, g_qa[l], w_uq[l], g_kva[l], w_ukv[l])
        o_moba = moba_group(mq, mk, mv, rel_bias)
        y = jnp.concatenate([o_mla, o_moba], axis=-1) @ w_out[l]
        x = x + gt_a * y
        h = rmsnorm(x, g_ffn[l]) * (1.0 + sc_f) + sh_f
        x = x + gt_f * peer_ffn(h, w_pq[l], peer_keys[l], peer_u[l], peer_v[l])
    return rmsnorm(x, g_final)


_drawn_inputs = setup_inputs


def setup_inputs(seed=0):
    import zlib

    import numpy as np

    out = dict(_drawn_inputs(seed))
    spreads = {}
    factors = {'b_ada': 3.813, 'g_mix': 8.0, 'g_qa': 8.0, 'g_kva': 8.0, 'g_ffn': 6.344, 'g_final': 2.914}
    for name, (base, spread) in spreads.items():
        noise = np.random.default_rng([zlib.crc32(name.encode()), seed]).standard_normal(out[name].shape)
        drawn = base * np.exp(spread * noise) if base else spread * noise
        out[name] = __import__('jax').numpy.asarray(drawn.astype(out[name].dtype))
    for name, factor in factors.items():
        out[name] = (out[name] * factor).astype(out[name].dtype)
    return out
```

```python
from contextlib import ExitStack

import numpy as np

import concourse.bass as bass
from concourse import mybir

F32 = mybir.dt.float32
F32R = mybir.dt.float32r
I32 = mybir.dt.int32
U32 = mybir.dt.uint32
ALU = mybir.AluOpType
ACT = mybir.ActivationFunctionType
AX = mybir.AxisListType

P = 128
T = 256
TT = T // P
D = 1024
KD = D // P
EPS = 1e-6
Q_LORA, KV_LORA = 768, 256
CQ, CKV = Q_LORA // P, KV_LORA // P
HEADS = 8
NOPE, ROPE, HDIM = 64, 32, 64
MLA_SCALE = float((NOPE + ROPE) ** -0.5)
MOBA_SCALE = float(HDIM ** -0.5)
PAIRS = HEADS // 2
NKEYS = 128
PH = 8
TOPK = 16
BLOCKS = NKEYS
LOWEST = -3.0e38
MASKED = -1.0e30
THETA = 10000.0

SH_A, SC_A, GT_A, SH_F, SC_F, GT_F = (KD * i for i in range(6))
ADA = 6 * KD
ADA_FIRST = 2 * KD

V_C, V_B, V_GMIX, V_GQA, V_GKVA, V_GFFN = 0, 8, 56, 64, 70, 72
V_INV, V_SGN, V_EPS = 80, 81, 82
NVEC = 84

TWO_PI = 2.0 * np.pi
C1 = 6.28125
C2 = float(np.float32(TWO_PI - C1).view(np.int32) & ~0xFFF)
C2 = float((np.float32(TWO_PI - C1).view(np.int32) & np.int32(~0xFFF)).view(np.float32))
C3 = float(np.float32(TWO_PI - C1 - C2))
ROUND = 12582912.0
PI_IN = 3.1415925
HALF_PI = float(np.float32(np.pi / 2))

TILES = ([("cq", i) for i in range(CQ)] + [("ckv", i) for i in range(CKV)] + [("kr", 0), ("kr", 1)]
         + [("mq", i) for i in range(PAIRS)] + [("mk", i) for i in range(PAIRS)]
         + [("mv", i) for i in range(TT)]
         + [("qn", i) for i in range(PAIRS)] + [("qr", i) for i in range(4)]
         + [("kn", i) for i in range(PAIRS)] + [("v", i) for i in range(TT)])
Z_TILES = TILES.index(("qn", 0))
DVE_READS = ("cq", "ckv", "kr", "qr")
ACT_READS = ("mq", "mk", "mv", "qn", "kn", "v")
ADA_AFTER = {n: 2 if 20 <= n < 28 else 1 for n in range(10, 34)}


def tile_no(kind, i=0):
    return TILES.index((kind, i))


def dve_reads(n):
    return sum(kind in DVE_READS for kind, _ in TILES[:n + 1])


def act_reads(n):
    return sum(kind in ACT_READS for kind, _ in TILES[:n + 1])


def build(nc, consts, vecs, positions, xT, w_ada, w_in, w_uq, w_ukv, rel, w_out, w_pq, keys, u_tab, v_tab,
          g_final, out):
    base = (nc.sbuf_base + 63) // 64 * 64

    def place(name, at, shape, dt=F32):
        return nc.alloc_sbuf_tensor_at(name, shape, dt, offset=base + 4 * at)

    AG = place("AG", 0, [P, BLOCKS, T])
    W_IN = place("W_IN", 0, [P, 22, KD, P])
    W_MV = W_IN[:, 18:22].rearrange("p c k n -> p (c k n)").rearrange("p (k n) -> p k n", k=KD)
    W_UQ = place("W_UQ", 22528, [P, 8, CQ, P])
    W_UKV = place("W_UKV", 28672, [P, 4, CKV, P])
    W_UV = place("W_UV", 29696, [P, CKV, 512])
    BT = place("BT", 30720, [P, HEADS, T])
    QN = place("QN", 0, [P, HEADS, T])
    QR = place("QR", 2048, [P, HEADS, T])
    OT = place("OT", 4096, [P, KD, T])
    RT = place("RT", 4096, [P, 2, T])
    W_OUT = place("W_OUT", 6144, [P, KD, KD, P])
    W_PQ = place("W_PQ", 14336, [P, KD, KD, P])
    KEYS = place("KEYS", 22528, [P, PH, 2 * NKEYS])
    SC = place("SC", 28672, [P, TT * PH, 2, NKEYS])
    TI = place("TI", 24576, [P, TT * PH, 2, TOPK])
    BEST = place("BEST", 25088, [P, TT * PH, TOPK])
    POS = place("POS", 25344, [P, TT * PH, TOPK], U32)
    WK = place("WK", 25600, [P, 2, NKEYS])
    CAND = place("CAND", 25856, [P, TOPK, TOPK])
    TV = place("TV", 26112, [P, 2, TOPK])
    TIU = place("TIU", 26144, [P, 2, TOPK], U32)
    BV = place("BV", 26176, [P, TOPK])
    PU = place("PU", 26192, [P, TOPK], U32)
    AIU = place("AIU", 26240, [P, 2, TT * PH, TOPK], U32)
    AIF = place("AIF", 26752, [P, 2, TT * PH, TOPK])
    EQ = place("EQ", 27264, [P, 4, TOPK, TOPK])
    GSUM = place("GSUM", 28288, [P, TT * PH])
    GREC = place("GREC", 28304, [P, TT * PH])

    XT = place("XT", 32768, [P, KD, T])
    HT = place("HT", 34816, [P, KD, T])
    OHJ = place("OHJ", 34816, [P, 2, 4, P])
    OHI = place("OHI", 35840, [P, 2, 4, P])
    DIAG = place("DIAG", 34816, [P, KD, P])
    WH = place("WH", 34816, [P, 2, T], F32R)
    WL = place("WL", 35328, [P, 2, T], F32R)
    QM = place("QM", 36864, [P, HEADS, T])
    H2H = place("H2H", 36864, [P, KD, T], F32R)
    X1 = place("X1", 36864, [P, TT, D])
    KM = place("KM", 38912, [P, PAIRS, T])
    KN = place("KN", 39936, [P, PAIRS, T])
    H2L = place("H2L", 38912, [P, KD, T], F32R)
    GTB = place("GTB", 38912, [P, D])
    GFB = place("GFB", 39936, [P, D])
    VM = place("VM", 40960, [P, TT, 512])
    VN = place("VN", 41984, [P, TT, 512])
    QP = place("QP", 40960, [P, PH, T])
    GTOK = place("GTOK", 40960, [P, TT * PH, TOPK])
    ITOK = place("ITOK", 41216, [P, 2, TT * PH, TOPK])
    RANKED = place("RANKED", 41728, [P, 3, T])
    RING = place("RING", 43008, [P, 4, D])
    CQT = place("CQT", 47104, [P, CQ + CKV, T])
    S = place("S", 47104, [P, 2, 2, T])
    PR = place("PR", 48128, [P, 2, 2, T])
    HI = place("HI", 47104, [P, 2, D], F32R)
    SQ = place("SQ", 49152, [P, KD, T])
    PT = place("PT", 49152, [P, 2, 2, 2, P])
    LO = place("LO", 49152, [P, 2, D], F32R)
    EPI = place("EPI", 47104, [P, TT, 2, D])
    KR = place("KR", 51200, [P, T])
    COS = place("COS", 51456, [P, T])
    SIN = place("SIN", 51712, [P, T])
    RSTD = place("RSTD", 51968, [P, T])
    CONST = place("CONST", 52224, [P, 512])
    IDENT, IOTA, MASK = CONST[:, 0:128], CONST[:, 128:256], CONST[:, 256:512]
    ONES = place("ONES", 52736, [P, P])
    VEC = place("VEC", 52864, [P, NVEC])
    MOD = place("MOD", 52952, [P, ADA])
    GAIN1 = place("GAIN1", 53000, [P, KD])
    GAIN2 = place("GAIN2", 53008, [P, KD])
    SILU = place("SILU", 53016, [P, 3, KD])
    NMAX = place("NMAX", 53040, [P, 2, 2])
    SUM = place("SUM", 53048, [P, 2, 2])
    REC = place("REC", 53056, [P, 2, 2])
    SSQ = place("SSQ", 53064, [P, 3, TT])
    ANG = CQT

    with ExitStack() as ctx:
        PS = ctx.enter_context(nc.psum_tensor("PS", [P, 8, 512], F32))

        def sem(name):
            return ctx.enter_context(nc.semaphore(name))

        s_const, s_vec, s_pos, s_x, s_bias = (sem(n) for n in ("s_const", "s_vec", "s_pos", "s_x", "s_bias"))
        s_win = [sem(f"s_win{i}") for i in range(5)]
        s_wuq, s_wukv, s_wout, s_wpq, s_keys = (sem(n) for n in ("s_wuq", "s_wukv", "s_wout", "s_wpq", "s_keys"))
        s_ring = [sem(f"s_ring{j}") for j in range(4)]
        s_gf, s_out = sem("s_gf"), sem("s_out")
        s_ones, s_zero, s_zeroq = sem("s_ones"), sem("s_zero"), sem("s_zeroq")
        s_exp, s_silu = sem("s_exp"), sem("s_silu")
        s_sq, s_ssq, s_root, s_rstd = sem("s_sq"), sem("s_ssq"), sem("s_root"), sem("s_rstd")
        s_ada, s_mod, s_modc, s_h = sem("s_ada"), sem("s_mod"), sem("s_modc"), sem("s_h")
        s_ang, s_trig = sem("s_ang"), sem("s_trig")
        s_tile, s_dread, s_aread = sem("s_tile"), sem("s_dread"), sem("s_aread")
        s_lat, s_rope, s_mask = sem("s_lat"), sem("s_rope"), sem("s_mask")
        s_s, s_sm, s_nm, s_p, s_pn, s_t, s_pt, s_o, s_ot = (
            sem(n) for n in ("s_s", "s_sm", "s_nm", "s_p", "s_pn", "s_t", "s_pt", "s_o", "s_ot"))
        s_y, s_x1, s_h2, s_h2h, s_h2l = (sem(n) for n in ("s_y", "s_x1", "s_h2", "s_h2h", "s_h2l"))
        s_q, s_qc, s_k, s_sc = (sem(n) for n in ("s_q", "s_qc", "s_k", "s_sc"))
        s_uh, s_ul, s_umm, s_gelu = (sem(n) for n in ("s_uh", "s_ul", "s_umm", "s_gelu"))
        s_tk, s_held, s_best, s_gexp, s_ranks, s_rt, s_ranked = (
            sem(n) for n in ("s_tk", "s_held", "s_best", "s_gexp", "s_ranks", "s_rt", "s_ranked"))
        s_diag, s_gtb, s_x1t, s_x1c, s_gtbc = (sem(n) for n in ("s_diag", "s_gtb", "s_x1t", "s_x1c", "s_gtbc"))
        s_oh, s_gmm, s_gated = sem("s_oh"), sem("s_gmm"), sem("s_gated")
        s_vh, s_vl, s_vmm = sem("s_vh"), sem("s_vl"), sem("s_vmm")
        s_e1, s_e2, s_e3, s_e4, s_e5 = (sem(f"s_e{i}") for i in range(1, 6))
        s_d = sem("s_d")

        block = ctx.enter_context(nc.Block())

        UNITS = [(g, qt) for g in range(2 * PAIRS) for qt in range(TT)]
        WIN_SPLIT = [0, 6, 10, 14, 18, 22]

        @block.sync
        def _(sp):
            sp.dma_start(XT[:], xT).then_inc(s_x, 16)
            sp.dma_start(VEC[:], vecs).then_inc(s_vec, 16)

            def load_ada(c):
                if c >= 4:
                    sp.wait_ge(s_ada, c - 3)
                sp.dma_start(RING[:, c % 4, :], w_ada[c]).then_inc(s_ring[c % 4], 16)

            def load_in(i):
                a, b = WIN_SPLIT[i], WIN_SPLIT[i + 1]
                sp.dma_start(W_IN[:, a:b].rearrange("p c k n -> p (c k n)"),
                             w_in[:, a * D:b * D]).then_inc(s_win[i], 16)

            for c in range(4):
                load_ada(c)
            sp.dma_start(CONST[:], consts).then_inc(s_const, 16)
            sp.dma_start(ANG[:, 0, :].bitcast(I32), positions.partition_broadcast(P)).then_inc(s_pos, 16)
            for c in range(4, ADA_FIRST):
                load_ada(c)
            load_in(0)
            load_in(1)
            for c in range(ADA_FIRST, ADA_FIRST + 4):
                load_ada(c)
            for i in range(2, 5):
                load_in(i)
            sp.dma_start(W_UQ[:], w_uq).then_inc(s_wuq, 16)
            sp.dma_start(W_UKV[:], w_ukv[:, 0:1024]).then_inc(s_wukv, 16)
            sp.dma_start(W_UV[:], w_ukv[:, 1024:2048]).then_inc(s_wukv, 16)
            sp.dma_start(BT[:], rel).then_inc(s_bias, 16)
            for c in range(ADA_FIRST + 4, ADA):
                load_ada(c)
            sp.wait_ge(s_tile, Z_TILES)
            sp.dma_start(W_OUT[:], w_out).then_inc(s_wout, 16)
            sp.dma_start(W_PQ[:], w_pq).then_inc(s_wpq, 16)
            sp.wait_ge(s_tile, tile_no("qr", 3) + 1)
            sp.dma_start(KEYS[:], keys).then_inc(s_keys, 16)

            for j in range(4):
                sp.wait_ge(s_ada, ADA - 3 + j)
                sp.dma_start(RING[:, j, :], u_tab[j]).then_inc(s_ring[j], 16)
            with sp.Fori(1, BLOCKS // 4) as i:
                for j in range(4):
                    sp.wait_ge(s_ul, i * 4 + j - 3)
                    sp.dma_start(RING[:, j, :], u_tab[bass.ds(i * 4 + j, 1)].rearrange("o p d -> (o p) d"))\
                      .then_inc(s_ring[j], 16)
            for j in range(4):
                sp.wait_ge(s_ul, BLOCKS - 3 + j)
                sp.dma_start(RING[:, j, :], v_tab[j]).then_inc(s_ring[j], 16)
            sp.wait_ge(s_umm, BLOCKS)
            sp.dma_start(GFB[:], g_final.partition_broadcast(P)).then_inc(s_gf, 16)
            with sp.Fori(1, BLOCKS // 4) as i:
                for j in range(4):
                    sp.wait_ge(s_vl, i * 4 + j - 3)
                    sp.dma_start(RING[:, j, :], v_tab[bass.ds(i * 4 + j, 1)].rearrange("o p d -> (o p) d"))\
                      .then_inc(s_ring[j], 16)
            for tt in range(TT):
                sp.wait_ge(s_e5, tt + 1)
                sp.dma_start(out[tt * P:(tt + 1) * P, :], EPI[:, tt, 0, :]).then_inc(s_out, 16)
            sp.wait_ge(s_out, 16 * TT)

        @block.gpsimd
        def _(pool):
            nc.gpsimd.memset(ONES[:], 1.0).then_inc(s_ones, 1)
            nc.gpsimd.memset(QM[:], 0.0).then_inc(s_zero, 1)
            pool.wait_ge(s_tile, 4)
            nc.gpsimd.memset(QN[:], 0.0).then_inc(s_zeroq, 1)
            nc.gpsimd.memset(QR[:], 0.0).then_inc(s_zeroq, 1)

        @block.scalar
        def _(act):
            act.wait_ge(s_vec, 16)
            nc.scalar.activation(SILU[:, 0, :], VEC[:, V_C:V_C + KD], ACT.Exp, scale=-1.0).then_inc(s_exp, 1)
            act.wait_ge(s_x, 16)
            for k in range(KD):
                nc.scalar.activation(SQ[:, k, :], XT[:, k, :], ACT.Square).then_inc(s_sq, 1)

            def root(n, width, bank):
                act.wait_ge(s_ssq, n + 1)
                nc.scalar.activation(RSTD[:], PS[:, bank, 0:T], ACT.Sqrt, bias=VEC[:, V_EPS:V_EPS + 1],
                                     scale=1.0 / width).then_inc(s_root, 1)

            root(0, D, 5)
            act.wait_ge(s_ang, 1)
            nc.scalar.activation(SIN[:], ANG[:, 1, :], ACT.Sin).then_inc(s_trig, 1)
            nc.scalar.activation(COS[:], ANG[:, 2, :], ACT.Sin).then_inc(s_trig, 1)

            for n, (kind, i) in enumerate(TILES):
                bank = n % 4
                if kind in ACT_READS:
                    act.wait_ge(s_tile, n + 1)
                if kind in ("cq", "ckv"):
                    act.wait_ge(s_dread, n + 1)
                    if n == 0:
                        act.wait_ge(s_ssq, 1)
                    nc.scalar.activation(SQ[:, n, :], CQT[:, n, :], ACT.Square).then_inc(s_sq, 1)
                elif kind in ("mq", "qn"):
                    to = QM if kind == "mq" else QN
                    act.wait_ge(s_zero if kind == "mq" else s_zeroq, 1)
                    nc.scalar.copy(to[0:64, 2 * i, :], PS[0:64, bank, 0:T])
                    nc.scalar.copy(to[64:128, 2 * i + 1, :], PS[64:128, bank, 0:T]).then_inc(s_aread, 1)
                elif kind in ("mk", "kn"):
                    nc.scalar.copy((KM if kind == "mk" else KN)[:, i, :], PS[:, bank, 0:T]).then_inc(s_aread, 1)
                elif kind in ACT_READS:
                    nc.scalar.copy((VM if kind == "mv" else VN)[:, i, :], PS[:, bank, :]).then_inc(s_aread, 1)
                if (kind, i) == ("ckv", CKV - 1):
                    act.wait_ge(s_h, 2 * KD)
                    root(1, Q_LORA, 4)
                    act.wait_ge(s_lat, CQ)
                    root(2, KV_LORA, 5)

            N = len(UNITS)
            for step in range(N + 2):
                if step < N:
                    u, b = step, step % 2
                    W = P * (UNITS[u][1] + 1)
                    act.wait_ge(s_nm, u + 1)
                    if u >= 2:
                        act.wait_ge(s_t, u - 1)
                    for j in range(2):
                        ins = nc.scalar.activation(PR[:, b, j, 0:W], S[:, b, j, 0:W], ACT.Exp,
                                                   bias=NMAX[:, b, j:j + 1], accum_out=SUM[:, b, j:j + 1])
                    ins.then_inc(s_p, 1)
                if 1 <= step <= N:
                    u, b = step - 1, (step - 1) % 2
                    nb = UNITS[u][1] + 1
                    act.wait_ge(s_t, u + 1)
                    if u >= 2:
                        act.wait_ge(s_o, u - 1)
                    nc.scalar.copy(PT[:, b, :, 0:nb, :],
                                   PS[:, 6 + b, 0:2 * nb * P].rearrange("p (j n q) -> p j n q", j=2, n=nb))\
                      .then_inc(s_pt, 1)
                if step >= 2:
                    u, b = step - 2, (step - 2) % 2
                    g, qt = UNITS[u]
                    act.wait_ge(s_o, u + 1)
                    nc.scalar.copy(OT[0:64, g, qt * P:(qt + 1) * P], PS[0:64, b, 0:P])
                    nc.scalar.copy(OT[64:128, g, qt * P:(qt + 1) * P], PS[64:128, b, P:2 * P]).then_inc(s_ot, 1)

            for d in range(KD):
                act.wait_ge(s_x1, d + 1)
                nc.scalar.activation(SQ[:, d, :], XT[:, d, :], ACT.Square).then_inc(s_sq, 1)
            root(3, D, 4)
            for k in range(KD):
                act.wait_ge(s_h2, k + 1)
                nc.scalar.copy(H2H[:, k, :], HT[:, k, :]).then_inc(s_h2h, 1)
            for h in range(PH):
                act.wait_ge(s_q, h + 1)
                nc.scalar.copy(QP[:, h, :], PS[:, h % 4, 0:T]).then_inc(s_qc, 1)
            for n in range(TT * PH):
                act.wait_ge(s_k, n + 1)
                nc.scalar.copy(SC[:, n].rearrange("p a b -> p (a b)"), PS[:, 4 + n % 4, 0:T]).then_inc(s_sc, 1)

            def u_step(j, at, first=False):
                act.wait_ge(s_ring[j], at * 4 + (ADA * 4 + 16))
                if not first or j >= 2:
                    act.wait_ge(s_umm, at + j - 1)
                nc.scalar.copy(HI[:, j % 2, :], RING[:, j, :]).then_inc(s_uh, 1)
                if not first or j >= 2:
                    nc.scalar.activation(AG[:, bass.ds(at + j - 2, 1), :].rearrange("p o t -> p (o t)"),
                                         PS[:, (j + 2) % 4, 0:T], ACT.Gelu).then_inc(s_gelu, 1)

            for j in range(4):
                u_step(j, 0, first=True)
            with act.Fori(1, 24) as i:
                for j in range(4):
                    u_step(j, i * 4)
            act.wait_ge(s_best, 1)
            nc.scalar.activation(GTOK[:], GTOK[:], ACT.Exp).then_inc(s_gexp, 1)
            with act.Fori(24, BLOCKS // 4) as i:
                for j in range(4):
                    u_step(j, i * 4)
            for b in range(BLOCKS - 2, BLOCKS):
                act.wait_ge(s_umm, b + 1)
                nc.scalar.activation(AG[:, b, :], PS[:, b % 4, 0:T], ACT.Gelu).then_inc(s_gelu, 1)
            for b in range(4):
                act.wait_ge(s_x1t, b + 1)
                nc.scalar.copy(X1[:, b // 2, (b % 2) * 512:(b % 2 + 1) * 512], PS[:, b, :]).then_inc(s_x1c, 1)

            def v_step(j, at, first=False):
                act.wait_ge(s_ring[j], at * 4 + ((ADA + BLOCKS) * 4 + 16))
                if not first or j >= 2:
                    act.wait_ge(s_vmm, at + j - 1)
                nc.scalar.copy(HI[:, j % 2, :], RING[:, j, :]).then_inc(s_vh, 1)
                if first and j == 0:
                    act.wait_ge(s_gated, T // 4)
                nc.scalar.copy(WH[:, j % 2, :], AG[:, bass.ds(at + j, 1), :].rearrange("p o t -> p (o t)"))\
                  .then_inc(s_vh, 1)

            for j in range(4):
                v_step(j, 0, first=True)
            with act.Fori(1, BLOCKS // 4) as i:
                for j in range(4):
                    v_step(j, i * 4)
            for tt in range(TT):
                act.wait_ge(s_e2, tt + 1)
                nc.scalar.activation(EPI[:, tt, 0, :], EPI[:, tt, 1, :], ACT.Square,
                                     accum_out=SSQ[:, 0, tt:tt + 1]).then_inc(s_e3, 1)
            act.wait_ge(s_e3, TT)
            nc.scalar.activation(SSQ[:, 1, :], SSQ[:, 0, :], ACT.Sqrt, bias=VEC[:, V_EPS:V_EPS + 1],
                                 scale=1.0 / D).then_inc(s_e4, 1)

        @block.vector
        def _(dve):
            V = nc.vector
            done = [0]

            def step(ins):
                ins.then_inc(s_d, 1)
                done[0] += 1
                dve.wait_ge(s_d, done[0])

            dve.wait_ge(s_exp, 1)
            step(V.tensor_scalar(SILU[:, 1, :], SILU[:, 0, :], 1.0, None, ALU.add))
            step(V.reciprocal(SILU[:, 0, :], SILU[:, 1, :]))
            V.tensor_tensor(SILU[:, 2, :], SILU[:, 0, :], VEC[:, V_C:V_C + KD], ALU.mult).then_inc(s_silu, 1)

            dve.wait_ge(s_pos, 16)
            step(V.tensor_copy(ANG[:, 1, :], ANG[:, 0, :].bitcast(I32)))
            step(V.tensor_scalar(ANG[:, 0, :], ANG[:, 1, :], VEC[:, V_INV:V_INV + 1], None, ALU.mult))
            step(V.tensor_scalar(ANG[:, 1, :], ANG[:, 0, :], 1.0 / TWO_PI, ROUND, ALU.mult, ALU.add))
            step(V.tensor_scalar(ANG[:, 1, :], ANG[:, 1, :], ROUND, None, ALU.subtract))
            for c in (C1, C2, C3):
                step(V.scalar_tensor_tensor(out=ANG[:, 0, :], in0=ANG[:, 1, :], scalar=-c, in1=ANG[:, 0, :],
                                            op0=ALU.mult, op1=ALU.add))
            step(V.tensor_scalar(ANG[:, 1, :], ANG[:, 0, :], PI_IN, -PI_IN, ALU.min, ALU.max))
            step(V.scalar_tensor_tensor(out=ANG[:, 2, :], in0=ANG[:, 1, :], scalar=-1.0, in1=ANG[:, 1, :],
                                        op0=ALU.mult, op1=ALU.max))
            V.tensor_scalar(ANG[:, 2, :], ANG[:, 2, :], -1.0, HALF_PI, ALU.mult, ALU.add).then_inc(s_ang, 1)

            def modulated(gain, shift, n, to):
                dve.wait_ge(s_root, n)
                step(V.reciprocal(RSTD[:], RSTD[:]))
                for k in range(KD):
                    step(V.tensor_tensor(HT[:, k, :], XT[:, k, :], RSTD[:], ALU.mult))
                    V.tensor_scalar(HT[:, k, :], HT[:, k, :], gain[:, k:k + 1], MOD[:, shift + k:shift + k + 1],
                                    ALU.mult, ALU.add).then_inc(to, 1)

            dve.wait_ge(s_mod, 1)
            step(V.tensor_tensor(MOD[:, 0:ADA_FIRST], PS[:, 7, 0:ADA_FIRST], VEC[:, V_B:V_B + ADA_FIRST], ALU.add))
            step(V.scalar_tensor_tensor(out=GAIN1[:], in0=MOD[:, SC_A:SC_A + KD], scalar=1.0,
                                        in1=VEC[:, V_GMIX:V_GMIX + KD], op0=ALU.add, op1=ALU.mult))
            modulated(GAIN1, SH_A, 1, s_h)
            dve.wait_ge(s_trig, 2)
            V.tensor_scalar(SIN[:], SIN[:], VEC[:, V_SGN:V_SGN + 1], None, ALU.mult).then_inc(s_rope, 1)
            dve.wait_ge(s_rope, 1)
            dve.wait_ge(s_const, 16)
            nc.vector.sem_inc(s_h, KD)

            rotated = [0]

            def rotate(n, i):
                a, b = PS[:, n % 4, 0:T], PS[:, (n + 1) % 4, 0:T]
                dve.wait_ge(s_tile, n + 2)
                dve.wait_ge(s_rope, 1 + rotated[0])
                V.tensor_tensor(RT[:, 0, :], a, COS[:], ALU.mult).then_inc(s_dread, 1)
                V.tensor_tensor(RT[:, 1, :], b, SIN[:], ALU.mult).then_inc(s_dread, 1)
                dve.wait_ge(s_dread, dve_reads(n + 1))
                if i is None:
                    V.tensor_tensor(KR[:], RT[:, 0, :], RT[:, 1, :], ALU.add).then_inc(s_rope, 1)
                else:
                    for h in range(4):
                        r = slice(32 * h, 32 * h + 32)
                        ins = V.tensor_tensor(QR[r, 4 * i + h, :], RT[r, 0, :], RT[r, 1, :], ALU.add)
                    ins.then_inc(s_rope, 1)
                rotated[0] += 1

            def latent(first, count, gain):
                step(V.reciprocal(RSTD[:], RSTD[:]))
                for i in range(count):
                    V.scalar_tensor_tensor(out=CQT[:, first + i, :], in0=CQT[:, first + i, :],
                                           scalar=VEC[:, gain + i:gain + i + 1], in1=RSTD[:],
                                           op0=ALU.mult, op1=ALU.mult).then_inc(s_lat, 1)

            for n, (kind, i) in enumerate(TILES):
                if kind in ("cq", "ckv"):
                    dve.wait_ge(s_tile, n + 1)
                    V.tensor_copy(CQT[:, n, :], PS[:, n % 4, 0:T]).then_inc(s_dread, 1)
                    if (kind, i) == ("ckv", CKV - 1):
                        dve.wait_ge(s_root, 2)
                        dve.wait_ge(s_dread, n + 1)
                        latent(0, CQ, V_GQA)
                        dve.wait_ge(s_root, 3)
                        latent(CQ, CKV, V_GKVA)
                elif kind == "kr" and i == 0:
                    rotate(n, None)
                    dve.wait_ge(s_bias, 16)
                    V.tensor_tensor(BT[:], BT[:], MASK.unsqueeze(1).broadcast_to([P, HEADS, T]), ALU.add)\
                     .then_inc(s_mask, 1)
                    dve.wait_ge(s_mask, 1)
                elif kind == "qr" and i % 2 == 0:
                    if i == 0:
                        dve.wait_ge(s_zeroq, 2)
                    rotate(n, i // 2)
            dve.wait_ge(s_mod, 2)
            V.tensor_tensor(MOD[:, ADA_FIRST:ADA], PS[:, 6, 0:ADA - ADA_FIRST],
                            VEC[:, V_B + ADA_FIRST:V_B + ADA], ALU.add).then_inc(s_modc, 1)
            dve.wait_ge(s_modc, 1)
            step(V.scalar_tensor_tensor(out=GAIN2[:], in0=MOD[:, SC_F:SC_F + KD], scalar=1.0,
                                        in1=VEC[:, V_GFFN:V_GFFN + KD], op0=ALU.add, op1=ALU.mult))

            N = len(UNITS)
            for at in range(N + 1):
                if at < N:
                    u, b = at, at % 2
                    g, qt = UNITS[u]
                    W = P * (qt + 1)
                    dve.wait_ge(s_s, u + 1)
                    if u >= 2:
                        dve.wait_ge(s_p, u - 1)
                    if g < PAIRS:
                        V.scalar_tensor_tensor(out=S[:, b, :, 0:W],
                                               in0=PS[:, 4 + b, 0:2 * W].rearrange("p (j k) -> p j k", j=2),
                                               scalar=MLA_SCALE,
                                               in1=MASK[:, T - W:T].unsqueeze(1).broadcast_to([P, 2, W]),
                                               op0=ALU.mult, op1=ALU.add).then_inc(s_sm, 1)
                    else:
                        h = 2 * (g - PAIRS)
                        V.scalar_tensor_tensor(out=S[:, b, :, 0:W],
                                               in0=PS[:, 4 + b, 0:2 * W].rearrange("p (j k) -> p j k", j=2),
                                               scalar=MOBA_SCALE, in1=BT[:, h:h + 2, T - W:T],
                                               op0=ALU.mult, op1=ALU.add).then_inc(s_sm, 1)
                    dve.wait_ge(s_sm, u + 1)
                    V.tensor_reduce(NMAX[:, b, :], S[:, b, :, 0:W], AX.X, ALU.max, negate=True).then_inc(s_nm, 1)
                if at >= 1:
                    u, b = at - 1, (at - 1) % 2
                    W = P * (UNITS[u][1] + 1)
                    dve.wait_ge(s_p, u + 1)
                    step(V.reciprocal(REC[:, b, :], SUM[:, b, :]))
                    for j in range(2):
                        ins = V.tensor_scalar(PR[:, b, j, 0:W], PR[:, b, j, 0:W], REC[:, b, j:j + 1], None, ALU.mult)
                    ins.then_inc(s_pn, 1)

            for d in range(KD):
                dve.wait_ge(s_y, d + 1)
                V.scalar_tensor_tensor(out=XT[:, d, :], in0=PS[:, d % 4, 0:T],
                                       scalar=MOD[:, GT_A + d:GT_A + d + 1], in1=XT[:, d, :],
                                       op0=ALU.mult, op1=ALU.add).then_inc(s_x1, 1)
            modulated(GAIN2, SH_F, 4, s_h2)
            for k in range(KD):
                dve.wait_ge(s_h2h, k + 1)
                V.tensor_tensor(H2L[:, k, :], HT[:, k, :], H2H[:, k, :].bitcast(F32), ALU.subtract).then_inc(s_h2l, 1)

            def low(j, at):
                dve.wait_ge(s_uh, at + j + 1)
                V.tensor_tensor(LO[:, j % 2, :], RING[:, j, :], HI[:, j % 2, :].bitcast(F32), ALU.subtract)\
                 .then_inc(s_ul, 1)

            STEPS = 20
            dve.wait_ge(s_sc, TT * PH)
            with dve.Fori(0, TT * PH) as u:
                count = [0]

                def ranked(ins):
                    ins.then_inc(s_tk, 1)
                    count[0] += 1

                def settled():
                    dve.wait_ge(s_tk, u * STEPS + count[0])
                    V.sem_inc(s_held, 1)

                low(0, u * 4)
                ranked(V.tensor_copy(WK[:], SC[:, bass.ds(u, 1)].rearrange("p o a b -> p (o a) b")))
                settled()
                for p in range(2):
                    ranked(V.max(TV[:, p, 0:8], WK[:, p, :]))
                settled()
                for p in range(2):
                    ranked(V.max_index(TIU[:, p, 0:8], TV[:, p, 0:8], WK[:, p, :]))
                settled()
                for p in range(2):
                    ranked(V.match_replace(WK[:, p, :], TV[:, p, 0:8], WK[:, p, :], LOWEST))
                low(1, u * 4)
                settled()
                for p in range(2):
                    ranked(V.max(TV[:, p, 8:16], WK[:, p, :]))
                settled()
                for p in range(2):
                    ranked(V.max_index(TIU[:, p, 8:16], TV[:, p, 8:16], WK[:, p, :]))
                ranked(V.tensor_tensor(CAND[:], TV[:, 0, :].unsqueeze(2).broadcast_to([P, TOPK, TOPK]),
                                       TV[:, 1, :].unsqueeze(1).broadcast_to([P, TOPK, TOPK]), ALU.add))
                settled()
                low(2, u * 4)
                cand = CAND[:].rearrange("p a b -> p (a b)")
                ranked(V.max(BV[:, 0:8], cand))
                settled()
                ranked(V.max_index(PU[:, 0:8], BV[:, 0:8], cand))
                settled()
                ranked(V.match_replace(cand, BV[:, 0:8], cand, LOWEST))
                settled()
                ranked(V.max(BV[:, 8:16], cand))
                settled()
                low(3, u * 4)
                ranked(V.max_index(PU[:, 8:16], BV[:, 8:16], cand))
                settled()
                ranked(V.tensor_copy(TI[:, bass.ds(u, 1)].rearrange("p o a b -> p (o a) b"), TIU[:]))
                ranked(V.tensor_copy(BEST[:, bass.ds(u, 1)].rearrange("p o a -> p (o a)"), BV[:]))
                ranked(V.tensor_copy(POS[:, bass.ds(u, 1)].rearrange("p o a -> p (o a)"), PU[:]))
                assert count[0] == STEPS, count

            low(0, 64)
            dve.wait_ge(s_tk, STEPS * TT * PH)
            step(V.tensor_scalar(AIU[:, 0], POS[:], 4, None, ALU.logical_shift_right))
            step(V.tensor_scalar(AIU[:, 1], POS[:], 15, None, ALU.bitwise_and))
            step(V.tensor_copy(AIF[:], AIU[:]))
            V.tensor_tensor(GTOK[:], BEST[:], BEST[:, :, 0:1].broadcast_to([P, TT * PH, TOPK]), ALU.subtract)\
             .then_inc(s_best, 1)
            b = 1
            iota16 = IOTA[:, 0:TOPK].unsqueeze(1).unsqueeze(1).broadcast_to([P, 4, TOPK, TOPK])
            for p in range(2):
                for q in range(TT * PH // 4):
                    hs = slice(4 * q, 4 * q + 4)
                    step(V.tensor_tensor(EQ[:], AIF[:, p, hs].unsqueeze(3).broadcast_to([P, 4, TOPK, TOPK]), iota16,
                                         ALU.is_equal))
                    low(b % 4, 64 + b // 4 * 4)
                    step(V.tensor_tensor(EQ[:], EQ[:], TI[:, hs, p].unsqueeze(2).broadcast_to([P, 4, TOPK, TOPK]),
                                         ALU.mult))
                    low((b + 1) % 4, 64 + (b + 1) // 4 * 4)
                    step(V.tensor_reduce(ITOK[:, p, hs, :], EQ[:], AX.X, ALU.add))
                    low((b + 2) % 4, 64 + (b + 2) // 4 * 4)
                    b += 3
            while b < 40:
                low(b % 4, 64 + b // 4 * 4)
                b += 1
            dve.wait_ge(s_gexp, 1)
            step(V.tensor_reduce(GSUM[:], GTOK[:], AX.X, ALU.add))
            step(V.reciprocal(GREC[:], GSUM[:]))
            V.tensor_tensor(GTOK[:], GTOK[:], GREC[:].unsqueeze(2).broadcast_to([P, TT * PH, TOPK]), ALU.mult)\
             .then_inc(s_ranks, 1)
            with dve.Fori(26, BLOCKS // 4) as i:
                for j in range(4):
                    low(j, i * 4)

            for k in range(KD):
                ins = V.tensor_scalar(DIAG[:, k, :], IDENT, MOD[:, GT_F + k:GT_F + k + 1], None, ALU.mult)
            ins.then_inc(s_diag, 1)
            dve.wait_ge(s_rt, 1)
            V.tensor_copy(RANKED[:, 0:2, :], PS[:, 6, :].rearrange("p (a t) -> p a t", a=2)).then_inc(s_ranked, 1)
            V.tensor_copy(RANKED[:, 2, :], PS[:, 7, 0:T]).then_inc(s_ranked, 1)
            dve.wait_ge(s_gtb, 1)
            V.tensor_copy(GTB[:], PS[:, 4:6, :].rearrange("p a b -> p (a b)")).then_inc(s_gtbc, 1)
            dve.wait_ge(s_ranked, 2)
            dve.wait_ge(s_gelu, BLOCKS)

            def onehots(j, t0):
                for t in range(4):
                    at = bass.ds(t0 + t, 1)
                    V.tensor_scalar(OHJ[:, j, t, :], IOTA, RANKED[:, 2, at], RANKED[:, 0, at], ALU.is_equal, ALU.mult)
                    ins = V.tensor_scalar(OHI[:, j, t, :], IOTA, RANKED[:, 1, at], None, ALU.is_equal)
                ins.then_inc(s_oh, 1)

            def gated(j, t0):
                a = AG[:, :, bass.ds(t0, 4)]
                V.tensor_tensor(a, PS[:, 4 + j, :].rearrange("p (t i) -> p i t", t=4), a, ALU.mult).then_inc(s_gated, 1)

            onehots(0, 0)
            onehots(1, 4)
            dve.wait_ge(s_gmm, 1)
            gated(0, 0)
            with dve.Fori(1, T // 8) as i:
                for j in range(2):
                    dve.wait_ge(s_gmm, i * 2 + j - 1)
                    onehots(j, i * 8 + 4 * j)
                    dve.wait_ge(s_gmm, i * 2 + j)
                    gated(1 - j, i * 8 + 4 * j - 4)
            dve.wait_ge(s_gmm, T // 4)
            gated(1, T - 4)

            def v_low(j, at):
                dve.wait_ge(s_vh, at * 2 + (2 * j + 2))
                V.tensor_tensor(LO[:, j % 2, :], RING[:, j, :], HI[:, j % 2, :].bitcast(F32), ALU.subtract)\
                 .then_inc(s_vl, 1)
                V.tensor_tensor(WL[:, j % 2, :], AG[:, bass.ds(at + j, 1), :].rearrange("p o t -> p (o t)"),
                                WH[:, j % 2, :].bitcast(F32), ALU.subtract).then_inc(s_e1, 1)

            with dve.Fori(0, BLOCKS // 4) as i:
                for j in range(4):
                    v_low(j, i * 4)
            dve.wait_ge(s_vmm, BLOCKS)
            dve.wait_ge(s_x1c, 4)
            dve.wait_ge(s_gtbc, 1)
            for tt in range(TT):
                step(V.tensor_tensor(EPI[:, tt, 0, :], PS[:, 2 * tt:2 * tt + 2, :].rearrange("p a b -> p (a b)"), GTB[:],
                                     ALU.mult))
                V.tensor_tensor(EPI[:, tt, 1, :], EPI[:, tt, 0, :], X1[:, tt, :], ALU.add).then_inc(s_e2, 1)
            dve.wait_ge(s_e4, 1)
            step(V.reciprocal(SSQ[:, 2, :], SSQ[:, 1, :]))
            dve.wait_ge(s_gf, 16)
            for tt in range(TT):
                V.scalar_tensor_tensor(out=EPI[:, tt, 0, :], in0=EPI[:, tt, 1, :], scalar=SSQ[:, 2, tt:tt + 1],
                                       in1=GFB[:], op0=ALU.mult, op1=ALU.mult).then_inc(s_e5, 1)

        @block.tensor
        def _(pe):
            mm = nc.tensor.matmul

            def sum_squares(bank, first, count):
                for k in range(count):
                    ins = mm(PS[:, bank, 0:T], ONES[:], SQ[:, first + k, :], start=(k == 0), stop=(k == count - 1))
                ins.then_inc(s_ssq, 1)

            def ada(c, bank, col):
                pe.wait_ge(s_ring[c % 4], 16 * (c // 4 + 1))
                w = RING[:, c % 4, :].rearrange("p (k n) -> p k n", k=KD)
                for k in range(KD):
                    ins = mm(PS[:, bank, col:col + 1], w[:, k, :], SILU[:, 2, k:k + 1], start=(k == 0), stop=(k == KD - 1))
                ins.then_inc(s_ada, 1)
                return ins

            pe.wait_ge(s_ones, 1)
            pe.wait_ge(s_sq, KD)
            sum_squares(5, 0, KD)
            pe.wait_ge(s_silu, 1)
            for c in range(ADA_FIRST):
                ada(c, 7, c)
            pe.wait_ge(s_ada, ADA_FIRST)
            nc.tensor.sem_inc(s_mod, 1)

            W_OF = {"cq": 0, "ckv": 6, "kr": 8, "mq": 10, "mk": 14}
            chunk = ADA_FIRST
            for n, (kind, i) in enumerate(TILES):
                bank = n % 4
                if n >= 4:
                    if TILES[n - 4][0] in DVE_READS:
                        pe.wait_ge(s_dread, dve_reads(n - 4))
                    if TILES[n - 4][0] in ACT_READS:
                        pe.wait_ge(s_aread, act_reads(n - 4))
                if kind in W_OF:
                    c = W_OF[kind] + i
                    pe.wait_ge(s_win[[c < b for b in WIN_SPLIT[1:]].index(True)], 16)
                    for k in range(KD):
                        if n == 0:
                            pe.wait_ge(s_h, k + 1)
                        ins = mm(PS[:, bank, 0:T], W_IN[:, c, k, :], HT[:, k, :], start=(k == 0), stop=(k == KD - 1))
                elif kind == "mv":
                    pe.wait_ge(s_win[4], 16)
                    for k in range(KD):
                        ins = mm(PS[:, bank, :], HT[:, k, i * P:(i + 1) * P], W_MV[:, k, :], start=(k == 0), stop=(k == KD - 1))
                elif kind in ("qn", "qr"):
                    pe.wait_ge(s_wuq, 16)
                    pe.wait_ge(s_lat, CQ)
                    c = i + (PAIRS if kind == "qr" else 0)
                    for k in range(CQ):
                        ins = mm(PS[:, bank, 0:T], W_UQ[:, c, k, :], CQT[:, k, :], start=(k == 0), stop=(k == CQ - 1))
                elif kind == "kn":
                    pe.wait_ge(s_wukv, 32)
                    pe.wait_ge(s_lat, CQ + CKV)
                    for k in range(CKV):
                        ins = mm(PS[:, bank, 0:T], W_UKV[:, i, k, :], CQT[:, CQ + k, :], start=(k == 0), stop=(k == CKV - 1))
                else:
                    for k in range(CKV):
                        ins = mm(PS[:, bank, :], CQT[:, CQ + k, i * P:(i + 1) * P], W_UV[:, k, :], start=(k == 0), stop=(k == CKV - 1))
                ins.then_inc(s_tile, 1)
                if (kind, i) == ("kr", 0):
                    pe.wait_ge(s_sq, KD + CQ + CKV)
                    sum_squares(4, 0, CQ)
                    sum_squares(5, CQ, CKV)
                for _ in range(ADA_AFTER.get(n, 0)):
                    ada(chunk, 6, chunk - ADA_FIRST)
                    chunk += 1
            assert chunk == ADA
            pe.wait_ge(s_ada, ADA)
            nc.tensor.sem_inc(s_mod, 1)

            N = len(UNITS)
            pe.wait_ge(s_aread, act_reads(len(TILES) - 1))
            pe.wait_ge(s_rope, 4)
            for at in range(N + 2):
                if at < N:
                    u, b = at, at % 2
                    g, qt = UNITS[u]
                    W = P * (qt + 1)
                    if u >= 2:
                        pe.wait_ge(s_sm, u - 1)
                    for j in range(2):
                        o, q = PS[:, 4 + b, j * W:(j + 1) * W], slice(qt * P, (qt + 1) * P)
                        h = 2 * (g % PAIRS) + j
                        if g < PAIRS:
                            mm(o, QN[:, h, q], KN[:, g, 0:W], start=True, stop=False)
                            ins = mm(o, QR[:, h, q], KR[:, 0:W], start=False, stop=True)
                        else:
                            ins = mm(o, QM[:, h, q], KM[:, g - PAIRS, 0:W], start=True, stop=True)
                    ins.then_inc(s_s, 1)
                if 1 <= at <= N:
                    u, b = at - 1, (at - 1) % 2
                    nb = UNITS[u][1] + 1
                    pe.wait_ge(s_pn, u + 1)
                    if u >= 2:
                        pe.wait_ge(s_pt, u - 1)
                    if u < 2:
                        pe.wait_ge(s_modc, 1)
                    for j in range(2):
                        for n in range(nb):
                            a = (j * nb + n) * P
                            ins = nc.tensor.transpose(PS[:, 6 + b, a:a + P], PR[:, b, j, n * P:(n + 1) * P], IDENT)
                    ins.then_inc(s_t, 1)
                if at >= 2:
                    u, b = at - 2, (at - 2) % 2
                    g, qt = UNITS[u]
                    nb = qt + 1
                    pe.wait_ge(s_pt, u + 1)
                    if u >= 2:
                        pe.wait_ge(s_ot, u - 1)
                    v = (VN if g < PAIRS else VM)
                    c = slice((g % PAIRS) * P, (g % PAIRS + 1) * P)
                    for j in range(2):
                        for n in range(nb):
                            ins = mm(PS[:, b, j * P:(j + 1) * P], v[:, n, c], PT[:, b, j, n, :], start=(n == 0), stop=(n == nb - 1))
                    ins.then_inc(s_o, 1)

            pe.wait_ge(s_wout, 16)
            pe.wait_ge(s_ot, N)
            for d in range(KD):
                if d >= 4:
                    pe.wait_ge(s_x1, d - 3)
                for k in range(KD):
                    ins = mm(PS[:, d % 4, 0:T], W_OUT[:, d, k, :], OT[:, k, :], start=(k == 0), stop=(k == KD - 1))
                ins.then_inc(s_y, 1)
            pe.wait_ge(s_sq, KD + CQ + CKV + KD)
            sum_squares(4, 0, KD)
            pe.wait_ge(s_wpq, 16)
            for h in range(PH):
                pe.wait_ge(s_x1, KD)
                if h >= 4:
                    pe.wait_ge(s_qc, h - 3)
                for k in range(KD):
                    if h == 0:
                        pe.wait_ge(s_h2, k + 1)
                    ins = mm(PS[:, h % 4, 0:T], W_PQ[:, h, k, :], HT[:, k, :], start=(k == 0), stop=(k == KD - 1))
                ins.then_inc(s_q, 1)
            pe.wait_ge(s_keys, 16)
            pe.wait_ge(s_root, 4)
            for n in range(TT * PH):
                tt, h = n // PH, n % PH
                pe.wait_ge(s_qc, h + 1 if tt == 0 else PH)
                if n >= 4:
                    pe.wait_ge(s_sc, n - 3)
                mm(PS[:, 4 + n % 4, 0:T], QP[:, h, tt * P:(tt + 1) * P], KEYS[:, h, :], start=True, stop=True).then_inc(s_k, 1)

            pe.wait_ge(s_h2l, KD)

            def u_block(j, at, first=False):
                pe.wait_ge(s_uh, at + j + 1)
                if not first:
                    pe.wait_ge(s_gelu, at + j - 3)
                hi = HI[:, j % 2, :].rearrange("p (k e) -> p k e", k=KD)
                lo = LO[:, j % 2, :].rearrange("p (k e) -> p k e", k=KD)
                o = PS[:, j, 0:T]
                for k in range(KD):
                    mm(o, hi[:, k, :], H2H[:, k, :], start=(k == 0), stop=False)
                    mm(o, hi[:, k, :], H2L[:, k, :], start=False, stop=False)
                pe.wait_ge(s_ul, at + j + 1)
                for k in range(KD):
                    ins = mm(o, lo[:, k, :], H2H[:, k, :], start=False, stop=(k == KD - 1))
                ins.then_inc(s_umm, 1)

            for j in range(4):
                u_block(j, 0, first=True)
            with pe.Fori(1, BLOCKS // 4) as i:
                for j in range(4):
                    u_block(j, i * 4)

            pe.wait_ge(s_ranks, 1)
            for a, src in enumerate((GTOK[:], ITOK[:, 0], ITOK[:, 1])):
                for tt in range(TT):
                    o = a * T + tt * P
                    ins = nc.tensor.transpose(PS[:, 6 + o // 512, o % 512:o % 512 + P],
                                              src[:, tt * PH:(tt + 1) * PH, :].rearrange("p h k -> p (h k)"), IDENT)
            ins.then_inc(s_rt, 1)
            pe.wait_ge(s_diag, 1)
            for k in range(KD):
                ins = mm(PS[:, 4 + k // 4, (k % 4) * P:(k % 4 + 1) * P], ONES[:], DIAG[:, k, :], start=True, stop=True)
            ins.then_inc(s_gtb, 1)
            pe.wait_ge(s_gelu, BLOCKS)
            for b in range(4):
                for q in range(4):
                    k = (b % 2) * 4 + q
                    ins = nc.tensor.transpose(PS[:, b, q * P:(q + 1) * P], XT[:, k, (b // 2) * P:(b // 2 + 1) * P], IDENT)
                ins.then_inc(s_x1t, 1)

            def gate_block(j):
                for t in range(4):
                    ins = mm(PS[:, 4 + j, t * P:(t + 1) * P], OHJ[:, j, t, :], OHI[:, j, t, :], start=True, stop=True)
                ins.then_inc(s_gmm, 1)

            pe.wait_ge(s_gtbc, 1)
            for j in range(2):
                pe.wait_ge(s_oh, j + 1)
                gate_block(j)
            with pe.Fori(1, T // 8) as i:
                for j in range(2):
                    pe.wait_ge(s_oh, i * 2 + j + 1)
                    pe.wait_ge(s_gated, i * 2 + j - 1)
                    gate_block(j)

            def v_block(j, at, first=False, last=False):
                pe.wait_ge(s_vh, at * 2 + (2 * j + 2))
                for tt in range(TT):
                    for h in range(2):
                        mm(PS[:, 2 * tt + h, :], WH[:, j % 2, tt * P:(tt + 1) * P], HI[:, j % 2, h * 512:(h + 1) * 512],
                           start=first, stop=False)
                pe.wait_ge(s_vl, at + j + 1)
                for tt in range(TT):
                    for h in range(2):
                        mm(PS[:, 2 * tt + h, :], WH[:, j % 2, tt * P:(tt + 1) * P], LO[:, j % 2, h * 512:(h + 1) * 512],
                           start=False, stop=False)
                pe.wait_ge(s_e1, at + j + 1)
                for tt in range(TT):
                    for h in range(2):
                        ins = mm(PS[:, 2 * tt + h, :], WL[:, j % 2, tt * P:(tt + 1) * P], HI[:, j % 2, h * 512:(h + 1) * 512],
                                 start=False, stop=last)
                ins.then_inc(s_vmm, 1)

            pe.wait_ge(s_x1c, 4)
            for j in range(4):
                v_block(j, 0, first=(j == 0))
            with pe.Fori(1, BLOCKS // 4 - 1) as i:
                for j in range(4):
                    v_block(j, i * 4)
            for j in range(4):
                v_block(j, BLOCKS - 4, last=(j == 3))


def t5_bucket(n):
    nf = np.maximum(n, 16).astype(np.float32)
    large = 16 + (np.log(nf / np.float32(16)) / np.float32(np.log(64.0)) * np.float32(16)).astype(np.int32)
    return np.where(n < 16, n, np.minimum(large, 31))


def kernel(x, c, positions, w_ada, b_ada, g_mix, w_in, g_qa, w_uq, g_kva, w_ukv, rel_bias, w_out, g_ffn, w_pq,
           peer_keys, peer_u, peer_v, g_final):
    import concourse.bacc as bacc
    from concourse.bass_utils import run_bass_kernel_spmd

    f = np.ascontiguousarray
    A = np.asarray

    def cols(v):
        return A(v).reshape(-1, P).T

    def stationary(w):
        k, n = w.shape
        return w.reshape(k // P, P, n // P, P).transpose(1, 2, 0, 3)

    consts = np.zeros((P, 512), np.float32)
    consts[:, 0:128] = np.eye(P)
    consts[:, 128:256] = np.arange(P)
    consts[:, 256:512] = np.where(np.arange(T)[None, :] > P + np.arange(P)[:, None], MASKED, 0.0)

    half = ROPE // 2
    row = np.arange(P) % ROPE
    inv = np.float32(THETA) ** (-np.arange(half, dtype=np.float32) / np.float32(half))
    vecs = np.zeros((P, NVEC), np.float32)
    for at, v in ((V_C, A(c)[0]), (V_B, A(b_ada)[0]), (V_GMIX, A(g_mix)[0]), (V_GQA, A(g_qa)[0]),
                  (V_GKVA, A(g_kva)[0]), (V_GFFN, A(g_ffn)[0])):
        v = cols(v)
        vecs[:, at:at + v.shape[1]] = v
    vecs[:, V_INV] = inv[row % half]
    vecs[:, V_SGN] = np.where(row < half, -1.0, 1.0)
    vecs[:, V_EPS] = EPS

    swap = (np.arange(ROPE) + half) % ROPE
    wi = A(w_in)[0]
    kr0 = Q_LORA + KV_LORA
    m0 = kr0 + ROPE
    order = np.concatenate([np.arange(kr0), np.tile(kr0 + np.arange(ROPE), 4), np.tile(kr0 + swap, 4),
                            m0 + np.arange(1024)])
    w_in_k = np.concatenate([stationary(wi[:, order]).reshape(P, -1),
                             wi[:, m0 + 1024:].reshape(KD, P, 512).transpose(1, 0, 2).reshape(P, -1)], axis=1)
    qk = NOPE + ROPE
    heads = np.arange(HEADS)[:, None] * qk
    r = (heads + NOPE + np.arange(ROPE)).reshape(2, -1)
    rs = (heads + NOPE + swap).reshape(2, -1)
    order = np.concatenate([(heads + np.arange(NOPE)).ravel(), r[0], rs[0], r[1], rs[1]])
    w_uq_k = stationary(A(w_uq)[0][:, order])
    heads = np.arange(HEADS)[:, None] * 128
    kn = A(w_ukv)[0][:, (heads + np.arange(64)).ravel()]
    vv = A(w_ukv)[0][:, (heads + 64 + np.arange(64)).ravel()]
    w_ukv_k = np.concatenate([stationary(kn).reshape(P, -1),
                              vv.reshape(CKV, P, 512).transpose(1, 0, 2).reshape(P, -1)], axis=1)
    distance = np.maximum(P + np.arange(P)[:, None] - np.arange(T)[None, :], 0)
    rel = f(A(rel_bias)[t5_bucket(distance)].transpose(0, 2, 1))
    pk = A(peer_keys)[0]
    keys = np.zeros((P, PH, 2 * NKEYS), np.float32)
    for p in range(2):
        keys[p * 64:(p + 1) * 64, :, p * NKEYS:(p + 1) * NKEYS] = pk[:, p].transpose(2, 0, 1)

    arrays = {
        "consts": consts, "vecs": vecs, "positions": f(A(positions)[0].astype(np.int32)),
        "xT": f(A(x)[0].reshape(T, KD, P).transpose(2, 1, 0)),
        "w_ada": f(A(w_ada)[0].reshape(KD, P, ADA, P).transpose(2, 1, 0, 3).reshape(ADA, P, D)),
        "w_in": f(w_in_k), "w_uq": f(w_uq_k), "w_ukv": f(w_ukv_k), "rel": rel,
        "w_out": f(stationary(A(w_out)[0])), "w_pq": f(stationary(A(w_pq)[0])), "keys": keys,
        "u_tab": f(A(peer_u)[0].reshape(BLOCKS, P, KD, P).transpose(0, 3, 2, 1).reshape(BLOCKS, P, D)),
        "v_tab": f(A(peer_v)[0].reshape(BLOCKS, P, D)),
        "g_final": f(A(g_final)),
    }
    nc = bacc.Bacc("TRN2", target_bir_lowering=False, num_devices=1)
    aps = [nc.dram_tensor(n, a.shape, mybir.dt.from_np(a.dtype), kind="ExternalInput").ap() for n, a in arrays.items()]
    out = nc.dram_tensor("out", (T, D), F32, kind="ExternalOutput").ap()
    build(nc, *aps, out)
    r = run_bass_kernel_spmd(nc, [arrays], core_ids=[0])
    return r.results[0]["out"].reshape(1, T, D)
```

```python
from contextlib import ExitStack

import numpy as np

import concourse.bass as bass
from concourse import mybir

F32 = mybir.dt.float32
F32R = mybir.dt.float32r
BF16 = mybir.dt.bfloat16
I32 = mybir.dt.int32
U32 = mybir.dt.uint32
ALU = mybir.AluOpType
ACT = mybir.ActivationFunctionType
AX = mybir.AxisListType

P = 128
T = 256
TT = T // P
D = 1024
KD = D // P
EPS = 1e-6
Q_LORA, KV_LORA = 768, 256
CQ, CKV = Q_LORA // P, KV_LORA // P
HEADS = 8
NOPE, ROPE, HDIM = 64, 32, 64
MLA_SCALE = float((NOPE + ROPE) ** -0.5)
MOBA_SCALE = float(HDIM ** -0.5)
PAIRS = HEADS // 2
NKEYS = 128
PH = 8
TOPK = 16
GT = 8
GROUPS = T // GT
ACT_ROWS = 6
LAST_U = 28
BLOCKS = NKEYS
LOWEST = -3.0e38
MASKED = -1.0e30
THETA = 10000.0

SH_A, SC_A, GT_A, SH_F, SC_F, GT_F = (KD * i for i in range(6))
ADA = 6 * KD
ADA_FIRST = 2 * KD

V_B, V_GMIX, V_GQA, V_GKVA, V_GFFN = 0, 48, 56, 62, 64
V_INV, V_SGN, V_EPS = 72, 73, 74
NVEC = 76

TWO_PI = 2.0 * np.pi
C1 = 6.28125
C2 = float(np.float32(TWO_PI - C1).view(np.int32) & ~0xFFF)
C2 = float((np.float32(TWO_PI - C1).view(np.int32) & np.int32(~0xFFF)).view(np.float32))
C3 = float(np.float32(TWO_PI - C1 - C2))
ROUND = 12582912.0
PI_IN = 3.1415925
HALF_PI = float(np.float32(np.pi / 2))

TILES = ([("cq", i) for i in range(CQ)] + [("ckv", i) for i in range(CKV)] + [("kr", 0), ("kr", 1)]
         + [("mq", i) for i in range(PAIRS)] + [("mk", i) for i in range(PAIRS)]
         + [("mv", i) for i in range(TT)]
         + [("qn", i) for i in range(PAIRS)] + [("qr", i) for i in range(4)]
         + [("kn", i) for i in range(PAIRS)] + [("v", i) for i in range(TT)])
Z_TILES = TILES.index(("qn", 0))
DVE_READS = ("cq", "ckv", "kr", "qr")
ACT_READS = ("mq", "mk", "mv", "qn", "kn", "v")


def tile_no(kind, i=0):
    return TILES.index((kind, i))


def dve_reads(n):
    return sum(kind in DVE_READS for kind, _ in TILES[:n + 1])


def act_reads(n):
    return sum(kind in ACT_READS for kind, _ in TILES[:n + 1])


def build(nc, consts, vecs, c_row, positions, xT, w_ada, w_in, w_uq, w_ukv, rel, w_out, w_pq, keys, u_tab, v_tab,
          g_final, out):
    base = (nc.sbuf_base + 63) // 64 * 64

    def place(name, at, shape, dt=F32):
        return nc.alloc_sbuf_tensor_at(name, shape, dt, offset=base + 4 * at)

    AG = place("AG", 0, [P, BLOCKS, T])
    W_IN = place("W_IN", 0, [P, 22, KD, P])
    W_MV = W_IN[:, 18:22].rearrange("p c k n -> p (c k n)").rearrange("p (k n) -> p k n", k=KD)
    W_UQ = place("W_UQ", 22528, [P, 8, CQ, P])
    W_UKV = place("W_UKV", 28672, [P, 4, CKV, P])
    W_UV = place("W_UV", 29696, [P, CKV, 512])
    SILU = place("SILU", 30720, [P, D])
    BT = place("BT", 22528, [P, HEADS, T])
    QN = place("QN", 0, [P, HEADS, T])
    QR = place("QR", 2048, [P, HEADS, T])
    OT = place("OT", 4096, [P, KD, T])
    RT = place("RT", 4096, [P, 2, T])
    W_OUT = place("W_OUT", 6144, [P, KD, KD, P])
    W_PQ = place("W_PQ", 14336, [P, KD, KD, P])
    KEYS = place("KEYS", 24576, [P, PH, 2 * NKEYS])
    SC = place("SC", 28672, [P, TT * PH, 2, NKEYS])
    TI = place("TI", 24576, [P, TT * PH, 2, TOPK])
    BEST = place("BEST", 25088, [P, TT * PH, TOPK])
    POS = place("POS", 25344, [P, TT * PH, TOPK], U32)
    WK = place("WK", 25600, [P, 2, 2, NKEYS])
    CAND = place("CAND", 26112, [P, 2, TOPK, TOPK])
    TV = place("TV", 26624, [P, 2, 2, TOPK])
    TIU = place("TIU", 26688, [P, 2, 2, TOPK], U32)
    BV = place("BV", 26752, [P, 2, TOPK])
    PU = place("PU", 26784, [P, 2, TOPK], U32)
    AIU = place("AIU", 25600, [P, 2, TT * PH, TOPK], U32)
    AIF = place("AIF", 26112, [P, 2, TT * PH, TOPK])
    EQ = place("EQ", 26880, [P, 4, TOPK, TOPK])
    GSUM = place("GSUM", 27904, [P, TT * PH])
    GREC = place("GREC", 27920, [P, TT * PH])

    XT = place("XT", 32768, [P, KD, T])
    HT = place("HT", 34816, [P, KD, T])
    OHI = place("OHI", 34816, [P, 2, GT, P])
    DIAG = place("DIAG", 34816, [P, KD, P])
    WH = place("WH", 34816, [P, 2, T], F32R)
    WL = place("WL", 35328, [P, 2, T], F32R)
    QM = place("QM", 36864, [P, HEADS, T])
    H2H = place("H2H", 36864, [P, KD, T], F32R)
    X1 = place("X1", 36864, [P, TT, D])
    KM = place("KM", 38912, [P, PAIRS, T])
    KN = place("KN", 39936, [P, PAIRS, T])
    H2L = place("H2L", 38912, [P, KD, T], F32R)
    GTB = place("GTB", 38912, [P, D])
    GFB = place("GFB", 39936, [P, D])
    VM = place("VM", 40960, [P, TT, 512])
    VN = place("VN", 41984, [P, TT, 512])
    QP = place("QP", 40960, [P, PH, T])
    GTOK = place("GTOK", 40960, [P, TT * PH, TOPK])
    ITOK = place("ITOK", 41216, [P, 2, TT * PH, TOPK])
    RANKED = place("RANKED", 41728, [P, 3, T])
    J16 = place("J16", 42496, [P, TT, P], BF16)
    ID16 = place("ID16", 42624, [P, P], BF16)
    ONE16 = place("ONE16", 42688, [P, P], BF16)
    NI16 = place("NI16", 42752, [P, P], BF16)
    RING = place("RING", 43008, [P, 4, D])
    CQT = place("CQT", 47104, [P, CQ + CKV, T])
    S = place("S", 47104, [P, 2, 2, T])
    PR = place("PR", 48128, [P, 2, 2, T])
    HI = place("HI", 47104, [P, 2, D], F32R)
    OHJ = place("OHJ", 47104, [P, 2, GT, P])
    AWAY = place("AWAY", 49152, [P, 2, GT, P])
    SQ = place("SQ", 49152, [P, KD, T])
    PT = place("PT", 49152, [P, 2, 2, 2, P])
    LO = place("LO", 49152, [P, 2, D], F32R)
    EPI = place("EPI", 47104, [P, TT, 2, D])
    KR = place("KR", 51200, [P, T])
    COS = place("COS", 51456, [P, T])
    SIN = place("SIN", 51712, [P, T])
    RSTD = place("RSTD", 51968, [P, T])
    CONST = place("CONST", 52224, [P, 512])
    IDENT, IOTA, MASK = CONST[:, 0:128], CONST[:, 128:256], CONST[:, 256:512]
    ONES = place("ONES", 52736, [P, P])
    VEC = place("VEC", 52864, [P, NVEC])
    MOD = place("MOD", 52952, [P, ADA])
    GAIN1 = place("GAIN1", 53000, [P, KD])
    GAIN2 = place("GAIN2", 53008, [P, KD])
    NMAX = place("NMAX", 53040, [P, 2, 2])
    SUM = place("SUM", 53048, [P, 2, 2])
    REC = place("REC", 53056, [P, 2, 2])
    SSQ = place("SSQ", 53064, [P, 3, TT])
    ANG = CQT

    with ExitStack() as ctx:
        PS = ctx.enter_context(nc.psum_tensor("PS", [P, 8, 512], F32))

        def sem(name):
            return ctx.enter_context(nc.semaphore(name))

        s_const, s_vec, s_pos, s_x, s_bias = (sem(n) for n in ("s_const", "s_vec", "s_pos", "s_x", "s_bias"))
        s_win = [sem(f"s_win{i}") for i in range(5)]
        s_wuq, s_wukv, s_wout, s_wpq, s_keys = (sem(n) for n in ("s_wuq", "s_wukv", "s_wout", "s_wpq", "s_keys"))
        s_ring = [sem(f"s_ring{j}") for j in range(4)]
        s_gf, s_out = sem("s_gf"), sem("s_out")
        s_ones, s_zero, s_zeroq = sem("s_ones"), sem("s_zero"), sem("s_zeroq")
        s_c, s_silu = sem("s_c"), sem("s_silu")
        s_sq, s_ssq, s_root, s_rstd = sem("s_sq"), sem("s_ssq"), sem("s_root"), sem("s_rstd")
        s_ada, s_modc, s_h = sem("s_ada"), sem("s_modc"), sem("s_h")
        s_ang, s_trig = sem("s_ang"), sem("s_trig")
        s_tile, s_dread, s_aread = sem("s_tile"), sem("s_dread"), sem("s_aread")
        s_lat, s_rope, s_mask = sem("s_lat"), sem("s_rope"), sem("s_mask")
        s_s, s_sm, s_nm, s_p, s_pn, s_t, s_pt, s_o, s_ot = (
            sem(n) for n in ("s_s", "s_sm", "s_nm", "s_p", "s_pn", "s_t", "s_pt", "s_o", "s_ot"))
        s_y, s_x1, s_h2, s_h2h, s_h2l = (sem(n) for n in ("s_y", "s_x1", "s_h2", "s_h2h", "s_h2l"))
        s_q, s_qc, s_k, s_sc = (sem(n) for n in ("s_q", "s_qc", "s_k", "s_sc"))
        s_uh, s_ul, s_umm, s_gelu = (sem(n) for n in ("s_uh", "s_ul", "s_umm", "s_gelu"))
        s_tk, s_held, s_best, s_gexp, s_ranks, s_rt, s_ranked = (
            sem(n) for n in ("s_tk", "s_held", "s_best", "s_gexp", "s_ranks", "s_rt", "s_ranked"))
        s_diag, s_gtb, s_x1t, s_x1c, s_gtbc = (sem(n) for n in ("s_diag", "s_gtb", "s_x1t", "s_x1c", "s_gtbc"))
        s_z16, s_z, s_away, s_ohi, s_ohj, s_gmm, s_gated = (
            sem(n) for n in ("s_z16", "s_z", "s_away", "s_ohi", "s_ohj", "s_gmm", "s_gated"))
        s_vh, s_vl, s_vmm = sem("s_vh"), sem("s_vl"), sem("s_vmm")
        s_e1, s_e2, s_e3, s_e4, s_e5 = (sem(f"s_e{i}") for i in range(1, 6))
        s_d = sem("s_d")

        block = ctx.enter_context(nc.Block())

        UNITS = [(g, qt) for g in range(2 * PAIRS) for qt in range(TT)]
        WIN_SPLIT = [0, 6, 10, 14, 18, 22]

        @block.sync
        def _(sp):
            sp.dma_start(SILU[:], c_row.partition_broadcast(P)).then_inc(s_c, 16)

            def load_ada(c):
                if c >= 4:
                    sp.wait_ge(s_ada, c - 3)
                sp.dma_start(RING[:, c % 4, :], w_ada[c]).then_inc(s_ring[c % 4], 16)

            def load_in(i):
                a, b = WIN_SPLIT[i], WIN_SPLIT[i + 1]
                sp.dma_start(W_IN[:, a:b].rearrange("p c k n -> p (c k n)"),
                             w_in[:, a * D:b * D]).then_inc(s_win[i], 16)

            for c in range(4):
                load_ada(c)
            sp.dma_start(XT[:], xT).then_inc(s_x, 16)
            sp.dma_start(VEC[:], vecs).then_inc(s_vec, 16)
            sp.dma_start(CONST[:], consts).then_inc(s_const, 16)
            sp.dma_start(ANG[:, 0, :].bitcast(I32), positions.partition_broadcast(P)).then_inc(s_pos, 16)
            for c in range(4, ADA_FIRST):
                load_ada(c)
            load_in(0)
            load_in(1)
            for c in range(ADA_FIRST, ADA_FIRST + 4):
                load_ada(c)
            for i in range(2, 5):
                load_in(i)
            sp.dma_start(W_UQ[:], w_uq).then_inc(s_wuq, 16)
            sp.dma_start(W_UKV[:], w_ukv[:, 0:1024]).then_inc(s_wukv, 16)
            sp.dma_start(W_UV[:], w_ukv[:, 1024:2048]).then_inc(s_wukv, 16)
            for c in range(ADA_FIRST + 4, ADA):
                load_ada(c)
            sp.wait_ge(s_tile, Z_TILES)
            sp.dma_start(W_OUT[:], w_out).then_inc(s_wout, 16)
            sp.dma_start(W_PQ[:], w_pq).then_inc(s_wpq, 16)
            sp.wait_ge(s_tile, tile_no("qr", 3) + 1)
            sp.dma_start(BT[:], rel).then_inc(s_bias, 16)
            sp.dma_start(KEYS[:], keys).then_inc(s_keys, 16)

            for j in range(4):
                sp.wait_ge(s_ada, ADA - 3 + j)
                sp.dma_start(RING[:, j, :], u_tab[j]).then_inc(s_ring[j], 16)
            with sp.Fori(1, BLOCKS // 4) as i:
                for j in range(4):
                    sp.wait_ge(s_ul, i * 4 + j - 3)
                    sp.dma_start(RING[:, j, :], u_tab[bass.ds(i * 4 + j, 1)].rearrange("o p d -> (o p) d"))\
                      .then_inc(s_ring[j], 16)
            for j in range(4):
                sp.wait_ge(s_ul, BLOCKS - 3 + j)
                sp.dma_start(RING[:, j, :], v_tab[j]).then_inc(s_ring[j], 16)
            sp.wait_ge(s_umm, BLOCKS)
            sp.dma_start(GFB[:], g_final.partition_broadcast(P)).then_inc(s_gf, 16)
            with sp.Fori(1, BLOCKS // 4) as i:
                for j in range(4):
                    sp.wait_ge(s_vl, i * 4 + j - 3)
                    sp.dma_start(RING[:, j, :], v_tab[bass.ds(i * 4 + j, 1)].rearrange("o p d -> (o p) d"))\
                      .then_inc(s_ring[j], 16)
            for tt in range(TT):
                sp.wait_ge(s_e5, tt + 1)
                sp.dma_start(out[tt * P:(tt + 1) * P, :], EPI[:, tt, 0, :]).then_inc(s_out, 16)
            sp.wait_ge(s_out, 16 * TT)

        @block.gpsimd
        def _(pool):
            nc.gpsimd.memset(ONES[:], 1.0).then_inc(s_ones, 1)
            nc.gpsimd.memset(QM[:], 0.0).then_inc(s_zero, 1)
            pool.wait_ge(s_tile, 4)
            nc.gpsimd.memset(QN[:], 0.0).then_inc(s_zeroq, 1)
            nc.gpsimd.memset(QR[:], 0.0).then_inc(s_zeroq, 1)

        @block.scalar
        def _(act):
            act.wait_ge(s_c, 16)
            nc.scalar.activation(SILU[:], SILU[:], ACT.Silu).then_inc(s_silu, 1)
            act.wait_ge(s_x, 16)
            for k in range(KD):
                nc.scalar.activation(SQ[:, k, :], XT[:, k, :], ACT.Square).then_inc(s_sq, 1)

            def root(n, width, bank):
                act.wait_ge(s_ssq, n + 1)
                nc.scalar.activation(RSTD[:], PS[:, bank, 0:T], ACT.Sqrt, bias=VEC[:, V_EPS:V_EPS + 1],
                                     scale=1.0 / width).then_inc(s_root, 1)

            act.wait_ge(s_ang, 1)
            nc.scalar.activation(SIN[:], ANG[:, 1, :], ACT.Sin).then_inc(s_trig, 1)
            nc.scalar.activation(COS[:], ANG[:, 2, :], ACT.Sin).then_inc(s_trig, 1)
            act.wait_ge(s_vec, 16)
            root(0, D, 5)

            for n, (kind, i) in enumerate(TILES):
                bank = n % 4
                if kind in ACT_READS:
                    act.wait_ge(s_tile, n + 1)
                if kind in ("cq", "ckv"):
                    act.wait_ge(s_dread, n + 1)
                    if n == 0:
                        act.wait_ge(s_ssq, 1)
                    nc.scalar.activation(SQ[:, n, :], CQT[:, n, :], ACT.Square).then_inc(s_sq, 1)
                elif kind in ("mq", "qn"):
                    to = QM if kind == "mq" else QN
                    act.wait_ge(s_zero if kind == "mq" else s_zeroq, 1)
                    nc.scalar.copy(to[0:64, 2 * i, :], PS[0:64, bank, 0:T])
                    nc.scalar.copy(to[64:128, 2 * i + 1, :], PS[64:128, bank, 0:T]).then_inc(s_aread, 1)
                elif kind in ("mk", "kn"):
                    nc.scalar.copy((KM if kind == "mk" else KN)[:, i, :], PS[:, bank, 0:T]).then_inc(s_aread, 1)
                elif kind in ACT_READS:
                    nc.scalar.copy((VM if kind == "mv" else VN)[:, i, :], PS[:, bank, :]).then_inc(s_aread, 1)
                if (kind, i) == ("ckv", CKV - 1):
                    act.wait_ge(s_h, 2 * KD)
                    root(1, Q_LORA, 4)
                    act.wait_ge(s_lat, CQ)
                    root(2, KV_LORA, 5)

            N = len(UNITS)
            for step in range(N + 3):
                if step < N:
                    u, b = step, step % 2
                    W = P * (UNITS[u][1] + 1)
                    act.wait_ge(s_nm, u + 1)
                    if u >= 2:
                        act.wait_ge(s_t, u - 1)
                    for j in range(2):
                        ins = nc.scalar.activation(PR[:, b, j, 0:W], S[:, b, j, 0:W], ACT.Exp,
                                                   bias=NMAX[:, b, j:j + 1], accum_out=SUM[:, b, j:j + 1])
                    ins.then_inc(s_p, 1)
                if 2 <= step < N + 2:
                    u, b = step - 2, step % 2
                    nb = UNITS[u][1] + 1
                    act.wait_ge(s_t, u + 1)
                    if u >= 2:
                        act.wait_ge(s_o, u - 1)
                    nc.scalar.copy(PT[:, b, :, 0:nb, :],
                                   PS[:, 6 + b, 0:2 * nb * P].rearrange("p (j n q) -> p j n q", j=2, n=nb))\
                      .then_inc(s_pt, 1)
                if step >= 3:
                    u, b = step - 3, (step - 3) % 2
                    g, qt = UNITS[u]
                    act.wait_ge(s_o, u + 1)
                    nc.scalar.copy(OT[0:64, g, qt * P:(qt + 1) * P], PS[0:64, b, 0:P])
                    nc.scalar.copy(OT[64:128, g, qt * P:(qt + 1) * P], PS[64:128, b, P:2 * P]).then_inc(s_ot, 1)

            for d in range(KD):
                act.wait_ge(s_x1, d + 1)
                nc.scalar.activation(SQ[:, d, :], XT[:, d, :], ACT.Square).then_inc(s_sq, 1)
            root(3, D, 4)
            for k in range(KD):
                act.wait_ge(s_h2, k + 1)
                nc.scalar.copy(H2H[:, k, :], HT[:, k, :]).then_inc(s_h2h, 1)
            for h in range(PH):
                act.wait_ge(s_q, h + 1)
                nc.scalar.copy(QP[:, h, :], PS[:, h % 4, 0:T]).then_inc(s_qc, 1)
            for n in range(TT * PH):
                act.wait_ge(s_k, n + 1)
                nc.scalar.copy(SC[:, n].rearrange("p a b -> p (a b)"), PS[:, 4 + n % 4, 0:T]).then_inc(s_sc, 1)

            def u_step(j, at, first=False):
                act.wait_ge(s_ring[j], at * 4 + (ADA * 4 + 16))
                if not first or j >= 2:
                    act.wait_ge(s_umm, at + j - 1)
                nc.scalar.copy(HI[:, j % 2, :], RING[:, j, :]).then_inc(s_uh, 1)
                if not first or j >= 2:
                    nc.scalar.activation(AG[:, bass.ds(at + j - 2, 1), :].rearrange("p o t -> p (o t)"),
                                         PS[:, (j + 2) % 4, 0:T], ACT.Gelu).then_inc(s_gelu, 1)

            for j in range(4):
                u_step(j, 0, first=True)
            with act.Fori(1, 24) as i:
                for j in range(4):
                    u_step(j, i * 4)
            act.wait_ge(s_best, 1)
            nc.scalar.activation(GTOK[:], GTOK[:], ACT.Exp).then_inc(s_gexp, 1)
            with act.Fori(24, BLOCKS // 4) as i:
                for j in range(4):
                    u_step(j, i * 4)
            for b in range(BLOCKS - 2, BLOCKS):
                act.wait_ge(s_umm, b + 1)
                nc.scalar.activation(AG[:, b, :], PS[:, b % 4, 0:T], ACT.Gelu).then_inc(s_gelu, 1)
            def away(j, g):
                for t in range(ACT_ROWS):
                    ins = nc.scalar.activation(AWAY[:, j, t, :], IOTA, ACT.Abs, bias=RANKED[:, 1, bass.ds(g * GT + t, 1)])
                ins.then_inc(s_away, 1)

            def onehot_i(j, g):
                act.wait_ge(s_away, g + 1)
                nc.scalar.activation(OHI[:, j, 0:ACT_ROWS], AWAY[:, j, 0:ACT_ROWS], ACT.Relu, scale=-1.0, bias=1.0)\
                  .then_inc(s_ohi, 1)

            act.wait_ge(s_ranked, 3)
            away(0, 0)
            onehot_i(0, 0)
            away(1, 1)
            for b in range(4):
                act.wait_ge(s_x1t, b + 1)
                nc.scalar.copy(X1[:, b // 2, (b % 2) * 512:(b % 2 + 1) * 512], PS[:, b, :]).then_inc(s_x1c, 1)

            with act.Fori(1, GROUPS // 2) as i:
                for j in range(2):
                    act.wait_ge(s_ohi, i * 2 + j - 1)
                    away(j, i * 2 + j)
                    act.wait_ge(s_gmm, i * 2 - 1)
                    onehot_i(1 - j, i * 2 + (j - 1))
            act.wait_ge(s_gmm, GROUPS - 2)
            onehot_i(1, GROUPS - 1)

            def v_step(j, at, first=False):
                act.wait_ge(s_ring[j], at * 4 + ((ADA + BLOCKS) * 4 + 16))
                if not first or j >= 2:
                    act.wait_ge(s_vmm, at + j - 1)
                if first and j == 0:
                    act.wait_ge(s_gmm, GROUPS)
                nc.scalar.copy(HI[:, j % 2, :], RING[:, j, :]).then_inc(s_vh, 1)
                if first and j == 0:
                    act.wait_ge(s_gated, GROUPS)
                nc.scalar.copy(WH[:, j % 2, :], AG[:, bass.ds(at + j, 1), :].rearrange("p o t -> p (o t)"))\
                  .then_inc(s_vh, 1)

            for j in range(4):
                v_step(j, 0, first=True)
            with act.Fori(1, BLOCKS // 4) as i:
                for j in range(4):
                    v_step(j, i * 4)
            for tt in range(TT):
                act.wait_ge(s_e2, tt + 1)
                nc.scalar.activation(EPI[:, tt, 0, :], EPI[:, tt, 1, :], ACT.Square,
                                     accum_out=SSQ[:, 0, tt:tt + 1]).then_inc(s_e3, 1)
            act.wait_ge(s_e3, TT)
            nc.scalar.activation(SSQ[:, 1, :], SSQ[:, 0, :], ACT.Sqrt, bias=VEC[:, V_EPS:V_EPS + 1],
                                 scale=1.0 / D).then_inc(s_e4, 1)

        @block.vector
        def _(dve):
            V = nc.vector
            done = [0]

            def step(ins):
                ins.then_inc(s_d, 1)
                done[0] += 1
                dve.wait_ge(s_d, done[0])

            def modulated(gain, shift, n, to):
                dve.wait_ge(s_root, n)
                step(V.reciprocal(RSTD[:], RSTD[:]))
                for k in range(KD):
                    step(V.tensor_tensor(HT[:, k, :], XT[:, k, :], RSTD[:], ALU.mult))
                    V.tensor_scalar(HT[:, k, :], HT[:, k, :], gain[:, k:k + 1], MOD[:, shift + k:shift + k + 1],
                                    ALU.mult, ALU.add).then_inc(to, 1)

            def ada(c):
                dve.wait_ge(s_ring[c % 4], 16 * (c // 4 + 1))
                w = RING[:, c % 4, :]
                V.tensor_tensor_reduce(w, w, SILU[:], 1.0, 0.0, ALU.mult, ALU.add, MOD[:, c:c + 1]).then_inc(s_ada, 1)

            dve.wait_ge(s_silu, 1)
            for c in range(8):
                ada(c)
            dve.wait_ge(s_vec, 16)
            dve.wait_ge(s_pos, 16)
            step(V.tensor_copy(ANG[:, 1, :], ANG[:, 0, :].bitcast(I32)))
            step(V.tensor_scalar(ANG[:, 0, :], ANG[:, 1, :], VEC[:, V_INV:V_INV + 1], None, ALU.mult))
            step(V.tensor_scalar(ANG[:, 1, :], ANG[:, 0, :], 1.0 / TWO_PI, ROUND, ALU.mult, ALU.add))
            step(V.tensor_scalar(ANG[:, 1, :], ANG[:, 1, :], ROUND, None, ALU.subtract))
            for c in (C1, C2, C3):
                step(V.scalar_tensor_tensor(out=ANG[:, 0, :], in0=ANG[:, 1, :], scalar=-c, in1=ANG[:, 0, :],
                                            op0=ALU.mult, op1=ALU.add))
            step(V.tensor_scalar(ANG[:, 1, :], ANG[:, 0, :], PI_IN, -PI_IN, ALU.min, ALU.max))
            step(V.scalar_tensor_tensor(out=ANG[:, 2, :], in0=ANG[:, 1, :], scalar=-1.0, in1=ANG[:, 1, :],
                                        op0=ALU.mult, op1=ALU.max))
            V.tensor_scalar(ANG[:, 2, :], ANG[:, 2, :], -1.0, HALF_PI, ALU.mult, ALU.add).then_inc(s_ang, 1)

            for c in range(8, ADA_FIRST):
                ada(c)
            dve.wait_ge(s_ada, ADA_FIRST)
            step(V.tensor_tensor(MOD[:, 0:ADA_FIRST], MOD[:, 0:ADA_FIRST], VEC[:, V_B:V_B + ADA_FIRST], ALU.add))
            step(V.scalar_tensor_tensor(out=GAIN1[:], in0=MOD[:, SC_A:SC_A + KD], scalar=1.0,
                                        in1=VEC[:, V_GMIX:V_GMIX + KD], op0=ALU.add, op1=ALU.mult))
            modulated(GAIN1, SH_A, 1, s_h)
            dve.wait_ge(s_trig, 2)
            V.tensor_scalar(SIN[:], SIN[:], VEC[:, V_SGN:V_SGN + 1], None, ALU.mult).then_inc(s_rope, 1)
            dve.wait_ge(s_rope, 1)
            dve.wait_ge(s_const, 16)
            nc.vector.sem_inc(s_h, KD)

            rotated = [0]

            def rotate(n, i):
                a, b = PS[:, n % 4, 0:T], PS[:, (n + 1) % 4, 0:T]
                dve.wait_ge(s_tile, n + 2)
                dve.wait_ge(s_rope, 1 + rotated[0])
                V.tensor_tensor(RT[:, 0, :], a, COS[:], ALU.mult).then_inc(s_dread, 1)
                V.tensor_tensor(RT[:, 1, :], b, SIN[:], ALU.mult).then_inc(s_dread, 1)
                dve.wait_ge(s_dread, dve_reads(n + 1))
                if i is None:
                    V.tensor_tensor(KR[:], RT[:, 0, :], RT[:, 1, :], ALU.add).then_inc(s_rope, 1)
                else:
                    for h in range(4):
                        r = slice(32 * h, 32 * h + 32)
                        ins = V.tensor_tensor(QR[r, 4 * i + h, :], RT[r, 0, :], RT[r, 1, :], ALU.add)
                    ins.then_inc(s_rope, 1)
                rotated[0] += 1

            def latent(first, count, gain):
                step(V.reciprocal(RSTD[:], RSTD[:]))
                for i in range(count):
                    V.scalar_tensor_tensor(out=CQT[:, first + i, :], in0=CQT[:, first + i, :],
                                           scalar=VEC[:, gain + i:gain + i + 1], in1=RSTD[:],
                                           op0=ALU.mult, op1=ALU.mult).then_inc(s_lat, 1)

            for n, (kind, i) in enumerate(TILES):
                if kind in ("cq", "ckv"):
                    dve.wait_ge(s_tile, n + 1)
                    V.tensor_copy(CQT[:, n, :], PS[:, n % 4, 0:T]).then_inc(s_dread, 1)
                    if (kind, i) == ("ckv", CKV - 1):
                        dve.wait_ge(s_root, 2)
                        dve.wait_ge(s_dread, n + 1)
                        latent(0, CQ, V_GQA)
                        dve.wait_ge(s_root, 3)
                        latent(CQ, CKV, V_GKVA)
                elif kind == "kr" and i == 0:
                    rotate(n, None)
                    for c in range(ADA_FIRST, ADA):
                        ada(c)
                elif kind == "qr" and i % 2 == 0:
                    if i == 0:
                        dve.wait_ge(s_zeroq, 2)
                    rotate(n, i // 2)
            dve.wait_ge(s_ada, ADA)
            V.tensor_tensor(MOD[:, ADA_FIRST:ADA], MOD[:, ADA_FIRST:ADA],
                            VEC[:, V_B + ADA_FIRST:V_B + ADA], ALU.add).then_inc(s_modc, 1)
            dve.wait_ge(s_modc, 1)
            step(V.scalar_tensor_tensor(out=GAIN2[:], in0=MOD[:, SC_F:SC_F + KD], scalar=1.0,
                                        in1=VEC[:, V_GFFN:V_GFFN + KD], op0=ALU.add, op1=ALU.mult))

            N = len(UNITS)
            for at in range(N + 1):
                if at < N:
                    u, b = at, at % 2
                    g, qt = UNITS[u]
                    W = P * (qt + 1)
                    dve.wait_ge(s_s, u + 1)
                    if u >= 2:
                        dve.wait_ge(s_p, u - 1)
                    if g == PAIRS and qt == 0:
                        dve.wait_ge(s_bias, 16)
                        V.tensor_tensor(BT[:], BT[:], MASK.unsqueeze(1).broadcast_to([P, HEADS, T]), ALU.add)\
                         .then_inc(s_mask, 1)
                        dve.wait_ge(s_mask, 1)
                    if g < PAIRS:
                        V.scalar_tensor_tensor(out=S[:, b, :, 0:W],
                                               in0=PS[:, 4 + b, 0:2 * W].rearrange("p (j k) -> p j k", j=2),
                                               scalar=MLA_SCALE,
                                               in1=MASK[:, T - W:T].unsqueeze(1).broadcast_to([P, 2, W]),
                                               op0=ALU.mult, op1=ALU.add).then_inc(s_sm, 1)
                    else:
                        h = 2 * (g - PAIRS)
                        V.scalar_tensor_tensor(out=S[:, b, :, 0:W],
                                               in0=PS[:, 4 + b, 0:2 * W].rearrange("p (j k) -> p j k", j=2),
                                               scalar=MOBA_SCALE, in1=BT[:, h:h + 2, T - W:T],
                                               op0=ALU.mult, op1=ALU.add).then_inc(s_sm, 1)
                    dve.wait_ge(s_sm, u + 1)
                    V.tensor_reduce(NMAX[:, b, :], S[:, b, :, 0:W], AX.X, ALU.max, negate=True).then_inc(s_nm, 1)
                if at >= 1:
                    u, b = at - 1, (at - 1) % 2
                    W = P * (UNITS[u][1] + 1)
                    dve.wait_ge(s_p, u + 1)
                    step(V.reciprocal(REC[:, b, :], SUM[:, b, :]))
                    for j in range(2):
                        ins = V.tensor_scalar(PR[:, b, j, 0:W], PR[:, b, j, 0:W], REC[:, b, j:j + 1], None, ALU.mult)
                    ins.then_inc(s_pn, 1)

            for d in range(KD):
                dve.wait_ge(s_y, d + 1)
                V.scalar_tensor_tensor(out=XT[:, d, :], in0=PS[:, d % 4, 0:T],
                                       scalar=MOD[:, GT_A + d:GT_A + d + 1], in1=XT[:, d, :],
                                       op0=ALU.mult, op1=ALU.add).then_inc(s_x1, 1)
            modulated(GAIN2, SH_F, 4, s_h2)
            for k in range(KD):
                dve.wait_ge(s_h2h, k + 1)
                V.tensor_tensor(H2L[:, k, :], HT[:, k, :], H2H[:, k, :].bitcast(F32), ALU.subtract).then_inc(s_h2l, 1)

            def low(j, at):
                dve.wait_ge(s_uh, at + j + 1)
                V.tensor_tensor(LO[:, j % 2, :], RING[:, j, :], HI[:, j % 2, :].bitcast(F32), ALU.subtract)\
                 .then_inc(s_ul, 1)

            PAIR = range(2)
            HALVES = [(a, p) for a in PAIR for p in range(2)]
            STEPS = 37
            dve.wait_ge(s_sc, TT * PH)
            with dve.Fori(0, TT * PH // 2) as w:
                count = [0]

                def ranked(ins):
                    ins.then_inc(s_tk, 1)
                    count[0] += 1

                def settled(steps):
                    dve.wait_ge(s_tk, w * STEPS + (count[0] - steps))
                    V.sem_inc(s_held, 1)

                low(0, w * 8)
                for a in PAIR:
                    ranked(V.tensor_copy(WK[:, a], SC[:, bass.ds(w * 2 + a, 1)].rearrange("p o a b -> p (o a) b")))
                for n, (a, p) in enumerate(HALVES):
                    if n % 2 == 0:
                        settled(1)
                    ranked(V.max(TV[:, a, p, 0:8], WK[:, a, p, :]))
                low(1, w * 8)
                for n, (a, p) in enumerate(HALVES):
                    if n % 2 == 0:
                        settled(2)
                    ranked(V.max_index(TIU[:, a, p, 0:8], TV[:, a, p, 0:8], WK[:, a, p, :]))
                low(2, w * 8)
                for n, (a, p) in enumerate(HALVES):
                    if n % 2 == 0:
                        settled(2)
                    ranked(V.match_replace(WK[:, a, p, :], TV[:, a, p, 0:8], WK[:, a, p, :], LOWEST))
                low(3, w * 8)
                for n, (a, p) in enumerate(HALVES):
                    if n % 2 == 0:
                        settled(2)
                    ranked(V.max(TV[:, a, p, 8:16], WK[:, a, p, :]))
                low(0, w * 8 + 4)
                for n, (a, p) in enumerate(HALVES):
                    if n % 2 == 0:
                        settled(2)
                    ranked(V.max_index(TIU[:, a, p, 8:16], TV[:, a, p, 8:16], WK[:, a, p, :]))
                for a in PAIR:
                    ranked(V.tensor_tensor(CAND[:, a], TV[:, a, 0, :].unsqueeze(2).broadcast_to([P, TOPK, TOPK]),
                                           TV[:, a, 1, :].unsqueeze(1).broadcast_to([P, TOPK, TOPK]), ALU.add))
                low(1, w * 8 + 4)
                cand = [CAND[:, a].rearrange("p a b -> p (a b)") for a in PAIR]
                for a in PAIR:
                    settled(1)
                    ranked(V.max(BV[:, a, 0:8], cand[a]))
                for a in PAIR:
                    settled(1)
                    ranked(V.max_index(PU[:, a, 0:8], BV[:, a, 0:8], cand[a]))
                low(2, w * 8 + 4)
                for a in PAIR:
                    settled(1)
                    ranked(V.match_replace(cand[a], BV[:, a, 0:8], cand[a], LOWEST))
                for a in PAIR:
                    settled(1)
                    ranked(V.max(BV[:, a, 8:16], cand[a]))
                low(3, w * 8 + 4)
                for a in PAIR:
                    settled(1)
                    ranked(V.max_index(PU[:, a, 8:16], BV[:, a, 8:16], cand[a]))
                two = bass.ds(w * 2, 2)
                ranked(V.tensor_copy(TI[:, two].rearrange("p a b c -> p (a b c)"), TIU[:].rearrange("p a b c -> p (a b c)")))
                settled(1)
                ranked(V.tensor_copy(BEST[:, two].rearrange("p a b -> p (a b)"), BV[:].rearrange("p a b -> p (a b)")))
                ranked(V.tensor_copy(POS[:, two].rearrange("p a b -> p (a b)"), PU[:].rearrange("p a b -> p (a b)")))
                STEPS_DONE = count[0]
            assert STEPS_DONE == STEPS, STEPS_DONE

            low(0, 64)
            dve.wait_ge(s_tk, STEPS * TT * PH // 2)
            step(V.tensor_scalar(AIU[:, 0], POS[:], 4, None, ALU.logical_shift_right))
            step(V.tensor_scalar(AIU[:, 1], POS[:], 15, None, ALU.bitwise_and))
            step(V.tensor_copy(AIF[:], AIU[:]))
            V.tensor_tensor(GTOK[:], BEST[:], BEST[:, :, 0:1].broadcast_to([P, TT * PH, TOPK]), ALU.subtract)\
             .then_inc(s_best, 1)
            b = 1
            iota16 = IOTA[:, 0:TOPK].unsqueeze(1).unsqueeze(1).broadcast_to([P, 4, TOPK, TOPK])
            for p in range(2):
                for q in range(TT * PH // 4):
                    hs = slice(4 * q, 4 * q + 4)
                    step(V.tensor_tensor(EQ[:], AIF[:, p, hs].unsqueeze(3).broadcast_to([P, 4, TOPK, TOPK]), iota16,
                                         ALU.is_equal))
                    low(b % 4, 64 + b // 4 * 4)
                    step(V.tensor_tensor(EQ[:], EQ[:], TI[:, hs, p].unsqueeze(2).broadcast_to([P, 4, TOPK, TOPK]),
                                         ALU.mult))
                    low((b + 1) % 4, 64 + (b + 1) // 4 * 4)
                    step(V.tensor_reduce(ITOK[:, p, hs, :], EQ[:], AX.X, ALU.add))
                    low((b + 2) % 4, 64 + (b + 2) // 4 * 4)
                    b += 3
            while b < 40:
                low(b % 4, 64 + b // 4 * 4)
                b += 1
            dve.wait_ge(s_gexp, 1)
            step(V.tensor_reduce(GSUM[:], GTOK[:], AX.X, ALU.add))
            step(V.reciprocal(GREC[:], GSUM[:]))
            V.tensor_tensor(GTOK[:], GTOK[:], GREC[:].unsqueeze(2).broadcast_to([P, TT * PH, TOPK]), ALU.mult)\
             .then_inc(s_ranks, 1)
            step(V.tensor_copy(J16[:], ITOK[:, 1].rearrange("p (a h) k -> p a (h k)", a=TT)))
            V.tensor_copy(ID16[:], IDENT).then_inc(s_z16, 1)
            V.tensor_copy(ONE16[:], ONES[:]).then_inc(s_z16, 1)
            V.tensor_scalar(NI16[:], IOTA, IDENT[:, 0:1], -1.0, ALU.mult, ALU.mult).then_inc(s_z16, 1)

            for k in range(KD):
                ins = V.tensor_scalar(DIAG[:, k, :], IDENT, MOD[:, GT_F + k:GT_F + k + 1], None, ALU.mult)
            ins.then_inc(s_diag, 1)
            with dve.Fori(26, LAST_U) as i:
                for j in range(4):
                    low(j, i * 4)
            dve.wait_ge(s_rt, 1)
            V.tensor_copy(RANKED[:, 0, :], PS[:, 6, 0:T]).then_inc(s_ranked, 1)
            V.tensor_scalar(RANKED[:, 1, :], PS[:, 6, T:2 * T], -1.0, None, ALU.mult).then_inc(s_ranked, 1)
            V.tensor_copy(RANKED[:, 2, :], PS[:, 6, T:2 * T]).then_inc(s_ranked, 1)
            with dve.Fori(LAST_U, BLOCKS // 4) as i:
                for j in range(4):
                    low(j, i * 4)
            dve.wait_ge(s_umm, BLOCKS)
            V.tensor_copy(GTB[:], PS[:, 4:6, :].rearrange("p a b -> p (a b)")).then_inc(s_gtbc, 1)
            dve.wait_ge(s_ranked, 3)
            dve.wait_ge(s_gelu, BLOCKS)

            def onehot_j(j, g):
                for t in range(ACT_ROWS, GT):
                    V.tensor_scalar(OHI[:, j, t, :], IOTA, RANKED[:, 2, bass.ds(g * GT + t, 1)], None, ALU.is_equal)
                dve.wait_ge(s_z, g + 1)
                V.scalar_tensor_tensor(out=OHJ[:, j], in0=PS[:, 2 * j:2 * j + 2, :].rearrange("p b (t i) -> p (b t) i", i=P),
                                       scalar=0.0, in1=RANKED[:, 0, bass.ds(g * GT, GT)].unsqueeze(2).broadcast_to([P, GT, P]),
                                       op0=ALU.is_equal, op1=ALU.mult).then_inc(s_ohj, 1)

            def gated(j, g):
                a = AG[:, :, bass.ds(g * GT, GT)]
                V.tensor_tensor(a, PS[:, 4 + 2 * j:6 + 2 * j, :].rearrange("p b (t i) -> p i (b t)", i=P), a, ALU.mult)\
                 .then_inc(s_gated, 1)

            onehot_j(0, 0)
            onehot_j(1, 1)
            dve.wait_ge(s_gmm, 1)
            gated(0, 0)
            with dve.Fori(1, GROUPS // 2) as i:
                for j in range(2):
                    dve.wait_ge(s_gmm, i * 2 + j - 1)
                    onehot_j(j, i * 2 + j)
                    dve.wait_ge(s_gmm, i * 2 + j)
                    gated(1 - j, i * 2 + (j - 1))
            dve.wait_ge(s_gmm, GROUPS)
            gated(1, GROUPS - 1)

            def v_low(j, at):
                dve.wait_ge(s_vh, at * 2 + (2 * j + 2))
                V.tensor_tensor(LO[:, j % 2, :], RING[:, j, :], HI[:, j % 2, :].bitcast(F32), ALU.subtract)\
                 .then_inc(s_vl, 1)
                V.tensor_tensor(WL[:, j % 2, :], AG[:, bass.ds(at + j, 1), :].rearrange("p o t -> p (o t)"),
                                WH[:, j % 2, :].bitcast(F32), ALU.subtract).then_inc(s_e1, 1)

            with dve.Fori(0, BLOCKS // 4) as i:
                for j in range(4):
                    v_low(j, i * 4)
            dve.wait_ge(s_vmm, BLOCKS)
            dve.wait_ge(s_x1c, 4)
            dve.wait_ge(s_gtbc, 1)
            for tt in range(TT):
                step(V.tensor_tensor(EPI[:, tt, 0, :], PS[:, 2 * tt:2 * tt + 2, :].rearrange("p a b -> p (a b)"), GTB[:],
                                     ALU.mult))
                V.tensor_tensor(EPI[:, tt, 1, :], EPI[:, tt, 0, :], X1[:, tt, :], ALU.add).then_inc(s_e2, 1)
            dve.wait_ge(s_e4, 1)
            step(V.reciprocal(SSQ[:, 2, :], SSQ[:, 1, :]))
            dve.wait_ge(s_gf, 16)
            for tt in range(TT):
                V.scalar_tensor_tensor(out=EPI[:, tt, 0, :], in0=EPI[:, tt, 1, :], scalar=SSQ[:, 2, tt:tt + 1],
                                       in1=GFB[:], op0=ALU.mult, op1=ALU.mult).then_inc(s_e5, 1)

        @block.tensor
        def _(pe):
            mm = nc.tensor.matmul

            def sum_squares(bank, first, count):
                for k in range(count):
                    ins = mm(PS[:, bank, 0:T], ONES[:], SQ[:, first + k, :], start=(k == 0), stop=(k == count - 1))
                ins.then_inc(s_ssq, 1)

            pe.wait_ge(s_ones, 1)
            pe.wait_ge(s_sq, KD)
            sum_squares(5, 0, KD)

            W_OF = {"cq": 0, "ckv": 6, "kr": 8, "mq": 10, "mk": 14}
            for n, (kind, i) in enumerate(TILES):
                bank = n % 4
                if n >= 4:
                    if TILES[n - 4][0] in DVE_READS:
                        pe.wait_ge(s_dread, dve_reads(n - 4))
                    if TILES[n - 4][0] in ACT_READS:
                        pe.wait_ge(s_aread, act_reads(n - 4))
                if kind in W_OF:
                    c = W_OF[kind] + i
                    pe.wait_ge(s_win[[c < b for b in WIN_SPLIT[1:]].index(True)], 16)
                    for k in range(KD):
                        if n == 0:
                            pe.wait_ge(s_h, k + 1)
                        ins = mm(PS[:, bank, 0:T], W_IN[:, c, k, :], HT[:, k, :], start=(k == 0), stop=(k == KD - 1))
                elif kind == "mv":
                    pe.wait_ge(s_win[4], 16)
                    for k in range(KD):
                        ins = mm(PS[:, bank, :], HT[:, k, i * P:(i + 1) * P], W_MV[:, k, :], start=(k == 0), stop=(k == KD - 1))
                elif kind in ("qn", "qr"):
                    pe.wait_ge(s_wuq, 16)
                    pe.wait_ge(s_lat, CQ)
                    c = i + (PAIRS if kind == "qr" else 0)
                    for k in range(CQ):
                        ins = mm(PS[:, bank, 0:T], W_UQ[:, c, k, :], CQT[:, k, :], start=(k == 0), stop=(k == CQ - 1))
                elif kind == "kn":
                    pe.wait_ge(s_wukv, 32)
                    pe.wait_ge(s_lat, CQ + CKV)
                    for k in range(CKV):
                        ins = mm(PS[:, bank, 0:T], W_UKV[:, i, k, :], CQT[:, CQ + k, :], start=(k == 0), stop=(k == CKV - 1))
                else:
                    for k in range(CKV):
                        ins = mm(PS[:, bank, :], CQT[:, CQ + k, i * P:(i + 1) * P], W_UV[:, k, :], start=(k == 0), stop=(k == CKV - 1))
                ins.then_inc(s_tile, 1)
                if (kind, i) == ("kr", 0):
                    pe.wait_ge(s_sq, KD + CQ + CKV)
                    sum_squares(4, 0, CQ)
                    sum_squares(5, CQ, CKV)

            N = len(UNITS)
            pe.wait_ge(s_aread, act_reads(len(TILES) - 1))
            pe.wait_ge(s_rope, 4)
            for at in range(N + 3):
                if at < N:
                    u, b = at, at % 2
                    g, qt = UNITS[u]
                    W = P * (qt + 1)
                    if u >= 2:
                        pe.wait_ge(s_sm, u - 1)
                    for j in range(2):
                        o, q = PS[:, 4 + b, j * W:(j + 1) * W], slice(qt * P, (qt + 1) * P)
                        h = 2 * (g % PAIRS) + j
                        if g < PAIRS:
                            mm(o, QN[:, h, q], KN[:, g, 0:W], start=True, stop=False)
                            ins = mm(o, QR[:, h, q], KR[:, 0:W], start=False, stop=True)
                        else:
                            ins = mm(o, QM[:, h, q], KM[:, g - PAIRS, 0:W], start=True, stop=True)
                    ins.then_inc(s_s, 1)
                if 2 <= at < N + 2:
                    u, b = at - 2, at % 2
                    nb = UNITS[u][1] + 1
                    pe.wait_ge(s_pn, u + 1)
                    if u >= 2:
                        pe.wait_ge(s_pt, u - 1)
                    for j in range(2):
                        for n in range(nb):
                            a = (j * nb + n) * P
                            ins = nc.tensor.transpose(PS[:, 6 + b, a:a + P], PR[:, b, j, n * P:(n + 1) * P], IDENT)
                    ins.then_inc(s_t, 1)
                if at >= 3:
                    u, b = at - 3, (at - 3) % 2
                    g, qt = UNITS[u]
                    nb = qt + 1
                    pe.wait_ge(s_pt, u + 1)
                    if u >= 2:
                        pe.wait_ge(s_ot, u - 1)
                    v = (VN if g < PAIRS else VM)
                    c = slice((g % PAIRS) * P, (g % PAIRS + 1) * P)
                    for j in range(2):
                        for n in range(nb):
                            ins = mm(PS[:, b, j * P:(j + 1) * P], v[:, n, c], PT[:, b, j, n, :], start=(n == 0), stop=(n == nb - 1))
                    ins.then_inc(s_o, 1)

            pe.wait_ge(s_wout, 16)
            pe.wait_ge(s_ot, N)
            for d in range(KD):
                if d >= 4:
                    pe.wait_ge(s_x1, d - 3)
                for k in range(KD):
                    ins = mm(PS[:, d % 4, 0:T], W_OUT[:, d, k, :], OT[:, k, :], start=(k == 0), stop=(k == KD - 1))
                ins.then_inc(s_y, 1)
            pe.wait_ge(s_sq, KD + CQ + CKV + KD)
            sum_squares(4, 0, KD)
            pe.wait_ge(s_wpq, 16)
            for h in range(PH):
                pe.wait_ge(s_x1, KD)
                if h >= 4:
                    pe.wait_ge(s_qc, h - 3)
                for k in range(KD):
                    if h == 0:
                        pe.wait_ge(s_h2, k + 1)
                    ins = mm(PS[:, h % 4, 0:T], W_PQ[:, h, k, :], HT[:, k, :], start=(k == 0), stop=(k == KD - 1))
                ins.then_inc(s_q, 1)
            pe.wait_ge(s_keys, 16)
            pe.wait_ge(s_root, 4)
            for n in range(TT * PH):
                tt, h = n // PH, n % PH
                pe.wait_ge(s_qc, h + 1 if tt == 0 else PH)
                if n >= 4:
                    pe.wait_ge(s_sc, n - 3)
                mm(PS[:, 4 + n % 4, 0:T], QP[:, h, tt * P:(tt + 1) * P], KEYS[:, h, :], start=True, stop=True).then_inc(s_k, 1)

            pe.wait_ge(s_h2l, KD)

            def u_block(j, at, first=False):
                pe.wait_ge(s_uh, at + j + 1)
                if not first:
                    pe.wait_ge(s_gelu, at + j - 3)
                hi = HI[:, j % 2, :].rearrange("p (k e) -> p k e", k=KD)
                lo = LO[:, j % 2, :].rearrange("p (k e) -> p k e", k=KD)
                o = PS[:, j, 0:T]
                for k in range(KD):
                    mm(o, hi[:, k, :], H2H[:, k, :], start=(k == 0), stop=False)
                    mm(o, hi[:, k, :], H2L[:, k, :], start=False, stop=False)
                pe.wait_ge(s_ul, at + j + 1)
                for k in range(KD):
                    ins = mm(o, lo[:, k, :], H2H[:, k, :], start=False, stop=(k == KD - 1))
                ins.then_inc(s_umm, 1)

            for j in range(4):
                u_block(j, 0, first=True)
            with pe.Fori(1, LAST_U) as i:
                for j in range(4):
                    u_block(j, i * 4)

            pe.wait_ge(s_ranks, 1)
            for a, src in enumerate((GTOK[:], ITOK[:, 0])):
                for tt in range(TT):
                    o = a * T + tt * P
                    ins = nc.tensor.transpose(PS[:, 6, o:o + P],
                                              src[:, tt * PH:(tt + 1) * PH, :].rearrange("p h k -> p (h k)"), IDENT)
            ins.then_inc(s_rt, 1)
            pe.wait_ge(s_diag, 1)
            for k in range(KD):
                ins = mm(PS[:, 4 + k // 4, (k % 4) * P:(k % 4 + 1) * P], ONES[:], DIAG[:, k, :], start=True, stop=True)
            ins.then_inc(s_gtb, 1)
            with pe.Fori(LAST_U, BLOCKS // 4) as i:
                for j in range(4):
                    u_block(j, i * 4)
            pe.wait_ge(s_gelu, BLOCKS)
            for b in range(4):
                for q in range(4):
                    k = (b % 2) * 4 + q
                    ins = nc.tensor.transpose(PS[:, b, q * P:(q + 1) * P], XT[:, k, (b // 2) * P:(b // 2 + 1) * P], IDENT)
                ins.then_inc(s_x1t, 1)

            def differences(j, g, tt):
                for q in range(2):
                    o = PS[:, 2 * j + q, :]
                    at = bass.ds(g * GT + (4 * q - tt * P), 4)
                    mm(o, J16[:, tt, :], ID16[:, at].unsqueeze(2).broadcast_to([P, 4, P]), start=True, stop=False)
                    ins = mm(o, ONE16[:], NI16[:].unsqueeze(1).broadcast_to([P, 4, P]), start=False, stop=True)
                ins.then_inc(s_z, 1)

            def gate_block(j, g):
                pe.wait_ge(s_ohi, g + 1)
                pe.wait_ge(s_ohj, g + 1)
                for t in range(GT):
                    ins = mm(PS[:, 4 + 2 * j + t // 4, (t % 4) * P:(t % 4 + 1) * P], OHJ[:, j, t, :], OHI[:, j, t, :],
                             start=True, stop=True)
                ins.then_inc(s_gmm, 1)

            pe.wait_ge(s_x1c, 4)
            pe.wait_ge(s_z16, 3)
            differences(0, 0, 0)
            differences(1, 1, 0)
            pe.wait_ge(s_gtbc, 1)
            for j in range(2):
                pe.wait_ge(s_ohj, j + 1)
                differences(j, j + 2, 0)
                gate_block(j, j)
            for tt in range(TT):
                first, last = tt * GROUPS // TT, (tt + 1) * GROUPS // TT
                with pe.Fori(max(first // 2 - 1, 1), last // 2 - 1) as i:
                    for j in range(2):
                        pe.wait_ge(s_ohj, i * 2 + j + 1)
                        differences(j, i * 2 + j + 2, tt)
                        pe.wait_ge(s_gated, i * 2 + j - 1)
                        gate_block(j, i * 2 + j)
            for g in range(GROUPS - 2, GROUPS):
                pe.wait_ge(s_gated, g - 1)
                gate_block(g % 2, g)

            def v_block(j, at, first=False, last=False):
                pe.wait_ge(s_vh, at * 2 + (2 * j + 2))
                for tt in range(TT):
                    for h in range(2):
                        mm(PS[:, 2 * tt + h, :], WH[:, j % 2, tt * P:(tt + 1) * P], HI[:, j % 2, h * 512:(h + 1) * 512],
                           start=first, stop=False)
                pe.wait_ge(s_vl, at + j + 1)
                for tt in range(TT):
                    for h in range(2):
                        mm(PS[:, 2 * tt + h, :], WH[:, j % 2, tt * P:(tt + 1) * P], LO[:, j % 2, h * 512:(h + 1) * 512],
                           start=False, stop=False)
                pe.wait_ge(s_e1, at + j + 1)
                for tt in range(TT):
                    for h in range(2):
                        ins = mm(PS[:, 2 * tt + h, :], WL[:, j % 2, tt * P:(tt + 1) * P], HI[:, j % 2, h * 512:(h + 1) * 512],
                                 start=False, stop=last)
                ins.then_inc(s_vmm, 1)

            pe.wait_ge(s_x1c, 4)
            for j in range(4):
                v_block(j, 0, first=(j == 0))
            with pe.Fori(1, BLOCKS // 4 - 1) as i:
                for j in range(4):
                    v_block(j, i * 4)
            for j in range(4):
                v_block(j, BLOCKS - 4, last=(j == 3))


def t5_bucket(n):
    nf = np.maximum(n, 16).astype(np.float32)
    large = 16 + (np.log(nf / np.float32(16)) / np.float32(np.log(64.0)) * np.float32(16)).astype(np.int32)
    return np.where(n < 16, n, np.minimum(large, 31))


def kernel(x, c, positions, w_ada, b_ada, g_mix, w_in, g_qa, w_uq, g_kva, w_ukv, rel_bias, w_out, g_ffn, w_pq,
           peer_keys, peer_u, peer_v, g_final):
    import concourse.bacc as bacc
    from concourse.bass_utils import run_bass_kernel_spmd

    f = np.ascontiguousarray
    A = np.asarray

    def cols(v):
        return A(v).reshape(-1, P).T

    def stationary(w):
        k, n = w.shape
        return w.reshape(k // P, P, n // P, P).transpose(1, 2, 0, 3)

    consts = np.zeros((P, 512), np.float32)
    consts[:, 0:128] = np.eye(P)
    consts[:, 128:256] = np.arange(P)
    consts[:, 256:512] = np.where(np.arange(T)[None, :] > P + np.arange(P)[:, None], MASKED, 0.0)

    half = ROPE // 2
    row = np.arange(P) % ROPE
    inv = np.float32(THETA) ** (-np.arange(half, dtype=np.float32) / np.float32(half))
    vecs = np.zeros((P, NVEC), np.float32)
    for at, v in ((V_B, A(b_ada)[0]), (V_GMIX, A(g_mix)[0]), (V_GQA, A(g_qa)[0]),
                  (V_GKVA, A(g_kva)[0]), (V_GFFN, A(g_ffn)[0])):
        v = cols(v)
        vecs[:, at:at + v.shape[1]] = v
    vecs[:, V_INV] = inv[row % half]
    vecs[:, V_SGN] = np.where(row < half, -1.0, 1.0)
    vecs[:, V_EPS] = EPS

    swap = (np.arange(ROPE) + half) % ROPE
    wi = A(w_in)[0]
    kr0 = Q_LORA + KV_LORA
    m0 = kr0 + ROPE
    order = np.concatenate([np.arange(kr0), np.tile(kr0 + np.arange(ROPE), 4), np.tile(kr0 + swap, 4),
                            m0 + np.arange(1024)])
    w_in_k = np.concatenate([stationary(wi[:, order]).reshape(P, -1),
                             wi[:, m0 + 1024:].reshape(KD, P, 512).transpose(1, 0, 2).reshape(P, -1)], axis=1)
    qk = NOPE + ROPE
    heads = np.arange(HEADS)[:, None] * qk
    r = (heads + NOPE + np.arange(ROPE)).reshape(2, -1)
    rs = (heads + NOPE + swap).reshape(2, -1)
    order = np.concatenate([(heads + np.arange(NOPE)).ravel(), r[0], rs[0], r[1], rs[1]])
    w_uq_k = stationary(A(w_uq)[0][:, order])
    heads = np.arange(HEADS)[:, None] * 128
    kn = A(w_ukv)[0][:, (heads + np.arange(64)).ravel()]
    vv = A(w_ukv)[0][:, (heads + 64 + np.arange(64)).ravel()]
    w_ukv_k = np.concatenate([stationary(kn).reshape(P, -1),
                              vv.reshape(CKV, P, 512).transpose(1, 0, 2).reshape(P, -1)], axis=1)
    distance = np.maximum(P + np.arange(P)[:, None] - np.arange(T)[None, :], 0)
    rel = f(A(rel_bias)[t5_bucket(distance)].transpose(0, 2, 1))
    pk = A(peer_keys)[0]
    keys = np.zeros((P, PH, 2 * NKEYS), np.float32)
    for p in range(2):
        keys[p * 64:(p + 1) * 64, :, p * NKEYS:(p + 1) * NKEYS] = pk[:, p].transpose(2, 0, 1)

    arrays = {
        "consts": consts, "vecs": vecs, "c_row": f(A(c)[0]), "positions": f(A(positions)[0].astype(np.int32)),
        "xT": f(A(x)[0].reshape(T, KD, P).transpose(2, 1, 0)),
        "w_ada": f(A(w_ada)[0].T.reshape(ADA, P, D)),
        "w_in": f(w_in_k), "w_uq": f(w_uq_k), "w_ukv": f(w_ukv_k), "rel": rel,
        "w_out": f(stationary(A(w_out)[0])), "w_pq": f(stationary(A(w_pq)[0])), "keys": keys,
        "u_tab": f(A(peer_u)[0].reshape(BLOCKS, P, KD, P).transpose(0, 3, 2, 1).reshape(BLOCKS, P, D)),
        "v_tab": f(A(peer_v)[0].reshape(BLOCKS, P, D)),
        "g_final": f(A(g_final)),
    }
    nc = bacc.Bacc("TRN2", target_bir_lowering=False, num_devices=1)
    aps = [nc.dram_tensor(n, a.shape, mybir.dt.from_np(a.dtype), kind="ExternalInput").ap() for n, a in arrays.items()]
    out = nc.dram_tensor("out", (T, D), F32, kind="ExternalOutput").ap()
    build(nc, *aps, out)
    r = run_bass_kernel_spmd(nc, [arrays], core_ids=[0])
    return r.results[0]["out"].reshape(1, T, D)
```

```python
from contextlib import ExitStack

import numpy as np

import concourse.bass as bass
from concourse import mybir

F32 = mybir.dt.float32
F32R = mybir.dt.float32r
BF16 = mybir.dt.bfloat16
I32 = mybir.dt.int32
U32 = mybir.dt.uint32
ALU = mybir.AluOpType
ACT = mybir.ActivationFunctionType
AX = mybir.AxisListType

P = 128
T = 256
TT = T // P
D = 1024
KD = D // P
EPS = 1e-6
Q_LORA, KV_LORA = 768, 256
CQ, CKV = Q_LORA // P, KV_LORA // P
HEADS = 8
NOPE, ROPE, HDIM = 64, 32, 64
MLA_SCALE = float((NOPE + ROPE) ** -0.5)
MOBA_SCALE = float(HDIM ** -0.5)
PAIRS = HEADS // 2
NKEYS = 128
PH = 8
TOPK = 16
GT = 8
GROUPS = T // GT
LAST_U = 28
BLOCKS = NKEYS
LOWEST = -3.0e38
MASKED = -1.0e30
THETA = 10000.0

SH_A, SC_A, GT_A, SH_F, SC_F, GT_F = (KD * i for i in range(6))
ADA = 6 * KD
ADA_FIRST = 2 * KD
ADA_BESIDE = 2 * KD
ADA_LATE = KD
ADA_EARLY = ADA - ADA_LATE
ADA_RING = ADA - ADA_BESIDE - ADA_LATE

V_B, V_GMIX, V_GQA, V_GKVA, V_GFFN = 0, 48, 56, 62, 64
V_INV, V_SGN, V_EPS = 72, 73, 74
NVEC = 76

TWO_PI = 2.0 * np.pi
C1 = 6.28125
C2 = float((np.float32(TWO_PI - C1).view(np.int32) & np.int32(~0xFFF)).view(np.float32))
C3 = float(np.float32(TWO_PI - C1 - C2))
ROUND = 12582912.0
PI_IN = 3.1415925
HALF_PI = float(np.float32(np.pi / 2))

TILES = ([("cq", i) for i in range(CQ)] + [("ckv", i) for i in range(CKV)] + [("kr", 0), ("kr", 1)]
         + [("mq", i) for i in range(PAIRS)] + [("mk", i) for i in range(PAIRS)]
         + [("mv", i) for i in range(TT)]
         + [("qn", i) for i in range(PAIRS)] + [("qr", i) for i in range(4)]
         + [("kn", i) for i in range(PAIRS)] + [("v", i) for i in range(TT)])
Z_TILES = TILES.index(("qn", 0))
Z_CHUNKS, UQ_CHUNKS = 22, 8
CHUNKS = Z_CHUNKS + UQ_CHUNKS + 2


POOL_LOWS = [c for c in range(CHUNKS) if c % 2 == 1]


def last_chunk(n):
    kind, i = TILES[n]
    if kind == "mv":
        return Z_CHUNKS - 1
    if kind in ("qn", "qr"):
        return Z_CHUNKS + i + (PAIRS if kind == "qr" else 0)
    if kind in ("kn", "v"):
        return CHUNKS - 2 + (kind == "v")
    return n
DVE_READS = ("cq", "ckv", "kr", "qr")
ACT_READS = ("mq", "mk", "mv", "qn", "kn", "v")


def tile_no(kind, i=0):
    return TILES.index((kind, i))


def dve_reads(n):
    return sum(kind in DVE_READS for kind, _ in TILES[:n + 1])


def act_reads(n):
    return sum(kind in ACT_READS for kind, _ in TILES[:n + 1])


def build(nc, consts, vecs, c_row, positions, xT, w_ada, w_in, w_uq, w_ukv, rel, w_out, w_pq, keys, u_tab, v_tab,
          g_final, out):
    base = (nc.sbuf_base + 63) // 64 * 64

    def place(name, at, shape, dt=F32):
        return nc.alloc_sbuf_tensor_at(name, shape, dt, offset=base + 4 * at)

    AG = place("AG", 0, [P, BLOCKS, T])
    W_IN = place("W_IN", 0, [P, 22, KD, P])
    W_UQ = place("W_UQ", 22528, [P, 8, CQ, P])
    W_UKV = place("W_UKV", 28672, [P, 2, D])
    W_INL = place("W_INL", 0, [P, Z_CHUNKS, D], F32R)
    W_UQL = place("W_UQL", 22528, [P, UQ_CHUNKS, CQ * P], F32R)
    W_UKVL = place("W_UKVL", 28672, [P, 2, D], F32R)
    WUH = place("WUH", 4608, [P, 2, CQ * P], F32R)
    SILU = place("SILU", 30720, [P, D])
    BT = place("BT", 22528, [P, HEADS, T])
    QN = place("QN", 0, [P, HEADS, T])
    QR = place("QR", 2048, [P, HEADS, T])
    OT = place("OT", 4096, [P, KD, T])
    OTL = place("OTL", 4096, [P, KD, T], F32R)
    RT = place("RT", 4096, [P, 2, T])
    W_OP = place("W_OP", 6144, [P, KD + PH, D])
    W_OPL = place("W_OPL", 6144, [P, KD + PH, D], F32R)
    W_OPH = place("W_OPH", 28672, [P, 2, D], F32R)
    W_GT = place("W_GT", 28672, [P, 4, D])
    KEYS = place("KEYS", 24576, [P, PH, 2 * NKEYS])
    SC = place("SC", 28672, [P, TT * PH, 2, NKEYS])
    TI = place("TI", 24576, [P, TT * PH, 2, TOPK])
    BEST = place("BEST", 25088, [P, TT * PH, TOPK])
    POS = place("POS", 25344, [P, TT * PH, TOPK], U32)
    WK = place("WK", 25600, [P, 2, 2, NKEYS])
    CAND = place("CAND", 26112, [P, 2, TOPK, TOPK])
    TV = place("TV", 26624, [P, 2, 2, TOPK])
    TIU = place("TIU", 26688, [P, 2, 2, TOPK], U32)
    BV = place("BV", 26752, [P, 2, TOPK])
    PU = place("PU", 26784, [P, 2, TOPK], U32)
    AIU = place("AIU", 25600, [P, 2, TT * PH, TOPK], U32)
    AIF = place("AIF", 26112, [P, 2, TT * PH, TOPK])
    EQ = place("EQ", 26880, [P, 4, TOPK, TOPK])
    GSUM = place("GSUM", 27904, [P, TT * PH])
    GREC = place("GREC", 27920, [P, TT * PH])

    XT = place("XT", 32768, [P, KD, T])
    HT = place("HT", 34816, [P, KD, T])
    HTL = place("HTL", 34816, [P, KD, T], F32R)
    OTH = place("OTH", 34816, [P, KD, T], F32R)
    OHI = place("OHI", 34816, [P, 2, GT, P])
    DIAG = place("DIAG", 34816, [P, KD, P])
    WH = place("WH", 34816, [P, 2, T], F32R)
    WL = place("WL", 35328, [P, 2, T], F32R)
    QM = place("QM", 36864, [P, HEADS, T])
    H2H = place("H2H", 36864, [P, KD, T], F32R)
    X1 = place("X1", 36864, [P, TT, D])
    ANG = place("ANG", 38912, [P, 3, T])
    KM = place("KM", 38912, [P, PAIRS, T])
    KN = place("KN", 39936, [P, PAIRS, T])
    H2L = place("H2L", 38912, [P, KD, T], F32R)
    GTB = place("GTB", 38912, [P, D])
    GFB = place("GFB", 39936, [P, D])
    VM = place("VM", 40960, [P, TT, 512])
    VN = place("VN", 41984, [P, TT, 512])
    QP = place("QP", 40960, [P, PH, T])
    GTOK = place("GTOK", 40960, [P, TT * PH, TOPK])
    ITOK = place("ITOK", 41216, [P, 2, TT * PH, TOPK])
    RANKED = place("RANKED", 41728, [P, 2, T])
    J16 = place("J16", 42496, [P, TT, P], BF16)
    ID16 = place("ID16", 42624, [P, P], BF16)
    ONE16 = place("ONE16", 42688, [P, P], BF16)
    NI16 = place("NI16", 42752, [P, P], BF16)
    BESIDE = (place("BESIDE0", 39936, [P, D]), place("BESIDE1", 41984, [P, D]), place("BESIDE2", 31744, [P, D]))
    RING = place("RING", 43008, [P, 4, D])
    HTH = place("HTH", 43008, [P, KD, T], F32R)
    WZH = place("WZH", 45056, [P, 2, D], F32R)
    WVH = place("WVH", 34816, [P, 2, D], F32R)
    CQH = place("CQH", 49152, [P, CQ + CKV, T], F32R)
    CQL = place("CQL", 47104, [P, CQ + CKV, T], F32R)
    CQT = place("CQT", 47104, [P, CQ + CKV, T])
    S = place("S", 47104, [P, 2, 2, T])
    PR = place("PR", 48128, [P, 2, 2, T])
    HI = place("HI", 47104, [P, 2, D], F32R)
    OHJ = place("OHJ", 47104, [P, 2, GT, P])
    AWAY = place("AWAY", 49152, [P, 2, GT, P])
    SQ = place("SQ", 49152, [P, KD, T])
    PT = place("PT", 49152, [P, 2, 2, 2, P])
    LO = place("LO", 49152, [P, 2, D], F32R)
    XG = place("XG", 43008, [P, D])
    EPI = place("EPI", 0, [P, TT, 2, D])
    KR = place("KR", 51200, [P, T])
    COS = place("COS", 51456, [P, T])
    SIN = place("SIN", 51712, [P, T])
    SILU2 = place("SILU2", 51200, [P, D])
    RSTD = place("RSTD", 51968, [P, T])
    CONST = place("CONST", 52224, [P, 512])
    IDENT, IOTA, MASK = CONST[:, 0:128], CONST[:, 128:256], CONST[:, 256:512]
    ONES = place("ONES", 52736, [P, P])
    VEC = place("VEC", 52864, [P, NVEC])
    MOD = place("MOD", 52952, [P, ADA])
    GAIN1 = place("GAIN1", 53000, [P, KD])
    GAIN2 = place("GAIN2", 53008, [P, KD])
    NMAX = place("NMAX", 53040, [P, 2, 2])
    SUM = place("SUM", 53048, [P, 2, 2])
    REC = place("REC", 53056, [P, 2, 2])
    SSQ = place("SSQ", 53064, [P, 3, TT])
    WARM = place("WARM", 53072, [P, 8])

    with ExitStack() as ctx:
        PS = ctx.enter_context(nc.psum_tensor("PS", [P, 8, 512], F32))

        def sem(name):
            return ctx.enter_context(nc.semaphore(name))

        s_const, s_vec, s_pos, s_x, s_bias = (sem(n) for n in ("s_const", "s_vec", "s_pos", "s_x", "s_bias"))
        s_win = [sem(f"s_win{i}") for i in range(12)]
        s_wuq, s_wout, s_wpq = ([sem(f"{n}{i}") for i in range(2)] for n in ("s_wuq", "s_wout", "s_wpq"))
        s_wukv, s_keys = sem("s_wukv"), sem("s_keys")
        s_ring = [sem(f"s_ring{j}") for j in range(4)]
        s_beside = [sem(f"s_beside{j}") for j in range(3)]
        s_wgt = [sem(f"s_wgt{i}") for i in range(4)]
        s_gf, s_out = sem("s_gf"), sem("s_out")
        s_ones, s_zero, s_zeroq = sem("s_ones"), sem("s_zero"), sem("s_zeroq")
        s_c, s_silu = sem("s_c"), sem("s_silu")
        s_sq, s_ssq, s_root = sem("s_sq"), sem("s_ssq"), sem("s_root")
        s_ada, s_xn, s_gain, s_h = sem("s_ada"), sem("s_xn"), sem("s_gain"), sem("s_h")
        s_ang, s_trig = sem("s_ang"), sem("s_trig")
        s_zlp = sem("s_zlp")
        s_zh, s_zl, s_mv, s_hh, s_hl = (sem(n) for n in ("s_zh", "s_zl", "s_mv", "s_hh", "s_hl"))
        s_tile, s_dread, s_aread = sem("s_tile"), sem("s_dread"), sem("s_aread")
        s_lat, s_lath, s_latl, s_rope, s_mask = (sem(n) for n in ("s_lat", "s_lath", "s_latl", "s_rope", "s_mask"))
        s_s, s_sm, s_nm, s_p, s_pn, s_t, s_pt, s_o, s_ot = (
            sem(n) for n in ("s_s", "s_sm", "s_nm", "s_p", "s_pn", "s_t", "s_pt", "s_o", "s_ot"))
        s_oth, s_otl, s_wh, s_wl, s_wlp = (sem(n) for n in ("s_oth", "s_otl", "s_wh", "s_wl", "s_wlp"))
        s_y, s_x1, s_h2, s_h2h, s_h2l = (sem(n) for n in ("s_y", "s_x1", "s_h2", "s_h2h", "s_h2l"))
        s_q, s_qc, s_k, s_sc = (sem(n) for n in ("s_q", "s_qc", "s_k", "s_sc"))
        s_uh, s_ul, s_umm, s_gelu = (sem(n) for n in ("s_uh", "s_ul", "s_umm", "s_gelu"))
        s_tk, s_held, s_best, s_gexp, s_ranks, s_rt, s_ranked = (
            sem(n) for n in ("s_tk", "s_held", "s_best", "s_gexp", "s_ranks", "s_rt", "s_ranked"))
        s_diag, s_gtb, s_x1t, s_x1c, s_gtbc = (sem(n) for n in ("s_diag", "s_gtb", "s_x1t", "s_x1c", "s_gtbc"))
        s_dist = sem("s_dist")
        s_z16, s_z, s_away, s_ohi, s_ohj, s_gmm, s_gated = (
            sem(n) for n in ("s_z16", "s_z", "s_away", "s_ohi", "s_ohj", "s_gmm", "s_gated"))
        s_vh, s_vl, s_vmm = sem("s_vh"), sem("s_vl"), sem("s_vmm")
        s_al = sem("s_al")
        s_sumd, s_ssq2, s_root2, s_rstd2, s_outv, s_outa = (
            sem(n) for n in ("s_sumd", "s_ssq2", "s_root2", "s_rstd2", "s_outv", "s_outa"))
        s_tile0, s_xg = sem("s_tile0"), sem("s_xg")
        s_d = sem("s_d")

        block = ctx.enter_context(nc.Block())

        S_BANK = (4, 5, 2, 3)
        STEPS = 37
        UNITS = [(g, qt) for g in range(2 * PAIRS) for qt in range(TT)]
        WIN_SPLIT = [0, 1, 2, 4, 6, 8, 10, 12, 14, 16, 18, 20, 22]

        def win_part(c):
            return [c < b for b in WIN_SPLIT[1:]].index(True)

        @block.sync
        def _(sp):
            sp.dma_start(SILU[:], c_row.partition_broadcast(P)).then_inc(s_c, 16)

            def load_ada(c):
                if c >= 4 and c != ADA_FIRST + ADA_BESIDE + c % 4:
                    sp.wait_ge(s_ada, c - 3)
                sp.dma_start(RING[:, c % 4, :], w_ada[c]).then_inc(s_ring[c % 4], 16)

            def load_in(c):
                sp.dma_start(W_IN[:, c].rearrange("p k n -> p (k n)"), w_in[:, c * D:(c + 1) * D])\
                  .then_inc(s_win[win_part(c)], 16)

            for c in range(4):
                load_ada(c)
            sp.dma_start(XT[:], xT).then_inc(s_x, 16)
            sp.dma_start(VEC[:], vecs).then_inc(s_vec, 16)
            for c in range(4, ADA_FIRST):
                load_ada(c)
            sp.dma_start(CONST[:], consts).then_inc(s_const, 16)
            sp.dma_start(ANG[:, 0, :].bitcast(I32), positions.partition_broadcast(P)).then_inc(s_pos, 16)
            def load_beside(c):
                if c >= ADA_FIRST + 3:
                    sp.wait_ge(s_ada, c - 2)
                sp.dma_start(BESIDE[c % 3][:], w_ada[c]).then_inc(s_beside[c % 3], 16)

            for c in range(8):
                load_in(c)
            for c in range(3):
                load_beside(ADA_FIRST + c)
            for c in range(8, 12):
                load_in(c)
            for c in range(12, Z_CHUNKS):
                load_beside(ADA_FIRST + c - 9)
                load_in(c)
                if c in (13, 16):
                    a = (c - 13) // 3
                    sp.dma_start(W_UQ[:, 4 * a:4 * a + 4], w_uq[:, 4 * a:4 * a + 4]).then_inc(s_wuq[a], 16)
                if c == 18:
                    sp.dma_start(W_UKV[:].rearrange("p c n -> p (c n)"), w_ukv).then_inc(s_wukv, 16)
            for a in range(3):
                load_beside(ADA_FIRST + Z_CHUNKS - 9 + a)
            sp.wait_ge(s_tile, Z_TILES)
            for c in range(ADA_FIRST + ADA_BESIDE, ADA_EARLY):
                load_ada(c)

            for j in range(4):
                sp.wait_ge(s_ada, ADA_EARLY - 3 + j)
                sp.dma_start(RING[:, j, :], u_tab[j]).then_inc(s_ring[j], 16)
            def load_u(i):
                for j in range(4):
                    sp.wait_ge(s_ul, i * 4 + j - 3)
                    sp.dma_start(RING[:, j, :], u_tab[bass.ds(i * 4 + j, 1)].rearrange("o p d -> (o p) d"))\
                      .then_inc(s_ring[j], 16)

            with sp.Fori(1, 18) as i:
                load_u(i)
            sp.wait_ge(s_tk, STEPS * TT * PH // 2)
            for c in range(ADA_LATE):
                if c >= 4:
                    sp.wait_ge(s_ada, ADA_EARLY + c - 3)
                sp.dma_start(W_GT[:, c % 4, :], w_ada[ADA_EARLY + c]).then_inc(s_wgt[c % 4], 16)
                load_u(18 + c)
            with sp.Fori(18 + ADA_LATE, BLOCKS // 4) as i:
                load_u(i)
            for j in range(4):
                sp.wait_ge(s_ul, BLOCKS - 3 + j)
                sp.dma_start(RING[:, j, :], v_tab[j]).then_inc(s_ring[j], 16)
            sp.wait_ge(s_umm, BLOCKS)
            sp.dma_start(GFB[:], g_final.partition_broadcast(P)).then_inc(s_gf, 16)
            with sp.Fori(1, BLOCKS // 4) as i:
                for j in range(4):
                    sp.wait_ge(s_vl, i * 4 + j - 3)
                    sp.dma_start(RING[:, j, :], v_tab[bass.ds(i * 4 + j, 1)].rearrange("o p d -> (o p) d"))\
                      .then_inc(s_ring[j], 16)
            sp.wait_ge(s_outv, 1)
            sp.wait_ge(s_outa, 1)
            sp.dma_start(out[P:2 * P, :], EPI[:, 1, 0, :]).then_inc(s_out, 16)
            sp.wait_ge(s_outv, 2)
            sp.dma_start(out[0:P, :], EPI[:, 0, 0, :]).then_inc(s_out, 16)
            sp.wait_ge(s_out, 16 * TT)

        def z_parts(c):
            if c < Z_CHUNKS:
                return W_IN[:, c].rearrange("p k n -> p (k n)"), WZH[:, c % 2, :], W_INL[:, c, :]
            c -= Z_CHUNKS
            if c < UQ_CHUNKS:
                return W_UQ[:, c].rearrange("p k n -> p (k n)"), WUH[:, c % 2, :], W_UQL[:, c, :]
            return W_UKV[:, c - UQ_CHUNKS, :], WVH[:, c % 2, :], W_UKVL[:, c - UQ_CHUNKS, :]

        @block.gpsimd
        def _(pool):
            nc.gpsimd.memset(ONES[:], 1.0).then_inc(s_ones, 1)
            nc.gpsimd.memset(QM[:], 0.0).then_inc(s_zero, 1)
            for c in POOL_LOWS:
                pool.wait_ge(s_zh, c + 1)
                a, h, to = z_parts(c)
                nc.gpsimd.tensor_tensor(to, a, h.bitcast(F32), ALU.subtract).then_inc(s_zlp, 1)
                if c in (17, 19):
                    for k in range(2) if c == 17 else range(2, CQ + CKV):
                        pool.wait_ge(s_lath, k + 1)
                        nc.gpsimd.tensor_tensor(CQL[:, k, :], CQT[:, k, :], CQH[:, k, :].bitcast(F32), ALU.subtract)\
                          .then_inc(s_latl, 1)
                if c == POOL_LOWS[1]:
                    pool.wait_ge(s_tile, 4)
                    nc.gpsimd.memset(QN[:], 0.0).then_inc(s_zeroq, 1)
                    nc.gpsimd.memset(QR[:], 0.0).then_inc(s_zeroq, 1)
            for g in range(2 * PAIRS):
                pool.wait_ge(s_oth, g + 1)
                nc.gpsimd.tensor_tensor(OTL[:, g, :], OT[:, g, :], OTH[:, g, :].bitcast(F32), ALU.subtract)\
                  .then_inc(s_otl, 1)
                if g == 2 * PAIRS - 2:
                    pool.wait_ge(s_wh, 1)
                    nc.gpsimd.tensor_tensor(W_OPL[:, 0, :], W_OP[:, 0, :], W_OPH[:, 0, :].bitcast(F32), ALU.subtract)\
                      .then_inc(s_wlp, 1)

            def distances(j, g):
                number = RANKED[:, 1, bass.ds(g * GT, GT)].unsqueeze(2).broadcast_to([P, GT, P])
                nc.gpsimd.tensor_tensor(AWAY[:, j], IOTA.unsqueeze(1).broadcast_to([P, GT, P]), number, ALU.add)\
                  .then_inc(s_dist, 1)

            pool.wait_ge(s_ranked, 2)
            pool.wait_ge(s_umm, BLOCKS)
            for g in range(2):
                distances(g, g)
            with pool.Fori(1, GROUPS // 2) as i:
                for j in range(2):
                    pool.wait_ge(s_ohi, i * 2 + j - 1)
                    distances(j, i * 2 + j)

        @block.scalar
        def _(act):
            act.wait_ge(s_c, 16)
            nc.scalar.activation(SILU[:], SILU[:], ACT.Silu).then_inc(s_silu, 1)
            act.wait_ge(s_x, 16)
            for k in range(KD):
                nc.scalar.activation(SQ[:, k, :], XT[:, k, :], ACT.Square).then_inc(s_sq, 1)

            def root(n, width, bank, to):
                act.wait_ge(s_ssq, n + 1)
                nc.scalar.activation(to[:], PS[:, bank, 0:T], ACT.Sqrt, bias=VEC[:, V_EPS:V_EPS + 1],
                                     scale=1.0 / width).then_inc(s_root, 1)

            act.wait_ge(s_vec, 16)
            root(0, D, 5, RSTD)
            def z_high(c):
                if c < 2:
                    act.wait_ge(s_ada, ADA_FIRST)
                if c < Z_CHUNKS:
                    part = win_part(c)
                    act.wait_ge(s_win[part], 16 * (WIN_SPLIT[part + 1] - WIN_SPLIT[part]))
                elif c < CHUNKS - 2:
                    act.wait_ge(s_wuq[(c - Z_CHUNKS) // 4], 16)
                else:
                    act.wait_ge(s_wukv, 16)
                src, to, _ = z_parts(c)
                if Z_CHUNKS - 4 <= c - 2 < Z_CHUNKS - 1:
                    act.wait_ge(s_mv, c - 2 - (Z_CHUNKS - 4) + 1)
                elif c >= 2:
                    act.wait_ge(s_tile, [last_chunk(n) for n in range(len(TILES))].index(c - 2) + 1
                                if c - 2 != Z_CHUNKS - 1 else Z_TILES)
                nc.scalar.copy(to, src).then_inc(s_zh, 1)

            def latent_high(k):
                act.wait_ge(s_lat, k + 1)
                nc.scalar.copy(CQH[:, k, :], CQT[:, k, :]).then_inc(s_lath, 1)

            def load_out(c):
                src, ready = (w_out, s_wout) if c < KD else (w_pq, s_wpq)
                act.dma_start(W_OP[:, c, :], src[:, c % KD].rearrange("p k n -> p (k n)")).then_inc(ready[c % KD // 4], 16)

            z_high(0)
            act.wait_ge(s_gain, 1)
            act.wait_ge(s_xn, KD)
            for k in range(KD):
                nc.scalar.activation(HTH[:, k, :], HT[:, k, :], ACT.Identity, scale=GAIN1[:, k:k + 1],
                                     bias=MOD[:, SH_A + k:SH_A + k + 1]).then_inc(s_hh, 1)
            z_high(1)
            for n, (kind, i) in enumerate(TILES):
                bank = n % 4
                for c in range(last_chunk(n - 1) + 3 if n else 2, min(last_chunk(n) + 3, CHUNKS)):
                    z_high(c)
                if kind in ACT_READS:
                    act.wait_ge(s_tile, n + 1)
                if kind in ("cq", "ckv"):
                    act.wait_ge(s_dread, n + 1)
                    nc.scalar.activation(SQ[:, n, :], CQT[:, n, :], ACT.Square).then_inc(s_sq, 1)
                elif kind in ("mq", "qn"):
                    to = QM if kind == "mq" else QN
                    act.wait_ge(s_zero if kind == "mq" else s_zeroq, 1)
                    nc.scalar.copy(to[0:64, 2 * i, :], PS[0:64, bank, 0:T])
                    nc.scalar.copy(to[64:128, 2 * i + 1, :], PS[64:128, bank, 0:T]).then_inc(s_aread, 1)
                elif kind in ("mk", "kn"):
                    nc.scalar.copy((KM if kind == "mk" else KN)[:, i, :], PS[:, bank, 0:T]).then_inc(s_aread, 1)
                elif kind in ACT_READS:
                    nc.scalar.copy((VM if kind == "mv" else VN)[:, i, :], PS[:, bank, :]).then_inc(s_aread, 1)
                if n == tile_no("kn") - 1:
                    act.wait_ge(s_ada, ADA_FIRST + ADA_BESIDE)
                if n == 6:
                    act.wait_ge(s_ang, 1)
                    nc.scalar.activation(SIN[:], ANG[:, 1, :], ACT.Sin).then_inc(s_trig, 1)
                    nc.scalar.activation(COS[:], ANG[:, 2, :], ACT.Sin).then_inc(s_trig, 1)
                if n == 9:
                    act.wait_ge(s_xn, KD)
                    root(1, Q_LORA, 4, RSTD)
                if n == 13:
                    act.wait_ge(s_lat, CQ)
                    root(2, KV_LORA, 5, RSTD)
                if n == len(TILES) - 1:
                    act.dma_start(BT[:], rel).then_inc(s_bias, 16)
                if n == 14:
                    for k in range(CQ):
                        latent_high(k)
                if n == 16:
                    for k in range(CQ, CQ + CKV):
                        latent_high(k)

            def high(c):
                act.wait_ge((s_wout if c < KD else s_wpq)[c % KD // 4], 64)
                if 2 <= c < KD + 2:
                    act.wait_ge(s_y, c - 1)
                elif c >= KD + 2:
                    act.wait_ge(s_q, c - KD - 1)
                nc.scalar.copy(W_OPH[:, c % 2, :], W_OP[:, c, :]).then_inc(s_wh, 1)

            N = len(UNITS)
            for step in range(N + 3):
                if step < N:
                    load_out(step)
                if step == N - 1:
                    act.dma_start(KEYS[:], keys).then_inc(s_keys, 16)
                if step < N:
                    u, b = step, step % 2
                    W = P * (UNITS[u][1] + 1)
                    act.wait_ge(s_nm, u + 1)
                    if u >= 2:
                        act.wait_ge(s_t, u - 1)
                    for j in range(2):
                        ins = nc.scalar.activation(PR[:, b, j, 0:W], S[:, b, j, 0:W], ACT.Exp,
                                                   bias=NMAX[:, b, j:j + 1], accum_out=SUM[:, b, j:j + 1])
                    ins.then_inc(s_p, 1)
                if 2 <= step < N + 2:
                    u, b = step - 2, step % 2
                    nb = UNITS[u][1] + 1
                    act.wait_ge(s_t, u + 1)
                    if u >= 2:
                        act.wait_ge(s_o, u - 1)
                    nc.scalar.copy(PT[:, b, :, 0:nb, :],
                                   PS[:, 6 + b, 0:2 * nb * P].rearrange("p (j n q) -> p j n q", j=2, n=nb))\
                      .then_inc(s_pt, 1)
                if step >= 3:
                    u, b = step - 3, (step - 3) % 2
                    g, qt = UNITS[u]
                    act.wait_ge(s_o, u + 1)
                    nc.scalar.copy(OT[0:64, g, qt * P:(qt + 1) * P], PS[0:64, b, 0:P])
                    nc.scalar.copy(OT[64:128, g, qt * P:(qt + 1) * P], PS[64:128, b, P:2 * P]).then_inc(s_ot, 1)
                    if qt == TT - 1:
                        act.wait_ge(s_ot, u + 1)
                        nc.scalar.copy(OTH[:, g, :], OT[:, g, :]).then_inc(s_oth, 1)
                if step in (N - 4, N):
                    act.wait_ge(s_tile, len(TILES))
                    high(step // N)

            nc.scalar.activation(WARM[:, 1:2], VEC[:, V_EPS:V_EPS + 1], ACT.Sqrt)
            for d in range(KD):
                high(d + 2)
                act.wait_ge(s_x1, d + 1)
                nc.scalar.activation(SQ[:, d, :], XT[:, d, :], ACT.Square).then_inc(s_sq, 1)
            root(3, D, 4, RSTD)
            for k in range(KD):
                act.wait_ge(s_h2, k + 1)
                nc.scalar.activation(H2H[:, k, :], HT[:, k, :], ACT.Identity, bias=MOD[:, SH_F + k:SH_F + k + 1])\
                  .then_inc(s_h2h, 1)
            def u_step(j, at, first=False):
                act.wait_ge(s_ring[j], at * 4 + (ADA_RING * 4 + 16))
                if not first or j >= 2:
                    act.wait_ge(s_umm, at + j - 1)
                nc.scalar.copy(HI[:, j % 2, :], RING[:, j, :]).then_inc(s_uh, 1)
                if not first or j >= 2:
                    nc.scalar.activation(AG[:, bass.ds(at + j - 2, 1), :].rearrange("p o t -> p (o t)"),
                                         PS[:, (j + 2) % 4, 0:T], ACT.Gelu).then_inc(s_gelu, 1)

            for h in range(PH):
                act.wait_ge(s_q, h + 1)
                if h < PH - 2:
                    high(KD + 2 + h)
                nc.scalar.copy(QP[:, h, :], PS[:, h % 4, 0:T]).then_inc(s_qc, 1)
                if h == PH - 4:
                    nc.scalar.copy(SILU2[:], SILU[:]).then_inc(s_silu, 1)
                if h in (PH - 3, PH - 2):
                    u_step(h - (PH - 3), 0, first=True)
            for n in range(TT * PH):
                act.wait_ge(s_k, n + 1)
                nc.scalar.copy(SC[:, n].rearrange("p a b -> p (a b)"), PS[:, 4 + n % 4, 0:T]).then_inc(s_sc, 1)

            for j in (2, 3):
                u_step(j, 0, first=True)
            with act.Fori(1, 24) as i:
                for j in range(4):
                    u_step(j, i * 4)
            act.wait_ge(s_best, 1)
            nc.scalar.activation(GTOK[:], GTOK[:], ACT.Exp).then_inc(s_gexp, 1)
            with act.Fori(24, BLOCKS // 4) as i:
                for j in range(4):
                    u_step(j, i * 4)
            for b in range(BLOCKS - 2, BLOCKS):
                act.wait_ge(s_umm, b + 1)
                nc.scalar.activation(AG[:, b, :], PS[:, b % 4, 0:T], ACT.Gelu).then_inc(s_gelu, 1)
            def away(j, g):
                act.wait_ge(s_dist, g + 1)
                nc.scalar.activation(AWAY[:, j], AWAY[:, j], ACT.Abs).then_inc(s_away, 1)

            def onehot_i(j, g):
                act.wait_ge(s_away, g + 1)
                nc.scalar.activation(OHI[:, j], AWAY[:, j], ACT.Relu, scale=-1.0, bias=1.0)\
                  .then_inc(s_ohi, 1)

            for b in range(4):
                act.wait_ge(s_x1t, b + 1)
                nc.scalar.copy(X1[:, b // 2, (b % 2) * 512:(b % 2 + 1) * 512], PS[:, b, :]).then_inc(s_x1c, 1)

            for g in range(2):
                away(g, g)
                onehot_i(g, g)
            with act.Fori(1, GROUPS // 2) as i:
                for j in range(2):
                    away(j, i * 2 + j)
                    act.wait_ge(s_gmm, i * 2 + j - 1)
                    onehot_i(j, i * 2 + j)

            def v_step(j, at, first=False):
                act.wait_ge(s_ring[j], at * 4 + ((ADA_RING + BLOCKS) * 4 + 16))
                if not first or j >= 2:
                    act.wait_ge(s_vmm, at + j - 1)
                if first and j == 0:
                    act.wait_ge(s_gmm, GROUPS)
                nc.scalar.copy(HI[:, j % 2, :], RING[:, j, :]).then_inc(s_vh, 1)
                if first and j == 0:
                    act.wait_ge(s_gated, GROUPS)
                nc.scalar.copy(WH[:, j % 2, :], AG[:, bass.ds(at + j, 1), :].rearrange("p o t -> p (o t)"))\
                  .then_inc(s_vh, 1)

            for j in range(4):
                v_step(j, 0, first=True)
            with act.Fori(1, BLOCKS // 4) as i:
                for j in range(4):
                    v_step(j, i * 4)
            nc.scalar.activation(WARM[:, 0:1], VEC[:, V_EPS:V_EPS + 1], ACT.Sqrt)
            for tt in range(TT):
                act.wait_ge(s_sumd, tt + 1)
                nc.scalar.activation(EPI[:, tt, 0, :], EPI[:, tt, 1, :], ACT.Square,
                                     accum_out=SSQ[:, 0, tt:tt + 1]).then_inc(s_ssq2, 1)
                act.wait_ge(s_ssq2, tt + 1)
                nc.scalar.activation(SSQ[:, 1, tt:tt + 1], SSQ[:, 0, tt:tt + 1], ACT.Sqrt, bias=VEC[:, V_EPS:V_EPS + 1],
                                     scale=1.0 / D).then_inc(s_root2, 1)
            act.wait_ge(s_rstd2, 1)
            act.wait_ge(s_xg, 1)
            nc.scalar.activation(EPI[:, 1, 0, 512:D], XG[:, 512:D], ACT.Identity, scale=SSQ[:, 2, 1:2]).then_inc(s_outa, 1)

        @block.vector
        def _(dve):
            V = nc.vector
            done = [0]

            def step(ins):
                ins.then_inc(s_d, 1)
                done[0] += 1
                dve.wait_ge(s_d, done[0])

            def ada(c):
                if ADA_FIRST <= c < ADA_FIRST + ADA_BESIDE:
                    dve.wait_ge(s_beside[c % 3], 16 * ((c - ADA_FIRST) // 3 + 1))
                    w = BESIDE[c % 3][:]
                else:
                    dve.wait_ge(s_ring[c % 4], 16 * ((c if c < ADA_FIRST else c - ADA_BESIDE) // 4 + 1))
                    w = RING[:, c % 4, :]
                V.tensor_tensor_reduce(w, w, SILU[:], 1.0, 0.0, ALU.mult, ALU.add, MOD[:, c:c + 1]).then_inc(s_ada, 1)

            dve.wait_ge(s_silu, 1)
            for c in range(ADA_FIRST):
                ada(c)
                if c == 9:
                    dve.wait_ge(s_root, 1)
                    step(V.reciprocal(RSTD[:], RSTD[:]))
                if c >= 10:
                    for k in range(2 * (c - 10), min(2 * (c - 10) + 2, KD)):
                        V.tensor_tensor(HT[:, k, :], XT[:, k, :], RSTD[:], ALU.mult).then_inc(s_xn, 1)
            dve.wait_ge(s_ada, ADA_FIRST)
            step(V.tensor_tensor(MOD[:, 0:ADA_FIRST], MOD[:, 0:ADA_FIRST], VEC[:, V_B:V_B + ADA_FIRST], ALU.add))
            V.scalar_tensor_tensor(out=GAIN1[:], in0=MOD[:, SC_A:SC_A + KD], scalar=1.0,
                                   in1=VEC[:, V_GMIX:V_GMIX + KD], op0=ALU.add, op1=ALU.mult).then_inc(s_gain, 1)
            dve.wait_ge(s_gain, 1)
            dve.wait_ge(s_xn, KD)

            def z_low(c):
                if c not in POOL_LOWS:
                    dve.wait_ge(s_zh, c + 1)
                    a, h, to = z_parts(c)
                    V.tensor_tensor(to, a, h.bitcast(F32), ALU.subtract).then_inc(s_zl, 1)

            for k in range(KD + 1):
                if k < KD:
                    dve.wait_ge(s_hh, k + 1)
                    V.tensor_scalar(HT[:, k, :], HT[:, k, :], GAIN1[:, k:k + 1], MOD[:, SH_A + k:SH_A + k + 1],
                                    ALU.mult, ALU.add).then_inc(s_h, 1)
                if k >= 1:
                    dve.wait_ge(s_h, k)
                    V.tensor_tensor(HTL[:, k - 1, :], HT[:, k - 1, :], HTH[:, k - 1, :].bitcast(F32), ALU.subtract)\
                     .then_inc(s_hl, 1)
            z_low(0)
            z_low(1)
            rotated = [0]

            def rotate(n, i):
                a, b = PS[:, n % 4, 0:T], PS[:, (n + 1) % 4, 0:T]
                dve.wait_ge(s_tile, n + 2)
                dve.wait_ge(s_rope, 1 + rotated[0])
                V.tensor_tensor(RT[:, 0, :], a, COS[:], ALU.mult).then_inc(s_dread, 1)
                V.tensor_tensor(RT[:, 1, :], b, SIN[:], ALU.mult).then_inc(s_dread, 1)
                dve.wait_ge(s_dread, dve_reads(n + 1))
                if i is None:
                    V.tensor_tensor(KR[:], RT[:, 0, :], RT[:, 1, :], ALU.add).then_inc(s_rope, 1)
                else:
                    for h in range(4):
                        r = slice(32 * h, 32 * h + 32)
                        ins = V.tensor_tensor(QR[r, 4 * i + h, :], RT[r, 0, :], RT[r, 1, :], ALU.add)
                    ins.then_inc(s_rope, 1)
                rotated[0] += 1

            def latent(k):
                gain = V_GQA + k if k < CQ else V_GKVA + k - CQ
                V.scalar_tensor_tensor(out=CQT[:, k, :], in0=CQT[:, k, :], scalar=VEC[:, gain:gain + 1], in1=RSTD[:],
                                       op0=ALU.mult, op1=ALU.mult).then_inc(s_lat, 1)

            LATENTS = {11: (0, 1, 2), 12: (3, 4, 5), 14: (6, 7)}
            ADA_NONE = (4, 9, 14, 18, 20, 21)
            made = ADA_FIRST
            for n, (kind, i) in enumerate(TILES):
                if kind in ("cq", "ckv"):
                    dve.wait_ge(s_tile, n + 1)
                    V.tensor_copy(CQT[:, n, :], PS[:, n % 4, 0:T]).then_inc(s_dread, 1)
                for c in range(last_chunk(n - 1) + 3 if n else 2, min(last_chunk(n) + 3, CHUNKS)):
                    z_low(c)
                if n == 4:
                    dve.wait_ge(s_vec, 16)
                    dve.wait_ge(s_pos, 16)
                    step(V.tensor_copy(ANG[:, 1, :], ANG[:, 0, :].bitcast(I32)))
                    step(V.tensor_scalar(ANG[:, 0, :], ANG[:, 1, :], VEC[:, V_INV:V_INV + 1], None, ALU.mult))
                    step(V.tensor_scalar(ANG[:, 1, :], ANG[:, 0, :], 1.0 / TWO_PI, ROUND, ALU.mult, ALU.add))
                    step(V.tensor_scalar(ANG[:, 1, :], ANG[:, 1, :], ROUND, None, ALU.subtract))
                    for c in (C1, C2, C3):
                        step(V.scalar_tensor_tensor(out=ANG[:, 0, :], in0=ANG[:, 1, :], scalar=-c, in1=ANG[:, 0, :],
                                                    op0=ALU.mult, op1=ALU.add))
                    step(V.tensor_scalar(ANG[:, 1, :], ANG[:, 0, :], PI_IN, -PI_IN, ALU.min, ALU.max))
                    step(V.scalar_tensor_tensor(out=ANG[:, 2, :], in0=ANG[:, 1, :], scalar=-1.0, in1=ANG[:, 1, :],
                                                op0=ALU.mult, op1=ALU.max))
                    V.tensor_scalar(ANG[:, 2, :], ANG[:, 2, :], -1.0, HALF_PI, ALU.mult, ALU.add).then_inc(s_ang, 1)
                if (kind, i) == ("kr", 1):
                    dve.wait_ge(s_trig, 2)
                    V.tensor_scalar(SIN[:], SIN[:], VEC[:, V_SGN:V_SGN + 1], None, ALU.mult).then_inc(s_rope, 1)
                    dve.wait_ge(s_rope, 1)
                    dve.wait_ge(s_const, 16)
                    rotate(n - 1, None)
                if kind == "qr" and i % 2 == 1:
                    dve.wait_ge(s_zeroq, 2)
                    rotate(n - 1, i // 2)
                if n == 10:
                    dve.wait_ge(s_root, 2)
                    step(V.reciprocal(RSTD[:], RSTD[:]))
                if n == 14:
                    dve.wait_ge(s_root, 3)
                    step(V.reciprocal(RSTD[:], RSTD[:]))
                for k in LATENTS.get(n, ()):
                    latent(k)
                if n >= 2 and n not in ADA_NONE and made < ADA_EARLY:
                    ada(made)
                    made += 1

            N = len(UNITS)

            def low_part(c):
                dve.wait_ge(s_wh, c + 1)
                V.tensor_tensor(W_OPL[:, c, :], W_OP[:, c, :], W_OPH[:, c % 2, :].bitcast(F32), ALU.subtract)\
                 .then_inc(s_wl, 1)

            for at in range(N + 1):
                if at < N:
                    u, b = at, at % 2
                    g, qt = UNITS[u]
                    W = P * (qt + 1)
                    dve.wait_ge(s_s, u + 1)
                    if u >= 2:
                        dve.wait_ge(s_p, u - 1)
                    if g == PAIRS and qt == 0:
                        dve.wait_ge(s_bias, 16)
                        V.tensor_tensor(BT[:], BT[:], MASK.unsqueeze(1).broadcast_to([P, HEADS, T]), ALU.add)\
                         .then_inc(s_mask, 1)
                        dve.wait_ge(s_mask, 1)
                    if g < PAIRS:
                        V.scalar_tensor_tensor(out=S[:, b, :, 0:W],
                                               in0=PS[:, S_BANK[u % 4], 0:2 * W].rearrange("p (j k) -> p j k", j=2),
                                               scalar=MLA_SCALE,
                                               in1=MASK[:, T - W:T].unsqueeze(1).broadcast_to([P, 2, W]),
                                               op0=ALU.mult, op1=ALU.add).then_inc(s_sm, 1)
                    else:
                        h = 2 * (g - PAIRS)
                        V.scalar_tensor_tensor(out=S[:, b, :, 0:W],
                                               in0=PS[:, S_BANK[u % 4], 0:2 * W].rearrange("p (j k) -> p j k", j=2),
                                               scalar=MOBA_SCALE, in1=BT[:, h:h + 2, T - W:T],
                                               op0=ALU.mult, op1=ALU.add).then_inc(s_sm, 1)
                    dve.wait_ge(s_sm, u + 1)
                    V.tensor_reduce(NMAX[:, b, :], S[:, b, :, 0:W], AX.X, ALU.max, negate=True).then_inc(s_nm, 1)
                if at >= 1:
                    u, b = at - 1, (at - 1) % 2
                    W = P * (UNITS[u][1] + 1)
                    dve.wait_ge(s_p, u + 1)
                    step(V.reciprocal(REC[:, b, :], SUM[:, b, :]))
                    for j in range(2):
                        ins = V.tensor_scalar(PR[:, b, j, 0:W], PR[:, b, j, 0:W], REC[:, b, j:j + 1], None, ALU.mult)
                    ins.then_inc(s_pn, 1)

            dve.wait_ge(s_ada, ADA_EARLY)
            step(V.tensor_tensor(MOD[:, ADA_FIRST:ADA_EARLY], MOD[:, ADA_FIRST:ADA_EARLY],
                                 VEC[:, V_B + ADA_FIRST:V_B + ADA_EARLY], ALU.add))
            step(V.scalar_tensor_tensor(out=GAIN2[:], in0=MOD[:, SC_F:SC_F + KD], scalar=1.0,
                                        in1=VEC[:, V_GFFN:V_GFFN + KD], op0=ALU.add, op1=ALU.mult))
            low_part(1)
            for d in range(KD):
                dve.wait_ge(s_y, d + 1)
                V.scalar_tensor_tensor(out=XT[:, d, :], in0=PS[:, d % 4, 0:T],
                                       scalar=MOD[:, GT_A + d:GT_A + d + 1], in1=XT[:, d, :],
                                       op0=ALU.mult, op1=ALU.add).then_inc(s_x1, 1)
                low_part(d + 2)
            dve.wait_ge(s_root, 4)
            step(V.reciprocal(RSTD[:], RSTD[:]))
            for k in range(KD):
                V.scalar_tensor_tensor(out=HT[:, k, :], in0=XT[:, k, :], scalar=GAIN2[:, k:k + 1], in1=RSTD[:],
                                       op0=ALU.mult, op1=ALU.mult).then_inc(s_h2, 1)
            for k in range(KD):
                dve.wait_ge(s_h2h, k + 1)
                V.scalar_tensor_tensor(out=H2L[:, k, :], in0=HT[:, k, :], scalar=MOD[:, SH_F + k:SH_F + k + 1],
                                       in1=H2H[:, k, :].bitcast(F32), op0=ALU.add, op1=ALU.subtract).then_inc(s_h2l, 1)
            for h in range(PH - 2):
                low_part(KD + 2 + h)

            def low(j, at):
                dve.wait_ge(s_uh, at + j + 1)
                V.tensor_tensor(LO[:, j % 2, :], RING[:, j, :], HI[:, j % 2, :].bitcast(F32), ALU.subtract)\
                 .then_inc(s_ul, 1)

            PAIR = range(2)
            HALVES = [(a, p) for a in PAIR for p in range(2)]
            with dve.Fori(0, TT * PH // 2) as w:
                count = [0]

                def ranked(ins):
                    ins.then_inc(s_tk, 1)
                    count[0] += 1

                def settled(steps):
                    dve.wait_ge(s_tk, w * STEPS + (count[0] - steps))
                    V.sem_inc(s_held, 1)

                low(0, w * 8)
                dve.wait_ge(s_sc, TT * PH)
                for a in PAIR:
                    ranked(V.tensor_copy(WK[:, a], SC[:, bass.ds(w * 2 + a, 1)].rearrange("p o a b -> p (o a) b")))
                for n, (a, p) in enumerate(HALVES):
                    if n % 2 == 0:
                        settled(1)
                    ranked(V.max(TV[:, a, p, 0:8], WK[:, a, p, :]))
                low(1, w * 8)
                for n, (a, p) in enumerate(HALVES):
                    if n % 2 == 0:
                        settled(2)
                    ranked(V.max_index(TIU[:, a, p, 0:8], TV[:, a, p, 0:8], WK[:, a, p, :]))
                low(2, w * 8)
                for n, (a, p) in enumerate(HALVES):
                    if n % 2 == 0:
                        settled(2)
                    ranked(V.match_replace(WK[:, a, p, :], TV[:, a, p, 0:8], WK[:, a, p, :], LOWEST))
                low(3, w * 8)
                for n, (a, p) in enumerate(HALVES):
                    if n % 2 == 0:
                        settled(2)
                    ranked(V.max(TV[:, a, p, 8:16], WK[:, a, p, :]))
                low(0, w * 8 + 4)
                for n, (a, p) in enumerate(HALVES):
                    if n % 2 == 0:
                        settled(2)
                    ranked(V.max_index(TIU[:, a, p, 8:16], TV[:, a, p, 8:16], WK[:, a, p, :]))
                for a in PAIR:
                    ranked(V.tensor_tensor(CAND[:, a], TV[:, a, 0, :].unsqueeze(2).broadcast_to([P, TOPK, TOPK]),
                                           TV[:, a, 1, :].unsqueeze(1).broadcast_to([P, TOPK, TOPK]), ALU.add))
                low(1, w * 8 + 4)
                cand = [CAND[:, a].rearrange("p a b -> p (a b)") for a in PAIR]
                for a in PAIR:
                    settled(1)
                    ranked(V.max(BV[:, a, 0:8], cand[a]))
                for a in PAIR:
                    settled(1)
                    ranked(V.max_index(PU[:, a, 0:8], BV[:, a, 0:8], cand[a]))
                low(2, w * 8 + 4)
                for a in PAIR:
                    settled(1)
                    ranked(V.match_replace(cand[a], BV[:, a, 0:8], cand[a], LOWEST))
                for a in PAIR:
                    settled(1)
                    ranked(V.max(BV[:, a, 8:16], cand[a]))
                low(3, w * 8 + 4)
                for a in PAIR:
                    settled(1)
                    ranked(V.max_index(PU[:, a, 8:16], BV[:, a, 8:16], cand[a]))
                two = bass.ds(w * 2, 2)
                ranked(V.tensor_copy(TI[:, two].rearrange("p a b c -> p (a b c)"), TIU[:].rearrange("p a b c -> p (a b c)")))
                settled(1)
                ranked(V.tensor_copy(BEST[:, two].rearrange("p a b -> p (a b)"), BV[:].rearrange("p a b -> p (a b)")))
                ranked(V.tensor_copy(POS[:, two].rearrange("p a b -> p (a b)"), PU[:].rearrange("p a b -> p (a b)")))
                STEPS_DONE = count[0]
            assert STEPS_DONE == STEPS, STEPS_DONE

            low(0, 64)
            dve.wait_ge(s_tk, STEPS * TT * PH // 2)
            step(V.tensor_scalar(AIU[:, 0], POS[:], 4, None, ALU.logical_shift_right))
            step(V.tensor_scalar(AIU[:, 1], POS[:], 15, None, ALU.bitwise_and))
            step(V.tensor_copy(AIF[:], AIU[:]))
            V.tensor_tensor(GTOK[:], BEST[:], BEST[:, :, 0:1].broadcast_to([P, TT * PH, TOPK]), ALU.subtract)\
             .then_inc(s_best, 1)

            def ada_late(c):
                dve.wait_ge(s_wgt[c % 4], 16 * (c // 4 + 1))
                w = W_GT[:, c % 4, :]
                V.tensor_tensor_reduce(w, w, SILU2[:], 1.0, 0.0, ALU.mult, ALU.add,
                                       MOD[:, ADA_EARLY + c:ADA_EARLY + c + 1]).then_inc(s_ada, 1)

            dve.wait_ge(s_silu, 2)
            b, late = 1, 0
            iota16 = IOTA[:, 0:TOPK].unsqueeze(1).unsqueeze(1).broadcast_to([P, 4, TOPK, TOPK])
            for p in range(2):
                for q in range(TT * PH // 4):
                    hs = slice(4 * q, 4 * q + 4)
                    step(V.tensor_tensor(EQ[:], AIF[:, p, hs].unsqueeze(3).broadcast_to([P, 4, TOPK, TOPK]), iota16,
                                         ALU.is_equal))
                    low(b % 4, 64 + b // 4 * 4)
                    step(V.tensor_tensor(EQ[:], EQ[:], TI[:, hs, p].unsqueeze(2).broadcast_to([P, 4, TOPK, TOPK]),
                                         ALU.mult))
                    low((b + 1) % 4, 64 + (b + 1) // 4 * 4)
                    step(V.tensor_reduce(ITOK[:, p, hs, :], EQ[:], AX.X, ALU.add))
                    low((b + 2) % 4, 64 + (b + 2) // 4 * 4)
                    b += 3
                    if b >= 10 + 4 * late:
                        ada_late(late)
                        late += 1
            while b < 40:
                low(b % 4, 64 + b // 4 * 4)
                b += 1
                if late < ADA_LATE and b >= 10 + 4 * late:
                    ada_late(late)
                    late += 1
            dve.wait_ge(s_gexp, 1)
            step(V.tensor_reduce(GSUM[:], GTOK[:], AX.X, ALU.add))
            step(V.reciprocal(GREC[:], GSUM[:]))
            V.tensor_tensor(GTOK[:], GTOK[:], GREC[:].unsqueeze(2).broadcast_to([P, TT * PH, TOPK]), ALU.mult)\
             .then_inc(s_ranks, 1)
            step(V.tensor_copy(J16[:], ITOK[:, 1].rearrange("p (a h) k -> p a (h k)", a=TT)))
            V.tensor_copy(ID16[:], IDENT).then_inc(s_z16, 1)
            V.tensor_copy(ONE16[:], ONES[:]).then_inc(s_z16, 1)
            V.tensor_scalar(NI16[:], IOTA, IDENT[:, 0:1], -1.0, ALU.mult, ALU.mult).then_inc(s_z16, 1)

            dve.wait_ge(s_ada, ADA)
            step(V.tensor_tensor(MOD[:, ADA_EARLY:ADA], MOD[:, ADA_EARLY:ADA], VEC[:, V_B + ADA_EARLY:V_B + ADA], ALU.add))
            for k in range(KD):
                ins = V.tensor_scalar(DIAG[:, k, :], IDENT, MOD[:, GT_F + k:GT_F + k + 1], None, ALU.mult)
            ins.then_inc(s_diag, 1)
            with dve.Fori(26, LAST_U) as i:
                for j in range(4):
                    low(j, i * 4)
            dve.wait_ge(s_rt, 1)
            V.tensor_copy(RANKED[:, 0, :], PS[:, 6, 0:T]).then_inc(s_ranked, 1)
            V.tensor_scalar(RANKED[:, 1, :], PS[:, 6, T:2 * T], -1.0, None, ALU.mult).then_inc(s_ranked, 1)
            with dve.Fori(LAST_U, BLOCKS // 4) as i:
                for j in range(4):
                    low(j, i * 4)
            dve.wait_ge(s_umm, BLOCKS)
            V.tensor_copy(GTB[:], PS[:, 4:6, :].rearrange("p a b -> p (a b)")).then_inc(s_gtbc, 1)
            dve.wait_ge(s_ranked, 2)
            dve.wait_ge(s_gelu, BLOCKS)

            def onehot_j(j, g):
                dve.wait_ge(s_z, g + 1)
                V.scalar_tensor_tensor(out=OHJ[:, j], in0=PS[:, 2 * j:2 * j + 2, :].rearrange("p b (t i) -> p (b t) i", i=P),
                                       scalar=0.0, in1=RANKED[:, 0, bass.ds(g * GT, GT)].unsqueeze(2).broadcast_to([P, GT, P]),
                                       op0=ALU.is_equal, op1=ALU.mult).then_inc(s_ohj, 1)

            def gated(j, g):
                a = AG[:, :, bass.ds(g * GT, GT)]
                V.tensor_tensor(a, PS[:, 4 + 2 * j:6 + 2 * j, :].rearrange("p b (t i) -> p i (b t)", i=P), a, ALU.mult)\
                 .then_inc(s_gated, 1)

            onehot_j(0, 0)
            onehot_j(1, 1)
            dve.wait_ge(s_gmm, 1)
            gated(0, 0)
            with dve.Fori(1, GROUPS // 2) as i:
                for j in range(2):
                    dve.wait_ge(s_gmm, i * 2 + j - 1)
                    onehot_j(j, i * 2 + j)
                    dve.wait_ge(s_gmm, i * 2 + j)
                    gated(1 - j, i * 2 + (j - 1))
            dve.wait_ge(s_gmm, GROUPS)
            gated(1, GROUPS - 1)

            def v_low(j, at):
                dve.wait_ge(s_vh, at * 2 + (2 * j + 2))
                V.tensor_tensor(LO[:, j % 2, :], RING[:, j, :], HI[:, j % 2, :].bitcast(F32), ALU.subtract)\
                 .then_inc(s_vl, 1)
                V.tensor_tensor(WL[:, j % 2, :], AG[:, bass.ds(at + j, 1), :].rearrange("p o t -> p (o t)"),
                                WH[:, j % 2, :].bitcast(F32), ALU.subtract).then_inc(s_al, 1)

            with dve.Fori(0, BLOCKS // 4) as i:
                for j in range(4):
                    v_low(j, i * 4)
            dve.wait_ge(s_x1c, 4)
            dve.wait_ge(s_gtbc, 1)
            for tt in range(TT):
                if tt == 0:
                    dve.wait_ge(s_tile0, 1)
                else:
                    dve.wait_ge(s_vmm, BLOCKS)
                step(V.tensor_tensor(EPI[:, tt, 0, :], PS[:, 2 * tt:2 * tt + 2, :].rearrange("p a b -> p (a b)"), GTB[:],
                                     ALU.mult))
                V.tensor_tensor(EPI[:, tt, 1, :], EPI[:, tt, 0, :], X1[:, tt, :], ALU.add).then_inc(s_sumd, 1)
            dve.wait_ge(s_gf, 16)
            dve.wait_ge(s_sumd, TT)
            V.tensor_tensor(XG[:], EPI[:, 1, 1, :], GFB[:], ALU.mult).then_inc(s_xg, 1)
            dve.wait_ge(s_root2, TT)
            V.reciprocal(SSQ[:, 2, :], SSQ[:, 1, :]).then_inc(s_rstd2, 1)
            dve.wait_ge(s_rstd2, 1)
            dve.wait_ge(s_xg, 1)
            V.tensor_scalar(EPI[:, 1, 0, 0:512], XG[:, 0:512], SSQ[:, 2, 1:2], None, ALU.mult).then_inc(s_outv, 1)
            V.scalar_tensor_tensor(out=EPI[:, 0, 0, :], in0=EPI[:, 0, 1, :], scalar=SSQ[:, 2, 0:1],
                                   in1=GFB[:], op0=ALU.mult, op1=ALU.mult).then_inc(s_outv, 1)

        @block.tensor
        def _(pe):
            mm = nc.tensor.matmul

            def sum_squares(bank, first, count):
                for k in range(count):
                    ins = mm(PS[:, bank, 0:T], ONES[:], SQ[:, first + k, :], start=(k == 0), stop=(k == count - 1))
                ins.then_inc(s_ssq, 1)

            pe.wait_ge(s_ones, 1)
            pe.wait_ge(s_sq, KD)
            sum_squares(5, 0, KD)

            def wait_low(c):
                if c in POOL_LOWS:
                    pe.wait_ge(s_zlp, POOL_LOWS.index(c) + 1)
                else:
                    pe.wait_ge(s_zl, c + 1 - sum(p < c for p in POOL_LOWS))

            def stationary_in_parts(o, c, wh, wl, hi, lo, count):
                pe.wait_ge(s_zh, c + 1)
                if c == Z_CHUNKS:
                    pe.wait_ge(s_lath, CQ + CKV)
                for k in range(count):
                    if c == 0:
                        pe.wait_ge(s_hh, k + 1)
                    mm(o, wh[:, k, :], hi[:, k, :], start=(k == 0), stop=False)
                if c == Z_CHUNKS:
                    pe.wait_ge(s_latl, CQ + CKV)
                for k in range(count):
                    if c == 0:
                        pe.wait_ge(s_hl, k + 1)
                    mm(o, wh[:, k, :], lo[:, k, :], start=False, stop=False)
                wait_low(c)
                for k in range(count):
                    ins = mm(o, wl[:, k, :], hi[:, k, :], start=False, stop=(k == count - 1))
                return ins

            def moving_in_parts(o, c, wh, wl, hi, lo, tt, at, count, first, last):
                t = slice(tt * P, (tt + 1) * P)
                pe.wait_ge(s_zh, c + 1)
                for k in range(count):
                    w = wh[:, k * 512:(k + 1) * 512]
                    mm(o, hi[:, at + k, t], w, start=(first and k == 0), stop=False)
                    mm(o, lo[:, at + k, t], w, start=False, stop=False)
                wait_low(c)
                for k in range(count):
                    ins = mm(o, hi[:, at + k, t], wl[:, k * 512:(k + 1) * 512], start=False, stop=(last and k == count - 1))
                return ins

            for n, (kind, i) in enumerate(TILES):
                bank = n % 4
                for m in ((n - 4, n - 3) if (kind, i) == ("mv", 0) else (n - 4,) if n >= 4 else ()):
                    if TILES[m][0] in DVE_READS:
                        pe.wait_ge(s_dread, dve_reads(m))
                    if TILES[m][0] in ACT_READS:
                        pe.wait_ge(s_aread, act_reads(m))
                c, o = last_chunk(n), PS[:, bank, 0:T]
                if kind in ("qn", "qr"):
                    wh = WUH[:, c % 2, :].rearrange("p (k n) -> p k n", k=CQ)
                    wl = W_UQL[:, c - Z_CHUNKS, :].rearrange("p (k n) -> p k n", k=CQ)
                    ins = stationary_in_parts(o, c, wh, wl, CQH[:, 0:CQ], CQL[:, 0:CQ], CQ)
                elif kind == "kn":
                    r = slice(i * CKV * P, (i + 1) * CKV * P)
                    wh = WVH[:, c % 2, r].rearrange("p (k n) -> p k n", k=CKV)
                    wl = W_UKVL[:, 0, r].rearrange("p (k n) -> p k n", k=CKV)
                    ins = stationary_in_parts(o, c, wh, wl, CQH[:, CQ:], CQL[:, CQ:], CKV)
                elif kind == "v":
                    ins = moving_in_parts(PS[:, bank, :], c, WVH[:, c % 2, :], W_UKVL[:, 1, :], CQH, CQL, i, CQ, CKV, True, True)
                elif kind == "mv" and i == 0:
                    for q in range(4):
                        for tt in range(TT):
                            ins = moving_in_parts(PS[:, bank + tt, :], Z_CHUNKS - 4 + q, WZH[:, q % 2, :],
                                                  W_INL[:, Z_CHUNKS - 4 + q, :], HTH, HTL, tt, 2 * q, 2, q == 0, q == 3)
                            if q == 3:
                                ins.then_inc(s_tile, 1)
                        if q < 3:
                            ins.then_inc(s_mv, 1)
                elif kind != "mv":
                    wh = WZH[:, c % 2, :].rearrange("p (k n) -> p k n", k=KD)
                    wl = W_INL[:, c, :].rearrange("p (k n) -> p k n", k=KD)
                    ins = stationary_in_parts(o, c, wh, wl, HTH, HTL, KD)
                if kind != "mv":
                    ins.then_inc(s_tile, 1)
                if (kind, i) == ("kr", 1):
                    pe.wait_ge(s_sq, KD + CQ + CKV)
                    sum_squares(4, 0, CQ)
                    sum_squares(5, CQ, CKV)

            N = len(UNITS)
            pe.wait_ge(s_aread, act_reads(len(TILES) - 1))
            pe.wait_ge(s_rope, 4)

            def scores(u):
                g, qt = UNITS[u]
                W = P * (qt + 1)
                if u >= 4:
                    pe.wait_ge(s_sm, u - 3)
                for j in range(2):
                    o, q = PS[:, S_BANK[u % 4], j * W:(j + 1) * W], slice(qt * P, (qt + 1) * P)
                    h = 2 * (g % PAIRS) + j
                    if g < PAIRS:
                        mm(o, QN[:, h, q], KN[:, g, 0:W], start=True, stop=False)
                        ins = mm(o, QR[:, h, q], KR[:, 0:W], start=False, stop=True)
                    else:
                        ins = mm(o, QM[:, h, q], KM[:, g - PAIRS, 0:W], start=True, stop=True)
                ins.then_inc(s_s, 1)

            for at in range(N + 3):
                if at == 0:
                    scores(0)
                if at + 1 < N:
                    scores(at + 1)
                if 2 <= at < N + 2:
                    u, b = at - 2, at % 2
                    nb = UNITS[u][1] + 1
                    pe.wait_ge(s_pn, u + 1)
                    if u >= 2:
                        pe.wait_ge(s_pt, u - 1)
                    for j in range(2):
                        for n in range(nb):
                            a = (j * nb + n) * P
                            ins = nc.tensor.transpose(PS[:, 6 + b, a:a + P], PR[:, b, j, n * P:(n + 1) * P], IDENT)
                    ins.then_inc(s_t, 1)
                if at >= 3:
                    u, b = at - 3, (at - 3) % 2
                    g, qt = UNITS[u]
                    nb = qt + 1
                    pe.wait_ge(s_pt, u + 1)
                    if u >= 2:
                        pe.wait_ge(s_ot, u - 1)
                    v = (VN if g < PAIRS else VM)
                    c = slice((g % PAIRS) * P, (g % PAIRS + 1) * P)
                    for j in range(2):
                        for n in range(nb):
                            ins = mm(PS[:, b, j * P:(j + 1) * P], v[:, n, c], PT[:, b, j, n, :], start=(n == 0), stop=(n == nb - 1))
                    ins.then_inc(s_o, 1)

            def op_parts(c):
                return (W_OPH[:, c % 2, :].rearrange("p (k n) -> p k n", k=KD),
                        W_OPL[:, c, :].rearrange("p (k n) -> p k n", k=KD))

            def in_parts(o, c, hi_ready, hi, lo_ready, lo):
                wh, wl = op_parts(c)
                pe.wait_ge(s_wh, c + 1)
                for k in range(KD):
                    if c % KD == 0:
                        pe.wait_ge(hi_ready, k + 1)
                    mm(o, wh[:, k, :], hi[:, k, :], start=(k == 0), stop=False)
                for k in range(KD):
                    if c % KD == 0:
                        pe.wait_ge(lo_ready, k + 1)
                    mm(o, wh[:, k, :], lo[:, k, :], start=False, stop=False)
                if c == 0:
                    pe.wait_ge(s_wlp, 1)
                else:
                    pe.wait_ge(s_wl, c)
                for k in range(KD):
                    ins = mm(o, wl[:, k, :], hi[:, k, :], start=False, stop=(k == KD - 1))
                return ins

            def square(k):
                pe.wait_ge(s_sq, KD + CQ + CKV + k + 1)
                ins = mm(PS[:, 4, 0:T], ONES[:], SQ[:, k, :], start=(k == 0), stop=(k == KD - 1))
                if k == KD - 1:
                    ins.then_inc(s_ssq, 1)

            pe.wait_ge(s_ot, N)
            for d in range(KD):
                if d >= 4:
                    pe.wait_ge(s_x1, d - 3)
                in_parts(PS[:, d % 4, 0:T], d, s_oth, OTH, s_otl, OTL).then_inc(s_y, 1)
                if d >= 2:
                    square(d - 2)
            square(KD - 2)
            square(KD - 1)
            pe.wait_ge(s_x1, KD)
            pe.wait_ge(s_wh, KD + 2)
            pairs = [(PS[:, h, 0:T], *op_parts(KD + h)) for h in range(2)]
            for ready, part in ((s_h2h, H2H), (s_h2l, H2L)):
                for k in range(KD):
                    pe.wait_ge(ready, k + 1)
                    for o, wh, wl in pairs:
                        mm(o, wh[:, k, :], part[:, k, :], start=(part is H2H and k == 0), stop=False)
            pe.wait_ge(s_wl, KD + 1)
            for o, wh, wl in pairs:
                for k in range(KD):
                    ins = mm(o, wl[:, k, :], H2H[:, k, :], start=False, stop=(k == KD - 1))
                ins.then_inc(s_q, 1)
            for h in range(2, PH):
                if h >= 4:
                    pe.wait_ge(s_qc, h - 3)
                in_parts(PS[:, h % 4, 0:T], KD + h, s_h2h, H2H, s_h2l, H2L).then_inc(s_q, 1)
            pe.wait_ge(s_keys, 16)
            pe.wait_ge(s_root, 4)
            for n in range(TT * PH):
                tt, h = n // PH, n % PH
                pe.wait_ge(s_qc, h + 1 if tt == 0 else PH)
                if n >= 4:
                    pe.wait_ge(s_sc, n - 3)
                mm(PS[:, 4 + n % 4, 0:T], QP[:, h, tt * P:(tt + 1) * P], KEYS[:, h, :], start=True, stop=True).then_inc(s_k, 1)

            pe.wait_ge(s_h2l, KD)

            def u_block(j, at, first=False):
                pe.wait_ge(s_uh, at + j + 1)
                if not first:
                    pe.wait_ge(s_gelu, at + j - 3)
                hi = HI[:, j % 2, :].rearrange("p (k e) -> p k e", k=KD)
                lo = LO[:, j % 2, :].rearrange("p (k e) -> p k e", k=KD)
                o = PS[:, j, 0:T]
                for k in range(KD):
                    mm(o, hi[:, k, :], H2H[:, k, :], start=(k == 0), stop=False)
                    mm(o, hi[:, k, :], H2L[:, k, :], start=False, stop=False)
                pe.wait_ge(s_ul, at + j + 1)
                for k in range(KD):
                    ins = mm(o, lo[:, k, :], H2H[:, k, :], start=False, stop=(k == KD - 1))
                ins.then_inc(s_umm, 1)

            for j in range(4):
                u_block(j, 0, first=True)
            with pe.Fori(1, LAST_U) as i:
                for j in range(4):
                    u_block(j, i * 4)

            pe.wait_ge(s_ranks, 1)
            for a, src in enumerate((GTOK[:], ITOK[:, 0])):
                for tt in range(TT):
                    o = a * T + tt * P
                    ins = nc.tensor.transpose(PS[:, 6, o:o + P],
                                              src[:, tt * PH:(tt + 1) * PH, :].rearrange("p h k -> p (h k)"), IDENT)
            ins.then_inc(s_rt, 1)
            pe.wait_ge(s_diag, 1)
            for k in range(KD):
                ins = mm(PS[:, 4 + k // 4, (k % 4) * P:(k % 4 + 1) * P], ONES[:], DIAG[:, k, :], start=True, stop=True)
            ins.then_inc(s_gtb, 1)
            with pe.Fori(LAST_U, BLOCKS // 4) as i:
                for j in range(4):
                    u_block(j, i * 4)
            pe.wait_ge(s_gelu, BLOCKS)
            for b in range(4):
                for q in range(4):
                    k = (b % 2) * 4 + q
                    ins = nc.tensor.transpose(PS[:, b, q * P:(q + 1) * P], XT[:, k, (b // 2) * P:(b // 2 + 1) * P], IDENT)
                ins.then_inc(s_x1t, 1)

            def differences(j, g, tt):
                for q in range(2):
                    o = PS[:, 2 * j + q, :]
                    at = bass.ds(g * GT + (4 * q - tt * P), 4)
                    mm(o, J16[:, tt, :], ID16[:, at].unsqueeze(2).broadcast_to([P, 4, P]), start=True, stop=False)
                    ins = mm(o, ONE16[:], NI16[:].unsqueeze(1).broadcast_to([P, 4, P]), start=False, stop=True)
                ins.then_inc(s_z, 1)

            def gate_block(j, g):
                pe.wait_ge(s_ohi, g + 1)
                pe.wait_ge(s_ohj, g + 1)
                for t in range(GT):
                    ins = mm(PS[:, 4 + 2 * j + t // 4, (t % 4) * P:(t % 4 + 1) * P], OHJ[:, j, t, :], OHI[:, j, t, :],
                             start=True, stop=True)
                ins.then_inc(s_gmm, 1)

            pe.wait_ge(s_x1c, 4)
            pe.wait_ge(s_z16, 3)
            differences(0, 0, 0)
            differences(1, 1, 0)
            pe.wait_ge(s_gtbc, 1)
            for j in range(2):
                pe.wait_ge(s_ohj, j + 1)
                differences(j, j + 2, 0)
                gate_block(j, j)
            for tt in range(TT):
                first, last = tt * GROUPS // TT, (tt + 1) * GROUPS // TT
                with pe.Fori(max(first // 2 - 1, 1), last // 2 - 1) as i:
                    for j in range(2):
                        pe.wait_ge(s_ohj, i * 2 + j + 1)
                        differences(j, i * 2 + j + 2, tt)
                        pe.wait_ge(s_gated, i * 2 + j - 1)
                        gate_block(j, i * 2 + j)
            for g in range(GROUPS - 2, GROUPS):
                pe.wait_ge(s_gated, g - 1)
                gate_block(g % 2, g)

            def v_block(j, at, first=False):
                pe.wait_ge(s_vh, at * 2 + (2 * j + 2))
                for tt in range(TT):
                    for h in range(2):
                        mm(PS[:, 2 * tt + h, :], WH[:, j % 2, tt * P:(tt + 1) * P], HI[:, j % 2, h * 512:(h + 1) * 512],
                           start=first, stop=False)
                pe.wait_ge(s_vl, at + j + 1)
                for tt in range(TT):
                    for h in range(2):
                        mm(PS[:, 2 * tt + h, :], WH[:, j % 2, tt * P:(tt + 1) * P], LO[:, j % 2, h * 512:(h + 1) * 512],
                           start=False, stop=False)
                pe.wait_ge(s_al, at + j + 1)
                for tt in range(TT):
                    for h in range(2):
                        ins = mm(PS[:, 2 * tt + h, :], WL[:, j % 2, tt * P:(tt + 1) * P], HI[:, j % 2, h * 512:(h + 1) * 512],
                                 start=False, stop=False)
                ins.then_inc(s_vmm, 1)

            def last_v_block():
                j = 3
                pe.wait_ge(s_vh, 2 * BLOCKS)
                pe.wait_ge(s_vl, BLOCKS)
                pe.wait_ge(s_al, BLOCKS)
                for tt in range(TT):
                    t = slice(tt * P, (tt + 1) * P)
                    for n, (w, v) in enumerate(((WH, HI), (WH, LO), (WL, HI))):
                        for h in range(2):
                            ins = mm(PS[:, 2 * tt + h, :], w[:, j % 2, t], v[:, j % 2, h * 512:(h + 1) * 512],
                                     start=False, stop=(n == 2))
                    ins.then_inc(s_tile0 if tt == 0 else s_vmm, 1)

            pe.wait_ge(s_x1c, 4)
            for j in range(4):
                v_block(j, 0, first=(j == 0))
            with pe.Fori(1, BLOCKS // 4 - 1) as i:
                for j in range(4):
                    v_block(j, i * 4)
            for j in range(3):
                v_block(j, BLOCKS - 4)
            last_v_block()


def t5_bucket(n):
    nf = np.maximum(n, 16).astype(np.float32)
    large = 16 + (np.log(nf / np.float32(16)) / np.float32(np.log(64.0)) * np.float32(16)).astype(np.int32)
    return np.where(n < 16, n, np.minimum(large, 31))


def kernel(x, c, positions, w_ada, b_ada, g_mix, w_in, g_qa, w_uq, g_kva, w_ukv, rel_bias, w_out, g_ffn, w_pq,
           peer_keys, peer_u, peer_v, g_final):
    import concourse.bacc as bacc
    from concourse.bass_utils import run_bass_kernel_spmd

    f = np.ascontiguousarray
    A = np.asarray

    def cols(v):
        return A(v).reshape(-1, P).T

    def stationary(w):
        k, n = w.shape
        return w.reshape(k // P, P, n // P, P).transpose(1, 2, 0, 3)

    consts = np.zeros((P, 512), np.float32)
    consts[:, 0:128] = np.eye(P)
    consts[:, 128:256] = np.arange(P)
    consts[:, 256:512] = np.where(np.arange(T)[None, :] > P + np.arange(P)[:, None], MASKED, 0.0)

    half = ROPE // 2
    row = np.arange(P) % ROPE
    inv = np.float32(THETA) ** (-np.arange(half, dtype=np.float32) / np.float32(half))
    vecs = np.zeros((P, NVEC), np.float32)
    for at, v in ((V_B, A(b_ada)[0]), (V_GMIX, A(g_mix)[0]), (V_GQA, A(g_qa)[0]),
                  (V_GKVA, A(g_kva)[0]), (V_GFFN, A(g_ffn)[0])):
        v = cols(v)
        vecs[:, at:at + v.shape[1]] = v
    vecs[:, V_INV] = inv[row % half]
    vecs[:, V_SGN] = np.where(row < half, -1.0, 1.0)
    vecs[:, V_EPS] = EPS

    swap = (np.arange(ROPE) + half) % ROPE
    wi = A(w_in)[0]
    kr0 = Q_LORA + KV_LORA
    m0 = kr0 + ROPE
    order = np.concatenate([np.arange(kr0), np.tile(kr0 + np.arange(ROPE), 4), np.tile(kr0 + swap, 4),
                            m0 + np.arange(1024)])
    w_in_k = np.concatenate([stationary(wi[:, order]).reshape(P, -1),
                             wi[:, m0 + 1024:].reshape(KD, P, 512).transpose(1, 0, 2).reshape(P, -1)], axis=1)
    qk = NOPE + ROPE
    heads = np.arange(HEADS)[:, None] * qk
    r = (heads + NOPE + np.arange(ROPE)).reshape(2, -1)
    rs = (heads + NOPE + swap).reshape(2, -1)
    order = np.concatenate([(heads + np.arange(NOPE)).ravel(), r[0], rs[0], r[1], rs[1]])
    w_uq_k = stationary(A(w_uq)[0][:, order])
    heads = np.arange(HEADS)[:, None] * 128
    kn = A(w_ukv)[0][:, (heads + np.arange(64)).ravel()]
    vv = A(w_ukv)[0][:, (heads + 64 + np.arange(64)).ravel()]
    w_ukv_k = np.concatenate([stationary(kn).reshape(P, -1),
                              vv.reshape(CKV, P, 512).transpose(1, 0, 2).reshape(P, -1)], axis=1)
    distance = np.maximum(P + np.arange(P)[:, None] - np.arange(T)[None, :], 0)
    rel = f(A(rel_bias)[t5_bucket(distance)].transpose(0, 2, 1))
    pk = A(peer_keys)[0]
    keys = np.zeros((P, PH, 2 * NKEYS), np.float32)
    for p in range(2):
        keys[p * 64:(p + 1) * 64, :, p * NKEYS:(p + 1) * NKEYS] = pk[:, p].transpose(2, 0, 1)

    arrays = {
        "consts": consts, "vecs": vecs, "c_row": f(A(c)[0]), "positions": f(A(positions)[0].astype(np.int32)),
        "xT": f(A(x)[0].reshape(T, KD, P).transpose(2, 1, 0)),
        "w_ada": f(A(w_ada)[0].T.reshape(ADA, P, D)),
        "w_in": f(w_in_k), "w_uq": f(w_uq_k), "w_ukv": f(w_ukv_k), "rel": rel,
        "w_out": f(stationary(A(w_out)[0])), "w_pq": f(stationary(A(w_pq)[0])), "keys": keys,
        "u_tab": f(A(peer_u)[0].reshape(BLOCKS, P, KD, P).transpose(0, 3, 2, 1).reshape(BLOCKS, P, D)),
        "v_tab": f(A(peer_v)[0].reshape(BLOCKS, P, D)),
        "g_final": f(A(g_final)),
    }
    nc = bacc.Bacc("TRN2", target_bir_lowering=False, num_devices=1)
    aps = [nc.dram_tensor(n, a.shape, mybir.dt.from_np(a.dtype), kind="ExternalInput").ap() for n, a in arrays.items()]
    out = nc.dram_tensor("out", (T, D), F32, kind="ExternalOutput").ap()
    build(nc, *aps, out)
    r = run_bass_kernel_spmd(nc, [arrays], core_ids=[0])
    return r.results[0]["out"].reshape(1, T, D)
```
